# Optimizing a Trainium2 kernel written in Bass

```python
import jax
import jax.numpy as jnp
from jax import lax
import numpy as np

D_MODEL = 1024
BATCH = 1
SEQ = 256
DEPTH = 1

ATT_HEADS = 8
ATT_HEAD_DIM = 64
ATT_WIDTH = ATT_HEADS * ATT_HEAD_DIM
MOBA_BLOCK = 256
MOBA_TOPK = 3
MOBA_QCHUNK = 32
HGRN_HEADS = 4
HGRN_EXPAND = 128
HGRN_VDIM = 128
HGRN_KEY_WIDTH = HGRN_HEADS * HGRN_EXPAND
HGRN_WIDTH = HGRN_HEADS * HGRN_VDIM
HGRN_CHUNK = 64
CONV_CH = 512
CONV_WIDTH = 31
N_BRANCH = 3
IN_COLS = 3 * ATT_WIDTH + 2 * HGRN_KEY_WIDTH + 2 * HGRN_WIDTH + 2 * CONV_CH + N_BRANCH * D_MODEL
N_GROUPS = 4
EXPERTS_PER_GROUP = 8
N_EXPERTS = N_GROUPS * EXPERTS_PER_GROUP
EXPERT_TOPK = 2
EXPERT_FF = 512

RMS_EPS = 1e-6
LN_EPS = 1e-5
NEG_INF = -1e30

kernel_name = 'hybrid_moba_hgrn2_conformer_hmoe'

def rms_norm(x, gain):
    xf = x.astype(jnp.float32)
    y = xf * lax.rsqrt(jnp.mean(xf * xf, axis=-1, keepdims=True) + RMS_EPS)
    return (y * gain.astype(jnp.float32)).astype(x.dtype)

def moba_attention(q, k, v):
    B, S, H, dh = q.shape
    n_blk = -(-S // MOBA_BLOCK)
    s_pad = n_blk * MOBA_BLOCK
    n_sel = min(MOBA_TOPK, n_blk)
    n_qc = S // MOBA_QCHUNK
    scale = dh ** -0.5
    pad = ((0, 0), (0, s_pad - S), (0, 0), (0, 0))
    qh = q.transpose(0, 2, 1, 3)
    kb = jnp.pad(k, pad).transpose(0, 2, 1, 3).reshape(B, H, n_blk, MOBA_BLOCK, dh)
    vb = jnp.pad(v, pad).transpose(0, 2, 1, 3).reshape(B, H, n_blk, MOBA_BLOCK, dh)
    k_mean = jnp.mean(kb.astype(jnp.float32), axis=3)
    q_blk = jnp.arange(S) // MOBA_BLOCK
    gate = jnp.einsum('bhsd,bhnd->bhsn', qh.astype(jnp.float32), k_mean)
    fully_past = jnp.arange(n_blk)[None, :] < q_blk[:, None]
    gate = jnp.where(fully_past, gate, NEG_INF)
    _, sel = lax.top_k(gate, n_sel)
    sel_valid = jnp.arange(n_sel)[None, :] < jnp.minimum(n_sel, q_blk)[:, None]

    def to_chunks(a):
        a = a.reshape(B, H, n_qc, MOBA_QCHUNK, a.shape[-1])
        return jnp.moveaxis(a, 2, 0)

    b_idx = jnp.arange(B)[:, None, None, None]
    h_idx = jnp.arange(H)[None, :, None, None]

    def attend_chunk(args):
        c, qc, sc, vc = args
        blk = (c * MOBA_QCHUNK) // MOBA_BLOCK
        qp = c * MOBA_QCHUNK + jnp.arange(MOBA_QCHUNK)
        kp = blk * MOBA_BLOCK + jnp.arange(MOBA_BLOCK)
        k_own = lax.dynamic_index_in_dim(kb, blk, axis=2, keepdims=False)
        v_own = lax.dynamic_index_in_dim(vb, blk, axis=2, keepdims=False)
        s_own = jnp.einsum('bhqd,bhkd->bhqk', qc, k_own).astype(jnp.float32) * scale
        s_own = jnp.where(kp[None, :] <= qp[:, None], s_own, NEG_INF)
        k_sel = kb[b_idx, h_idx, sc].reshape(B, H, MOBA_QCHUNK, n_sel * MOBA_BLOCK, dh)
        v_sel = vb[b_idx, h_idx, sc].reshape(B, H, MOBA_QCHUNK, n_sel * MOBA_BLOCK, dh)
        s_sel = jnp.einsum('bhqd,bhqkd->bhqk', qc, k_sel).astype(jnp.float32) * scale
        s_sel = jnp.where(jnp.repeat(vc, MOBA_BLOCK, axis=-1), s_sel, NEG_INF)
        p = jax.nn.softmax(jnp.concatenate([s_own, s_sel], axis=-1), axis=-1).astype(v.dtype)
        return (jnp.einsum('bhqk,bhkd->bhqd', p[..., :MOBA_BLOCK], v_own)
                + jnp.einsum('bhqk,bhqkd->bhqd', p[..., MOBA_BLOCK:], v_sel))

    o = lax.map(attend_chunk, (jnp.arange(n_qc), to_chunks(qh), to_chunks(sel),
                               sel_valid.reshape(n_qc, MOBA_QCHUNK, n_sel)))
    return jnp.moveaxis(o, 0, 2).reshape(B, H, S, dh).transpose(0, 2, 1, 3).reshape(B, S, H * dh)

def hgrn2_recurrence(q, f_raw, i, lower_bound):
    B, S, H, dk = q.shape
    dv = i.shape[-1]
    C = HGRN_CHUNK
    n_c = S // C
    fr = f_raw.astype(jnp.float32)
    lb = lower_bound.astype(jnp.float32)
    sig = jax.nn.sigmoid(fr)
    log_f = jnp.log(lb + (1.0 - lb) * sig)
    k_in = (1.0 - lb) * (1.0 - sig)
    q_act = jax.nn.silu(q.astype(jnp.float32))

    def to_chunks(a):
        return a.reshape(B, n_c, C, H, a.shape[-1]).transpose(1, 0, 3, 2, 4)

    causal = jnp.tril(jnp.ones((C, C), dtype=bool))[:, :, None]

    def chunk_step(state, xs):
        qc, kc, vc, gc = xs
        b = jnp.cumsum(gc, axis=2)
        o_inter = jnp.einsum('bhtk,bhkv->bhtv', qc * jnp.exp(b), state)
        rel = jnp.where(causal, b[:, :, :, None, :] - b[:, :, None, :, :], 0.0)
        decay = jnp.where(causal, jnp.exp(rel), 0.0)
        scores = jnp.einsum('bhtk,bhtsk,bhsk->bhts', qc, decay, kc)
        o = o_inter + jnp.einsum('bhts,bhsv->bhtv', scores, vc)
        b_end = b[:, :, -1:, :]
        state = (jnp.exp(b_end[:, :, 0, :])[..., None] * state
                 + jnp.einsum('bhsk,bhsv->bhkv', kc * jnp.exp(b_end - b), vc))
        return state, o

    state0 = jnp.zeros((B, H, dk, dv), jnp.float32)
    _, o = lax.scan(chunk_step, state0, (to_chunks(q_act), to_chunks(k_in),
                                         to_chunks(i.astype(jnp.float32)), to_chunks(log_f)))
    return o.transpose(1, 0, 3, 2, 4).reshape(B, S, H, dv)

def conformer_conv(a, b, w_dw, b_dw, ln_g, ln_b):
    u = a * jax.nn.sigmoid(b)
    u = lax.conv_general_dilated(u, w_dw[:, None, :].astype(u.dtype), window_strides=(1,),
                                 padding=[(CONV_WIDTH - 1, 0)],
                                 dimension_numbers=('NWC', 'WIO', 'NWC'),
                                 feature_group_count=CONV_CH)
    uf = u.astype(jnp.float32) + b_dw.astype(jnp.float32)
    mu = jnp.mean(uf, axis=-1, keepdims=True)
    var = jnp.mean(jnp.square(uf - mu), axis=-1, keepdims=True)
    uf = (uf - mu) * lax.rsqrt(var + LN_EPS) * ln_g.astype(jnp.float32) + ln_b.astype(jnp.float32)
    return jax.nn.silu(uf).astype(a.dtype)

def hybrid_mixer(h, w_in, b_gate, q_norm_g, k_norm_g, lower_bound, hgrn_norm_g, conv_w, conv_b,
                 conv_ln_g, conv_ln_b, w_att_o, w_hgrn_o, w_conv_o, w_out):
    B, S, _ = h.shape
    widths = [ATT_WIDTH] * 3 + [HGRN_KEY_WIDTH] * 2 + [HGRN_WIDTH] * 2 + [CONV_CH] * 2
    offsets = np.cumsum(widths).tolist()
    proj = h @ w_in
    aq, ak, av, hq, hf, hi, hg, ca, cb, gl = jnp.split(proj, offsets, axis=-1)
    att_shape = (B, S, ATT_HEADS, ATT_HEAD_DIM)
    q = rms_norm(aq.reshape(att_shape), q_norm_g)
    k = rms_norm(ak.reshape(att_shape), k_norm_g)
    y_att = moba_attention(q, k, av.reshape(att_shape)) @ w_att_o
    o = hgrn2_recurrence(hq.reshape(B, S, HGRN_HEADS, HGRN_EXPAND),
                         hf.reshape(B, S, HGRN_HEADS, HGRN_EXPAND),
                         hi.reshape(B, S, HGRN_HEADS, HGRN_VDIM),
                         lower_bound.reshape(HGRN_HEADS, HGRN_EXPAND))
    o = rms_norm(o, hgrn_norm_g) * jax.nn.silu(hg.reshape(B, S, HGRN_HEADS, HGRN_VDIM).astype(jnp.float32))
    y_rec = o.reshape(B, S, HGRN_WIDTH).astype(h.dtype) @ w_hgrn_o
    y_conv = conformer_conv(ca, cb, conv_w, conv_b, conv_ln_g, conv_ln_b) @ w_conv_o
    gates = jax.nn.sigmoid(gl + b_gate).reshape(B, S, N_BRANCH, D_MODEL)
    merged = gates[:, :, 0] * y_att + gates[:, :, 1] * y_rec + gates[:, :, 2] * y_conv
    return merged @ w_out

def hierarchical_moe(h, w_coarse, b_coarse, w_fine, b_fine, w_exp_in, w_exp_out):
    B, S, D = h.shape
    t = h.reshape(-1, D)
    p_grp = jax.nn.softmax((t @ w_coarse + b_coarse).astype(jnp.float32), axis=-1)
    p_top, grp = lax.top_k(p_grp, 1)
    fine = (t @ w_fine + b_fine).astype(jnp.float32).reshape(-1, N_GROUPS, EXPERTS_PER_GROUP)
    fine_sel = jnp.take_along_axis(fine, grp[:, :, None], axis=1)[:, 0]
    top_logit, local = lax.top_k(fine_sel, EXPERT_TOPK)
    w = jax.nn.softmax(top_logit, axis=-1) * p_top
    expert_id = grp * EXPERTS_PER_GROUP + local
    combine = jnp.sum(jax.nn.one_hot(expert_id, N_EXPERTS, dtype=jnp.float32) * w[..., None], axis=1)
    y = jnp.zeros(t.shape, jnp.float32)
    for e in range(N_EXPERTS):
        gate, up = jnp.split(t @ w_exp_in[e], 2, axis=-1)
        y = y + combine[:, e:e + 1] * ((jax.nn.silu(gate) * up) @ w_exp_out[e]).astype(jnp.float32)
    return y.astype(h.dtype).reshape(B, S, D)

def setup_inputs(seed: int = 0) -> dict:
    key = jax.random.key(seed)
    ks = jax.random.split(key, 23)
    L, D = DEPTH, D_MODEL

    def nrm(k, shape, scale):
        return jax.random.normal(k, shape, jnp.float32) * scale

    return {
        'x': nrm(ks[0], (BATCH, SEQ, D), 1.0),
        'mix_norm_g': 1.0 + nrm(ks[1], (L, D), 0.02),
        'w_in': nrm(ks[2], (L, D, IN_COLS), D ** -0.5),
        'b_gate': nrm(ks[3], (L, N_BRANCH * D), 0.02),
        'q_norm_g': 1.0 + nrm(ks[4], (L, ATT_HEAD_DIM), 0.02),
        'k_norm_g': 1.0 + nrm(ks[5], (L, ATT_HEAD_DIM), 0.02),
        'lb_logits': nrm(ks[6], (L, HGRN_KEY_WIDTH), 0.1),
        'hgrn_norm_g': 1.0 + nrm(ks[7], (L, HGRN_VDIM), 0.02),
        'conv_w': nrm(ks[8], (L, CONV_WIDTH, CONV_CH), CONV_WIDTH ** -0.5),
        'conv_b': nrm(ks[9], (L, CONV_CH), 0.02),
        'conv_ln_g': 1.0 + nrm(ks[10], (L, CONV_CH), 0.02),
        'conv_ln_b': nrm(ks[11], (L, CONV_CH), 0.02),
        'w_att_o': nrm(ks[12], (L, ATT_WIDTH, D), ATT_WIDTH ** -0.5),
        'w_hgrn_o': nrm(ks[13], (L, HGRN_WIDTH, D), HGRN_WIDTH ** -0.5),
        'w_conv_o': nrm(ks[14], (L, CONV_CH, D), CONV_CH ** -0.5),
        'w_out': nrm(ks[15], (L, D, D), D ** -0.5),
        'ffn_norm_g': 1.0 + nrm(ks[16], (L, D), 0.02),
        'w_coarse': nrm(ks[17], (L, D, N_GROUPS), D ** -0.5),
        'b_coarse': nrm(ks[18], (L, N_GROUPS), 0.01),
        'w_fine': nrm(ks[19], (L, D, N_EXPERTS), D ** -0.5),
        'b_fine': nrm(ks[20], (L, N_EXPERTS), 0.01),
        'w_exp_in': nrm(ks[21], (L, N_EXPERTS, D, 2 * EXPERT_FF), D ** -0.5),
        'w_exp_out': nrm(ks[22], (L, N_EXPERTS, EXPERT_FF, D), EXPERT_FF ** -0.5),
    }

def reference(x, mix_norm_g, w_in, b_gate, q_norm_g, k_norm_g, lb_logits, hgrn_norm_g, conv_w,
              conv_b, conv_ln_g, conv_ln_b, w_att_o, w_hgrn_o, w_conv_o, w_out, ffn_norm_g,
              w_coarse, b_coarse, w_fine, b_fine, w_exp_in, w_exp_out):
    lb_p = jax.nn.softmax(lb_logits.astype(jnp.float32), axis=0)
    lb_all = jnp.maximum(jnp.cumsum(lb_p, axis=0) - lb_p[0:1], 0.0)
    for l in range(DEPTH):
        h = rms_norm(x, mix_norm_g[l])
        x = x + hybrid_mixer(h, w_in[l], b_gate[l], q_norm_g[l], k_norm_g[l], lb_all[l],
                             hgrn_norm_g[l], conv_w[l], conv_b[l], conv_ln_g[l], conv_ln_b[l],
                             w_att_o[l], w_hgrn_o[l], w_conv_o[l], w_out[l])
        h = rms_norm(x, ffn_norm_g[l])
        x = x + hierarchical_moe(h, w_coarse[l], b_coarse[l], w_fine[l], b_fine[l],
                                 w_exp_in[l], w_exp_out[l])
    return x


_drawn_inputs = setup_inputs


def setup_inputs(seed=0):
    import zlib

    import numpy as np

    out = dict(_drawn_inputs(seed))
    spreads = {}
    factors = {'b_gate': 4.704,
     'q_norm_g': 11.907,
     'k_norm_g': 4.374,
     'hgrn_norm_g': 13.369,
     'conv_ln_b': 8.854,
     'b_coarse': 20.581,
     'b_fine': 10.177,
     'conv_b': 3.777,
     'conv_ln_g': 13.346,
     'ffn_norm_g': 4.197}
    for name, (base, spread) in spreads.items():
        noise = np.random.default_rng([zlib.crc32(name.encode()), seed]).standard_normal(out[name].shape)
        drawn = base * np.exp(spread * noise) if base else spread * noise
        out[name] = jnp.asarray(drawn.astype(out[name].dtype))
    for name, factor in factors.items():
        out[name] = (out[name] * factor).astype(out[name].dtype)
    return out
```

```python
from contextlib import ExitStack

import concourse.bass as bass
from concourse import mybir

ALU = mybir.AluOpType
ACT = mybir.ActivationFunctionType
F32 = mybir.dt.float32
I32 = mybir.dt.int32
AX_X = mybir.AxisListType.X

P = 128
NEG = -1e30
RMS_EPS = 1e-6
LN_EPS = 1e-5
LEAST_FORGET = 2.0 ** -63


class Chain:

    def __init__(self, eng, sem):
        self.eng, self.sem, self.n = eng, sem, 0

    def step(self, ins):
        ins.then_inc(self.sem, 1)
        self.n += 1
        return self.n

    def settle(self, upto=None):
        self.eng.wait_ge(self.sem, self.n if upto is None else upto)


def hybrid_decoder_layer(nc, x, mix_norm_g, w_in, b_gate, q_norm_g, k_norm_g, lb_logits, hgrn_norm_g,
                         conv_w, conv_b, conv_ln_g, conv_ln_b, w_att_o, w_hgrn_o, w_conv_o, w_out,
                         ffn_norm_g, w_coarse, b_coarse, w_fine, b_fine, w_exp_in, w_exp_out, out):
    _, SEQ, D = x.shape
    TT = SEQ // P
    KD = D // P
    HD = q_norm_g.shape[1]
    W = w_att_o.shape[1]
    CB = W // P
    AH = W // HD
    HH = W // hgrn_norm_g.shape[1]
    TAPS = conv_w.shape[1]
    G = w_coarse.shape[2]
    E = w_fine.shape[2]
    EG = E // G
    FF = w_exp_out.shape[2]
    FT = FF // P
    CHUNK = 64
    assert (SEQ, D, W, HD, HH, FF, EG) == (256, 1024, 512, 64, 4, 512, 8)
    SCALE = float(HD) ** -0.5
    S2 = TT * P

    with ExitStack() as ctx:
        def sb(name, shape, dt=F32):
            return ctx.enter_context(nc.sbuf_tensor(name, shape, dt))

        def sem(name):
            return ctx.enter_context(nc.semaphore(name))

        NSLOT = 6
        UNIT = 4096
        ring = sb("ring", [P, NSLOT, UNIT])
        xs = sb("xs", [P, TT, D])
        hT = sb("hT", [P, KD, S2])
        ident = sb("ident", [P, P])
        ones = sb("ones", [P, P])
        vecT = sb("vecT", [P, 64])
        tapT = sb("tapT", [P, TAPS * CB])
        causal = sb("causal", [P, 3, P])
        level_mask = sb("level_mask", [P, 8, P], I32)
        chunk_keep = sb("chunk_keep", [P, S2])
        w_router = sb("w_router", [P, KD, G + E])
        b_router = sb("b_router", [1, G + E])
        st = sb("st", [P, 512])
        K = 1024
        arena = sb("arena", [P, 21248])

        def at(k, n):
            o = int(k * K)
            return arena[:, o:o + n]

        def chan(k):
            return at(k, CB * S2).rearrange("p (c t) -> p c t", c=CB)

        def tok(k):
            return at(k, TT * W).rearrange("p (a w) -> p a w", a=TT)

        ps = ctx.enter_context(nc.psum_tensor("ps", [P, 8, 512], F32))

        def bank(b, n=1):
            return ps[:, b:b + n, :].rearrange("p b f -> p (b f)")

        h_tok = at(0, TT * D).rearrange("p (a d) -> p a d", a=TT)
        vec_rows = at(10.5, P)
        tap_rows = at(11, P)
        idx_s = at(2, P).bitcast(I32)
        idx_t = at(2.25, P).bitcast(I32)
        idx_x = at(2.5, P).bitcast(I32)
        hq, hk, hb = chan(0), chan(1), chan(2)
        hf = chan(3)
        Ex, Qx, Kx = [chan(3), chan(4)], [chan(5), chan(6)], [chan(7), chan(8)]
        ST = at(9, 3 * W).rearrange("p (a h t) -> p a h t", a=3, h=HH)
        hv, hg = tok(10.5), tok(11.5)
        h_sq, h_o = tok(5), tok(6)
        h_oT = chan(11.5)
        aq, ak, av = tok(12.5), tok(13.5), tok(14.5)
        a_sq = tok(4)
        qT, kT = chan(7), chan(8)
        Pm = at(0, 4 * 384).rearrange("p (h s) -> p h s", h=4)
        PT = at(2, 4 * 384).rearrange("p (h s) -> p h s", h=4)
        a_o = tok(13.5)
        a_oT = chan(12.5)
        PAD = TAPS - 1
        c_sig = chan(15.5)
        c_u = at(16.5, CB * (PAD + S2)).rearrange("p (c t) -> p c t", c=CB)
        c_acc = at(17.75, CB * S2).rearrange("p (c t) -> p c t", c=CB)
        gate = [chan(15.5), chan(16.5)]
        prod = c_acc
        merged = at(18.75, KD * S2).rearrange("p (k t) -> p k t", k=KD)

        MIXG, FFNG, BG, CVB, LNG, LNB, LB, HNG, QG, KG = 0, 8, 16, 40, 44, 48, 52, 56, 57, 58
        NVEC = 59

        s_x = sem("x_landed")
        s_small = sem("small_landed")
        s_router_w = sem("router_weights_landed")
        landed = [sem(f"slot{i}_landed") for i in range(NSLOT)]
        s_const = sem("constants_ready")
        s_pool = sem("pool_chain")
        s_dve = sem("dve_chain")
        s_act = sem("act_chain")
        s_masks = sem("level_masks_ready")
        s_ssq = sem("square_sums_ready")
        s_root = sem("roots_ready")
        s_h = sem("h_ready")
        s_hT_ps = sem("hT_in_psum")
        s_hT_odd = sem("hT_odd_tiles_ready")
        s_hT_even = sem("hT_even_tiles_ready")
        s_vec_ps = sem("vectors_in_psum")
        s_vec = sem("vectors_ready")
        s_full = sem("unit_in_psum")
        s_free = [sem("pair0_free"), sem("pair1_free")]
        s_csig = sem("conv_sigmoid_ready")
        s_taps = sem("conv_tap_done")
        s_u = sem("conv_gated_ready")
        s_f = sem("forget_ready")
        s_hf = sem("forget_sigmoid_ready")
        s_lf = sem("log_forget_ready")
        s_hq = sem("hgrn_q_ready")
        s_hi = sem("hgrn_values_ready")
        s_hg = sem("hgrn_outgate_ready")
        s_D = sem("exponents_ready")
        s_E = sem("decays_ready")
        s_K = sem("level_keys_ready")
        s_Q = sem("level_queries_ready")
        s_SC = sem("level_scores_in_psum")
        s_SCfree = sem("level_scores_taken")
        s_lb0 = sem("lb_shifted")
        s_lb1 = sem("lb_exp_ready")
        s_aq = sem("attention_inputs_ready")
        s_asq = sem("attention_squares_ready")
        s_conv_done = sem("conv_taps_complete")
        s_mean_ps = sem("conv_mean_in_psum")
        s_cdev = sem("conv_deviation_ready")
        s_csq = sem("conv_squares_ready")
        s_var_ps = sem("conv_var_in_psum")
        s_cvar = sem("conv_var_ready")
        s_croot = sem("conv_root_ready")
        s_cn = sem("conv_normalised")
        s_convT = sem("conv_out_ready")
        s_ho_ps = sem("hgrn_o_in_psum")
        s_hosq = sem("hgrn_o_squares_ready")
        s_hms = sem("hgrn_ms_ready")
        s_hroot = sem("hgrn_root_ready")
        s_hon = sem("hgrn_o_normalised")
        s_hoT_ps = sem("hgrn_oT_in_psum")
        s_hoT = sem("hgrn_oT_ready")
        s_ams = sem("attention_ms_ready")
        s_aroot = sem("attention_roots_ready")
        s_an = sem("attention_qk_normalised")
        s_qkT_ps = sem("qkT_in_psum")
        s_qkT = sem("qkT_ready")
        s_asc_ps = sem("attention_scores_in_psum")
        s_amax = sem("attention_max_ready")
        s_aexp = sem("attention_exp_ready")
        s_PT_ps = sem("PT_in_psum")
        s_PT = sem("PT_ready")
        s_ao_ps = sem("attention_o_in_psum")
        s_ao = sem("attention_o_ready")
        s_aoT_ps = sem("attention_oT_in_psum")
        s_aoT = sem("attention_oT_ready")
        s_gate = sem("gate_half_ready")
        s_gate_used = sem("gate_half_used")
        s_merged = sem("merged_ready")
        s_x2 = sem("x2_ready")
        s_ssq2 = sem("square_sums2_ready")
        s_ms2 = sem("mean_squares2_ready")
        s_root2 = sem("root2_ready")
        s_h2 = sem("h2_ready")
        s_h2T_ps = sem("h2T_in_psum")
        s_h2T_odd = sem("h2T_odd_tiles_ready")
        s_h2T_even = sem("h2T_even_tiles_ready")
        s_ms = sem("mean_squares_ready")
        s_log_ps = sem("router_logits_in_psum")
        s_rsub = sem("router_exponents_ready")
        s_rexp = sem("router_exp_ready")
        s_H_ps = sem("expert_hidden_in_psum")
        s_sil = sem("expert_silu_ready")
        s_act2 = sem("expert_act_ready")
        s_T_ps = sem("expert_actT_in_psum")
        s_T = sem("expert_actT_ready")
        s_Y_ps = sem("expert_out_in_psum")
        s_Yfree = sem("expert_out_taken")
        s_out = sem("out_stored")

        wi = w_in[0].rearrange("(k p) n -> p k n", p=P)
        IN = {n: i for i, n in enumerate(["aq", "ak", "av", "hq", "hf", "hi", "hg", "ca", "cb"])}

        def in_cols(c):
            return wi[:, :, c * W:(c + 1) * W]

        def o_rows(w):
            return w[0].rearrange("(k p) n -> p k n", p=P)

        wo = w_out[0].rearrange("(k p) n -> p k n", p=P)
        order = ["cb", "ca", "hf", "hq", "hi", "hg", "aq", "ak", "av"]
        sources = [in_cols(IN[n]) for n in order]
        for b, w in ((2, w_conv_o), (1, w_hgrn_o), (0, w_att_o)):
            sources += [in_cols(9 + 2 * b), in_cols(10 + 2 * b), o_rows(w)]
        sources += [wo[:, :, 0:W], wo[:, :, W:D]]
        NMIX = len(sources)
        L_OUT = 18
        LAST_UNIT = [*range(9), 9, 10, 12, 13, 14, 16, 17, 18, 20, 22, 22]
        exp_in = w_exp_in[0].rearrange("(q j) d n -> q j d n", j=2)
        exp_out = w_exp_out[0].rearrange("(q j) d n -> q j d n", j=2)

        def slot(l):
            return ring[:, l % NSLOT, :]

        def wcols(l):
            return slot(l).rearrange("p (k n) -> p k n", k=KD)

        def wrows(l):
            return slot(l).rearrange("p (k n) -> p k n", k=CB)

        def wait_landed(eng, l):
            eng.wait_ge(landed[l % NSLOT], 16 * (l // NSLOT + 1))

        h2 = at(0, TT * D).rearrange("p (a d) -> p a d", a=TT)
        e_sil = at(4, FF)
        e_act = at(4.5, FF)
        e_actT = at(5, FF).rearrange("p (f t) -> p f t", f=FT)
        NL = G + E
        RO = 6.0

        def rt(i, n):
            return at(RO + i / 8, TT * n).rearrange("p (a e) -> p a e", a=TT)
        logits = rt(0, NL)
        r_fine, r_pen, r_oh1, r_oh2, r_tmp, combine = (rt(i, E) for i in range(1, 7))
        r_iota = rt(7, E)
        r_s = [at(RO + 1 + i / 64, TT).rearrange("p (a e) -> p a e", a=TT) for i in range(12)]
        r_grp = at(RO + 1.25, TT * G).rearrange("p (a e) -> p a e", a=TT)
        r_e4 = at(RO + 1.3, TT * G).rearrange("p (a e) -> p a e", a=TT)
        r_i4 = at(RO + 1.35, TT * G).rearrange("p (a e) -> p a e", a=TT)
        r_t4 = at(RO + 1.4, TT * G).rearrange("p (a e) -> p a e", a=TT)

        block = ctx.enter_context(nc.Block())

        EXP = 3

        @block.sync
        def _(sp):
            for l, src in enumerate(sources):
                if l >= NSLOT:
                    sp.wait_ge(s_full, LAST_UNIT[l - NSLOT] + 1)
                k = KD if src.shape[1] == KD else CB
                sp.dma_start(slot(l).rearrange("p (k n) -> p k n", k=k), src).then_inc(landed[l % NSLOT], 16)
            def load_expert(q, j, part):
                l = NMIX + EXP * j + part
                if part < 2:
                    src = exp_in[bass.ds(q, 1), j, :, part * FF:(part + 1) * FF].rearrange("a (k p) n -> p (a k) n", p=P)
                    dst = wcols(l)
                else:
                    src = exp_out[bass.ds(q, 1), j, :, :].rearrange("a (k p) n -> p (a k) n", p=P)
                    dst = wrows(l)
                sp.dma_start(dst, src).then_inc(landed[l % NSLOT], 16)

            for j in range(2):
                for part in range(EXP):
                    sp.wait_ge(s_full, LAST_UNIT[NMIX - NSLOT + EXP * j + part] + 1)
                    load_expert(0, j, part)
            with nc.Fori(1, E // 2, 1, engines=[sp.engine]) as q:
                for j in range(2):
                    for part in range(EXP):
                        sp.wait_ge(s_H_ps if part < 2 else s_Y_ps, q * (2 * TT) + (j + 1 - 2) * TT)
                        load_expert(q, j, part)
            sp.wait_ge(s_Yfree, 2 * E + 1)
            sp.dma_start(out[0].rearrange("(a p) d -> p a d", p=P), xs[:, :, :]).then_inc(s_out, 16)
            sp.wait_ge(s_out, 16)

        @block.gpsimd
        def _(pool):
            ch = Chain(pool, s_pool)
            ch.step(nc.gpsimd.memset(ident[:], 0.0))
            ch.step(nc.gpsimd.memset(causal[:], 0.0))
            ch.step(nc.gpsimd.iota(idx_s, [[0, P]], base=0, channel_multiplier=1))
            ch.step(nc.gpsimd.iota(idx_t, [[1, P]], base=0, channel_multiplier=0))
            ch.step(nc.gpsimd.memset(ones[:], 1.0))
            ch.step(nc.gpsimd.memset(chunk_keep[:], 1.0))
            ch.step(nc.gpsimd.memset(c_u[:, :, 0:PAD], 0.0))
            ch.settle()
            nc.gpsimd.affine_select(out=ident[:], in_=ident[:], compare_op=ALU.not_equal, fill=1.0, base=0,
                                    pattern=[[-1, P]], channel_multiplier=1).then_inc(s_const, 1)
            for c in (0, 2):
                nc.gpsimd.affine_select(out=causal[:, c, :], in_=causal[:, c, :], compare_op=ALU.is_ge, fill=NEG,
                                        base=0, pattern=[[-1, P]], channel_multiplier=1).then_inc(s_const, 1)
            nc.gpsimd.memset(chunk_keep[:].rearrange("p (c i) -> p c i", i=CHUNK)[:, :, 0:1], 0.0)\
                .then_inc(s_const, 1)
            pool.wait_ge(s_masks, 1)
            nc.gpsimd.affine_select(out=idx_x, in_=idx_x, compare_op=ALU.is_ge, fill=4096.0, base=0,
                                    pattern=[[1, P]], channel_multiplier=-1).then_inc(s_const, 1)
            for i in range(8):
                m = 128 >> i
                pool.wait_ge(s_E, i + 1)
                if i >= 2:
                    pool.wait_ge(s_SC, i - 1)
                kv = hk.rearrange("p c t -> p (c t)").rearrange("p (b a m) -> p b a m", a=2, m=m)
                ev = Ex[i % 2].rearrange("p c t -> p (c t)").rearrange("p (b a m) -> p b a m", a=2, m=m)
                ov = Kx[i % 2].rearrange("p c t -> p (c t)").rearrange("p (b a m) -> p b a m", a=2, m=m)
                if i < 2:
                    nc.gpsimd.memset(ov[:, :, 1, :], 0.0).then_inc(s_K, 1)
                nc.gpsimd.tensor_tensor(ov[:, :, 0, :], kv[:, :, 0, :], ev[:, :, 0, :], ALU.mult).then_inc(s_K, 1)

        @block.scalar
        def _(act):
            ch = Chain(act, s_act)
            for a in range(TT):
                act.dma_start(xs[:, a, :], x[0, a * P:(a + 1) * P, :]).then_inc(s_x, 16)
            rows = [(MIXG, mix_norm_g, 8), (FFNG, ffn_norm_g, 8), (BG, b_gate, 24), (CVB, conv_b, 4),
                    (LNG, conv_ln_g, 4), (LNB, conv_ln_b, 4), (LB, lb_logits, 4), (HNG, hgrn_norm_g, 1)]
            for r, v, n in rows:
                act.dma_start(vec_rows[r:r + n, :], v[0].rearrange("(r p) -> r p", p=P)).then_inc(s_small, 16)
            for r, v in ((QG, q_norm_g), (KG, k_norm_g)):
                for i in range(P // HD):
                    act.dma_start(vec_rows[r:r + 1, i * HD:(i + 1) * HD], v[0:1, :]).then_inc(s_small, 16)
            act.dma_start(tap_rows[0:TAPS * CB, :], conv_w[0].rearrange("j (c p) -> (j c) p", p=P)).then_inc(s_small, 16)
            act.dma_start(b_router[0:1, 0:G], b_coarse[0:1, :]).then_inc(s_router_w, 16)
            act.dma_start(b_router[0:1, G:G + E], b_fine[0:1, :]).then_inc(s_router_w, 16)
            act.dma_start(w_router[:, :, 0:G], w_coarse[0].rearrange("(k p) n -> p k n", p=P)).then_inc(s_router_w, 16)
            act.dma_start(w_router[:, :, G:G + E], w_fine[0].rearrange("(k p) n -> p k n", p=P)).then_inc(s_router_w, 16)
            act.wait_ge(s_x, 16 * TT)
            for a in range(TT):
                nc.scalar.activation(at(4 + a, D), xs[:, a, :], ACT.Square, accum_out=st[:, a:a + 1]).then_inc(s_ssq, 1)
            act.wait_ge(s_ms, 1)
            nc.scalar.activation(st[:, 6:8], st[:, 4:6], ACT.Sqrt).then_inc(s_root, 1)
            act.wait_ge(s_vec, 1)
            for k in range(1, KD, 2):
                act.wait_ge(s_hT_ps, k // 2 + 1)
                nc.scalar.activation(hT[:, k, :], bank(4 + k // 2)[:, S2:2 * S2], ACT.Copy,
                                     scale=vecT[:, MIXG + k:MIXG + k + 1]).then_inc(s_hT_odd, 1)
            act.wait_ge(s_lb0, 1)
            nc.scalar.activation(st[:, 20:24], st[:, 16:20], ACT.Exp).then_inc(s_lb1, 1)

            def unit(u):
                return bank(2 * (u % 2), 2)

            act.wait_ge(s_full, 1)
            nc.scalar.activation(c_sig, unit(0).rearrange("p (c t) -> p c t", c=CB), ACT.Sigmoid).then_inc(s_free[0], 1)
            act.wait_ge(s_full, 3)
            nc.scalar.activation(hf, unit(2).rearrange("p (c t) -> p c t", c=CB), ACT.Sigmoid).then_inc(s_free[0], 1)
            act.wait_ge(s_full, 4)
            nc.scalar.activation(hq, unit(3).rearrange("p (c t) -> p c t", c=CB), ACT.Silu).then_inc(s_free[1], 1)
            act.wait_ge(s_full, 5)
            nc.scalar.activation(hv, unit(4).rearrange("p (a w) -> p a w", a=TT), ACT.Copy).then_inc(s_free[0], 1)
            act.wait_ge(s_full, 6)
            nc.scalar.activation(hg, unit(5).rearrange("p (a w) -> p a w", a=TT), ACT.Silu).then_inc(s_free[1], 1)
            for j, buf in enumerate((aq, ak, av)):
                act.wait_ge(s_full, 7 + j)
                nc.scalar.activation(buf, unit(6 + j).rearrange("p (a w) -> p a w", a=TT), ACT.Copy)\
                    .then_inc(s_free[j % 2], 1)
            act.wait_ge(s_f, 1)
            nc.scalar.activation(hf, hf, ACT.Ln).then_inc(s_lf, 1)
            for i in range(8):
                act.wait_ge(s_D, i + 1)
                nc.scalar.activation(Ex[i % 2], Ex[i % 2], ACT.Exp).then_inc(s_E, 1)

            act.wait_ge(s_cdev, 1)
            nc.scalar.activation(c_sig, c_acc, ACT.Square).then_inc(s_csq, 1)
            act.wait_ge(s_cvar, 1)
            nc.scalar.activation(c_u[:, 0, 0:S2], c_u[:, 0, 0:S2], ACT.Sqrt).then_inc(s_croot, 1)
            act.wait_ge(s_ho_ps, 1)
            nc.scalar.activation(h_sq, bank(4, 2).rearrange("p (a w) -> p a w", a=TT), ACT.Square).then_inc(s_hosq, 1)
            act.wait_ge(s_hms, 1)
            nc.scalar.activation(st[:, 48:56], st[:, 40:48], ACT.Sqrt).then_inc(s_hroot, 1)
            for j, buf in enumerate((aq, ak)):
                if j == 0:
                    act.wait_ge(s_SC, 8)
                act.wait_ge(s_free[j % 2], 4 if j == 0 else 4)
                if j:
                    act.wait_ge(s_ams, 1)
                nc.scalar.activation(a_sq, buf, ACT.Square).then_inc(s_asq, 1)
            act.wait_ge(s_ams, 2)
            nc.scalar.activation(st[:, 96:128], st[:, 64:96], ACT.Sqrt).then_inc(s_aroot, 1)
            act.wait_ge(s_cn, 1)
            for c in range(CB):
                nc.scalar.activation(c_acc[:, c, :], c_acc[:, c, :], ACT.Silu, bias=vecT[:, LNB + c:LNB + c + 1],
                                     scale=vecT[:, LNG + c:LNG + c + 1]).then_inc(s_convT, 1)
            def gates(b, n):
                for half in range(2):
                    u = [9, 13, 17][n] + half
                    act.wait_ge(s_full, u + 1)
                    if n == 0:
                        act.wait_ge(s_convT, 4)
                    else:
                        act.wait_ge(s_free[(u - 2) % 2], (u - 2) // 2 + 1)
                    for c in range(CB):
                        last = nc.scalar.activation(gate[half][:, c, :], unit(u)[:, c * S2:(c + 1) * S2], ACT.Sigmoid,
                                                    bias=vecT[:, BG + 8 * b + 4 * half + c:BG + 8 * b + 4 * half + c + 1])
                        if c < CB - 1:
                            last.then_inc(s_act, 1)
                    last.then_inc(s_free[u % 2], 1)

            def hgrn_oT():
                act.wait_ge(s_hoT_ps, 1)
                nc.scalar.activation(h_oT, bank(6, 2).rearrange("p (c t) -> p c t", c=CB), ACT.Copy,
                                     scale=vecT[:, HNG:HNG + 1]).then_inc(s_hoT, 1)

            def softmax_half(g):
                act.wait_ge(s_amax, g + 1)
                for h in range(4):
                    for a in range(TT):
                        w = slice(0, P) if a == 0 else slice(P, 3 * P)
                        nc.scalar.activation(Pm[:, h, w], Pm[:, h, w], ACT.Exp, scale=SCALE,
                                             bias=st[:, 144 + 2 * h + a:145 + 2 * h + a],
                                             accum_out=st[:, 160 + 8 * g + 2 * h + a:161 + 8 * g + 2 * h + a])\
                            .then_inc(s_aexp, 1)
                act.wait_ge(s_PT_ps, g + 1)
                if g:
                    act.wait_ge(s_ao_ps, g)
                nc.scalar.activation(PT, ps[:, 4:8, 0:384], ACT.Copy).then_inc(s_PT, 1)

            hgrn_oT()
            gates(2, 0)
            softmax_half(0)
            softmax_half(1)
            gates(1, 1)
            act.wait_ge(s_aoT_ps, 1)
            nc.scalar.activation(a_oT, bank(6, 2).rearrange("p (c t) -> p c t", c=CB), ACT.Copy).then_inc(s_aoT, 1)
            gates(0, 2)

            act.wait_ge(s_x2, 2)
            for a in range(TT):
                nc.scalar.activation(at(2 + a, D), xs[:, a, :], ACT.Square, accum_out=st[:, 200 + a:201 + a]).then_inc(s_ssq2, 1)
            act.wait_ge(s_ms2, 1)
            nc.scalar.activation(st[:, 206:208], st[:, 204:206], ACT.Sqrt).then_inc(s_root2, 1)
            for k in range(1, KD, 2):
                act.wait_ge(s_h2T_ps, k // 2 + 1)
                nc.scalar.activation(hT[:, k, :], bank(4 + k // 2)[:, S2:2 * S2], ACT.Copy,
                                     scale=vecT[:, FFNG + k:FFNG + k + 1]).then_inc(s_h2T_odd, 1)
            act.wait_ge(s_rsub, 1)
            nc.scalar.activation(r_e4, r_e4, ACT.Exp).then_inc(s_rexp, 1)
            act.wait_ge(s_rsub, 2)
            nc.scalar.activation(r_s[5], r_s[5], ACT.Exp).then_inc(s_rexp, 1)
            with nc.Fori(0, E, 1, engines=[act.engine]) as e:
                for a in range(TT):
                    act.wait_ge(s_H_ps, e * TT + (a + 1))
                    nc.scalar.activation(e_sil, bank(0), ACT.Silu).then_inc(s_sil, 1)
                    act.wait_ge(s_T_ps, e * TT + (a + 1))
                    nc.scalar.activation(e_actT.rearrange("p f t -> p (f t)"), bank(2), ACT.Copy).then_inc(s_T, 1)

        @block.vector
        def _(dve):
            v = nc.vector
            ch = Chain(dve, s_dve)
            s = ch.step

            def unit(u):
                return bank(2 * (u % 2), 2)

            dve.wait_ge(s_pool, 7)
            v.tensor_tensor(idx_x, idx_s, idx_t, ALU.bitwise_xor).then_inc(s_masks, 1)
            dve.wait_ge(s_ssq, 2)
            v.tensor_scalar(st[:, 4:6], st[:, 0:2], 1.0 / D, RMS_EPS, ALU.mult, ALU.add).then_inc(s_ms, 1)
            dve.wait_ge(s_root, 1)
            s(v.reciprocal(st[:, 8:10], st[:, 6:8]))
            ch.settle()
            for a in range(TT):
                v.tensor_scalar(h_tok[:, a, :], xs[:, a, :], st[:, 8 + a:9 + a], None, ALU.mult).then_inc(s_h, 1)
            dve.wait_ge(s_vec_ps, 1)
            v.tensor_copy(vecT[:, 0:NVEC], bank(0)[:, 0:NVEC])
            v.tensor_copy(tapT[:], bank(0)[:, P:P + TAPS * CB]).then_inc(s_vec, 1)
            for k in range(0, KD, 2):
                dve.wait_ge(s_hT_ps, k // 2 + 1)
                if k == 0:
                    dve.wait_ge(s_vec, 1)
                dve.wait_ge(s_hT_odd, k // 2 + 1)
                v.tensor_scalar(hT[:, k, :], bank(4 + k // 2)[:, 0:S2], vecT[:, MIXG + k:MIXG + k + 1], None,
                                ALU.mult).then_inc(s_hT_even, 1)
            dve.wait_ge(s_const, 5)
            for i in range(8):
                s(v.tensor_scalar(level_mask[:, i, :], idx_x, float(P >> i), None, ALU.is_lt))
            lbt = vecT[:, LB:LB + HH]
            v.tensor_tensor(st[:, 16:20], lbt, lbt, ALU.subtract).then_inc(s_lb0, 1)
            dve.wait_ge(s_lb1, 1)
            s(v.reciprocal(st[:, 24:28], st[:, 20:24]))
            ch.settle()
            s(v.tensor_tensor(st[:, 28:32], st[:, 20:24], st[:, 24:28], ALU.mult))
            ch.settle()
            s(v.tensor_tensor(st[:, 28:32], st[:, 28:32], st[:, 28:32], ALU.subtract))
            ch.settle()
            s(v.tensor_scalar(st[:, 28:32], st[:, 28:32], 0.0, None, ALU.max))
            ch.settle()
            s(v.tensor_scalar(st[:, 32:36], st[:, 28:32], -1.0, 1.0, ALU.mult, ALU.add))
            s(v.tensor_scalar(st[:, 36:40], st[:, 28:32], 1.0, -1.0, ALU.mult, ALU.add))
            ch.settle()
            lb, one_lb, lb_one = 28, 32, 36
            dve.wait_ge(s_free[0], 1)
            dve.wait_ge(s_full, 2)
            v.tensor_tensor(c_u[:, :, PAD:PAD + S2], unit(1).rearrange("p (c t) -> p c t", c=CB), c_sig, ALU.mult)\
                .then_inc(s_free[1], 1)
            dve.wait_ge(s_free[1], 1)
            for c in range(CB):
                v.tensor_scalar(c_acc[:, c, :], c_u[:, c, 0:S2], tapT[:, c:c + 1], vecT[:, CVB + c:CVB + c + 1],
                                ALU.mult, ALU.add).then_inc(s_taps, 1)
            with nc.Fori(1, TAPS, 1, engines=[dve.engine]) as j:
                for c in range(CB):
                    dve.wait_ge(s_taps, j * CB + (c + 1 - CB))
                    v.scalar_tensor_tensor(out=c_acc[:, c, :], in0=c_u[:, c, bass.ds(j, S2)],
                                           scalar=tapT[:, bass.ds(j * CB + c, 1)], in1=c_acc[:, c, :],
                                           op0=ALU.mult, op1=ALU.add).then_inc(s_taps, 1)
            dve.wait_ge(s_free[0], 2)
            for h in range(HH):
                s(v.tensor_scalar(hk[:, h, :], hf[:, h, :], st[:, lb_one + h:lb_one + h + 1],
                                  st[:, one_lb + h:one_lb + h + 1], ALU.mult, ALU.add))
            ch.settle()
            for h in range(HH):
                s(v.tensor_scalar(hf[:, h, :], hf[:, h, :], st[:, one_lb + h:one_lb + h + 1],
                                  st[:, lb + h:lb + h + 1], ALU.mult, ALU.add))
            ch.settle()
            v.tensor_scalar(hf, hf, LEAST_FORGET, None, ALU.max).then_inc(s_f, 1)
            dve.wait_ge(s_mean_ps, 1)
            mean = bank(4)[:, 0:S2]
            v.scalar_tensor_tensor(out=c_acc, in0=mean.unsqueeze(1).broadcast_to([P, CB, S2]), scalar=-1.0 / W,
                                   in1=c_acc, op0=ALU.mult, op1=ALU.add).then_inc(s_cdev, 1)
            dve.wait_ge(s_lf, 1)
            for h in range(HH):
                s(v.tensor_tensor_scan(hb[:, h, :], chunk_keep[:], hf[:, h, :], 0.0, ALU.mult, ALU.add))
            ch.settle()

            def halves(t, m):
                return t.rearrange("p c t -> p (c t)").rearrange("p (b a m) -> p b a m", a=2, m=m)

            def exponents(i):
                m = P >> i
                if i >= 2:
                    dve.wait_ge(s_K, 2 if i == 2 else i + 1)
                    dve.wait_ge(s_Q, i - 1)
                D = Ex[i % 2]
                dv, bv = halves(D, m), halves(hb, m)
                if m <= CHUNK:
                    nb = HH * S2 // (2 * m)
                    ref = bv[:, :, 0, m - 1:m].broadcast_to([P, nb, m])
                    if m < CHUNK:
                        v.tensor_tensor(dv[:, :, 1, :], bv[:, :, 1, :], ref, ALU.subtract)
                    else:
                        v.tensor_copy(dv[:, :, 1, :], bv[:, :, 1, :])
                    v.tensor_tensor(dv[:, :, 0, :], ref, bv[:, :, 0, :], ALU.subtract).then_inc(s_D, 1)
                else:
                    dc = D.rearrange("p h (c t) -> p h c t", t=CHUNK)
                    bc = hb.rearrange("p h (c t) -> p h c t", t=CHUNK)

                    def end(c):
                        return bc[:, :, c, CHUNK - 1:CHUNK].broadcast_to([P, HH, CHUNK])
                    s(v.tensor_tensor(dc[:, :, 0, :], end(0), bc[:, :, 0, :], ALU.subtract))
                    v.tensor_tensor(dc[:, :, 1, :], end(1), bc[:, :, 1, :], ALU.subtract)
                    v.tensor_copy(dc[:, :, 2, :], bc[:, :, 2, :])
                    v.tensor_tensor(dc[:, :, 3, :], bc[:, :, 3, :], end(2), ALU.add)
                    ch.settle()
                    v.tensor_tensor(dc[:, :, 0, :], dc[:, :, 0, :], end(1), ALU.add).then_inc(s_D, 1)

            def queries(i):
                m = P >> i
                dve.wait_ge(s_E, i + 1)
                if i == 0:
                    dve.wait_ge(s_free[1], 2)
                if i >= 2:
                    dve.wait_ge(s_SC, i - 1)
                ov, qv, ev = halves(Qx[i % 2], m), halves(hq, m), halves(Ex[i % 2], m)
                if i < 2:
                    s(v.memset(ov[:, :, 0, :], 0.0))
                    ch.settle()
                v.tensor_tensor(ov[:, :, 1, :], qv[:, :, 1, :], ev[:, :, 1, :], ALU.mult).then_inc(s_Q, 1)

            def take(i):
                b = 4 + 2 * (i % 2)
                dve.wait_ge(s_SC, i + 1)
                if i == 0:
                    v.tensor_copy(ST[:, 2, :, :], bank(b).rearrange("p (h t) -> p h t", h=HH)).then_inc(s_SCfree, 1)
                else:
                    if i == 1:
                        s(v.memset(ST[:, 0:2, :, :], 0.0))
                        ch.settle()
                    else:
                        dve.wait_ge(s_SCfree, i)
                    mask = level_mask[:, i - 1, :].unsqueeze(1).broadcast_to([P, 2 * HH, P])
                    v.copy_predicated(ST[:, 0:2, :, :].rearrange("p a h t -> p (a h) t"), mask,
                                      bank(b, 2).rearrange("p (g t) -> p g t", t=P)).then_inc(s_SCfree, 1)

            exponents(0)
            for i in range(8):
                if i + 1 < 8:
                    exponents(i + 1)
                queries(i)
                if i:
                    take(i - 1)
            take(7)
            take(8)
            dve.wait_ge(s_var_ps, 1)
            root = c_u[:, 0, 0:S2]
            v.tensor_scalar(root, bank(7)[:, 0:S2], 1.0 / W, LN_EPS, ALU.mult, ALU.add).then_inc(s_cvar, 1)
            dve.wait_ge(s_croot, 1)
            s(v.reciprocal(c_u[:, 1, 0:S2], root))
            ch.settle()
            v.tensor_tensor(c_acc, c_acc, c_u[:, 1:2, 0:S2].broadcast_to([P, CB, S2]), ALU.mult).then_inc(s_cn, 1)
            dve.wait_ge(s_hosq, 1)
            s(v.tensor_reduce(st[:, 40:48], h_sq.rearrange("p a (h w) -> p (a h) w", w=P), AX_X, ALU.add))
            ch.settle()
            v.tensor_scalar(st[:, 40:48], st[:, 40:48], 1.0 / P, RMS_EPS, ALU.mult, ALU.add).then_inc(s_hms, 1)
            dve.wait_ge(s_hroot, 1)
            s(v.reciprocal(st[:, 56:64], st[:, 48:56]))
            ch.settle()
            s(v.tensor_tensor(h_o.rearrange("p a (h w) -> p (a h) w", w=P),
                              bank(4, 2).rearrange("p (g w) -> p g w", w=P),
                              st[:, 56:64].unsqueeze(2).broadcast_to([P, TT * HH, P]), ALU.mult))
            ch.settle()
            dve.wait_ge(s_free[1], 3)
            v.tensor_tensor(h_o, h_o, hg, ALU.mult).then_inc(s_hon, 1)
            for j in range(2):
                dve.wait_ge(s_asq, j + 1)
                s(v.tensor_reduce(st[:, 64 + 16 * j:80 + 16 * j], a_sq.rearrange("p a (h w) -> p (a h) w", w=HD),
                                  AX_X, ALU.add))
                ch.settle()
                v.tensor_scalar(st[:, 64 + 16 * j:80 + 16 * j], st[:, 64 + 16 * j:80 + 16 * j], 1.0 / HD, RMS_EPS,
                                ALU.mult, ALU.add).then_inc(s_ams, 1)
            dve.wait_ge(s_aroot, 1)
            s(v.reciprocal(st[:, 96:128], st[:, 96:128]))
            ch.settle()
            for j, buf in enumerate((aq, ak)):
                b = buf.rearrange("p a (h w) -> p (a h) w", w=HD)
                v.tensor_tensor(b, b, st[:, 96 + 16 * j:112 + 16 * j].unsqueeze(2).broadcast_to([P, TT * AH, HD]),
                                ALU.mult).then_inc(s_an, 1)
            for j, (buf, g) in enumerate(((qT, QG), (kT, KG))):
                dve.wait_ge(s_qkT_ps, j + 1)
                v.tensor_scalar(buf, bank(4 + 2 * j, 2)
                                .rearrange("p (c t) -> p c t", c=CB), vecT[:, g:g + 1], None, ALU.mult)\
                    .then_inc(s_qkT, 1)
            def merge(n):
                for half in range(2):
                    u = [11, 15, 19][n] + half
                    dve.wait_ge(s_full, u + 1)
                    dve.wait_ge(s_free[(u - 2) % 2], (u - 2) // 2 + 1)
                    y = unit(u).rearrange("p (c t) -> p c t", c=CB)
                    m = merged[:, 4 * half:4 * half + 4, :]
                    to = m if n == 0 else prod
                    if n:
                        dve.wait_ge(s_gate_used, 2 * (n - 1) + half)
                    v.tensor_tensor(to, gate[half], y, ALU.mult).then_inc(s_free[u % 2], 1)
                    dve.wait_ge(s_free[u % 2], u // 2 + 1)
                    if n:
                        v.tensor_tensor(m, m, prod, ALU.add).then_inc(s_gate_used, 1)

            merge(0)
            for g in range(2):
                dve.wait_ge(s_asc_ps, g + 1)
                if g:
                    dve.wait_ge(s_PT_ps, 1)
                s(v.tensor_tensor(Pm, ps[:, 4:8, 0:384],
                                  causal[:].rearrange("p a s -> p (a s)").unsqueeze(1).broadcast_to([P, 4, 384]), ALU.add))
                ch.settle()
                mx = st[:, 128:136].rearrange("p (h a) -> p h a", a=TT)
                s(v.tensor_reduce(mx[:, :, 0], Pm[:, :, 0:P], AX_X, ALU.max))
                s(v.tensor_reduce(mx[:, :, 1], Pm[:, :, P:3 * P], AX_X, ALU.max))
                ch.settle()
                v.tensor_scalar(st[:, 144:152], st[:, 128:136], -SCALE, None, ALU.mult).then_inc(s_amax, 1)
                dve.wait_ge(s_aexp, 8 * (g + 1))
                s(v.reciprocal(st[:, 176 + 8 * g:184 + 8 * g], st[:, 160 + 8 * g:168 + 8 * g]))
                ch.settle()
                dve.wait_ge(s_ao_ps, g + 1)
                r = st[:, 176 + 8 * g:184 + 8 * g].rearrange("p (h a) -> p h a", a=TT)
                for a in range(TT):
                    v.tensor_tensor(a_o[:, a, 256 * g:256 * g + 256].rearrange("p (h w) -> p h w", w=HD),
                                    bank(4 + a)[:, 0:256].rearrange("p (h w) -> p h w", w=HD),
                                    r[:, :, a:a + 1].broadcast_to([P, 4, HD]), ALU.mult).then_inc(s_ao, 1)
            merge(1)
            merge(2)
            for a in range(TT):
                u = 21 + a
                dve.wait_ge(s_full, u + 1)
                v.tensor_tensor(xs[:, a, :], xs[:, a, :], unit(u), ALU.add).then_inc(s_x2, 1)
            dve.wait_ge(s_ssq2, 2)
            v.tensor_scalar(st[:, 204:206], st[:, 200:202], 1.0 / D, RMS_EPS, ALU.mult, ALU.add).then_inc(s_ms2, 1)
            dve.wait_ge(s_root2, 1)
            s(v.reciprocal(st[:, 208:210], st[:, 206:208]))
            ch.settle()
            for a in range(TT):
                v.tensor_scalar(h2[:, a, :], xs[:, a, :], st[:, 208 + a:209 + a], None, ALU.mult).then_inc(s_h2, 1)
            for k in range(0, KD, 2):
                dve.wait_ge(s_h2T_ps, k // 2 + 1)
                dve.wait_ge(s_h2T_odd, k // 2 + 1)
                v.tensor_scalar(hT[:, k, :], bank(4 + k // 2)[:, 0:S2], vecT[:, FFNG + k:FFNG + k + 1], None,
                                ALU.mult).then_inc(s_h2T_even, 1)

            def t3(o, a, b, op):
                s(v.tensor_tensor(o, a, b, op))
                ch.settle()

            def t1(o, a, s1, s2, op0, op1=None):
                s(v.tensor_scalar(o, a, s1, s2, op0, op1) if op1 is not None else v.tensor_scalar(o, a, s1, None, op0))
                ch.settle()

            def red(o, a, op):
                s(v.tensor_reduce(o, a, AX_X, op))
                ch.settle()

            def one_hot(o, vals, top, index, tmp, first, n):
                t3(tmp, vals, top.broadcast_to([P, TT, n]), ALU.is_equal)
                t1(tmp, tmp, -4096.0, 4096.0, ALU.mult, ALU.add)
                t3(tmp, tmp, index, ALU.add)
                red(first, tmp, ALU.min)
                t3(o, index, first.broadcast_to([P, TT, n]), ALU.is_equal)

            for j in range(E):
                last = v.memset(r_iota[:, :, j:j + 1], float(j))
                s(last)
            for j in range(G):
                s(v.memset(r_i4[:, :, j:j + 1], float(j)))
            dve.wait_ge(s_log_ps, 1)
            s(v.tensor_copy(logits, bank(0)[:, 0:TT * 64].rearrange("p (a e) -> p a e", a=TT)[:, :, 0:NL]))
            ch.settle()
            lc, lf = logits[:, :, 0:G], logits[:, :, G:NL]
            red(r_s[0], lc, ALU.max)
            one_hot(r_grp, lc, r_s[0], r_i4, r_t4, r_s[1], G)
            v.tensor_tensor(r_e4, lc, r_s[0].broadcast_to([P, TT, G]), ALU.subtract).then_inc(s_rsub, 1)
            grp_e = r_grp.unsqueeze(3).broadcast_to([P, TT, G, EG])

            def by_group(t):
                return t.rearrange("p a (g e) -> p a g e", g=G)
            for a in range(TT):
                s(v.tensor_copy(by_group(r_pen)[:, a], grp_e[:, a]))
            ch.settle()
            t3(r_fine, lf, r_pen, ALU.mult)
            t1(r_pen, r_pen, -NEG, NEG, ALU.mult, ALU.add)
            t3(r_fine, r_fine, r_pen, ALU.add)
            red(r_s[2], r_fine, ALU.max)
            one_hot(r_oh1, r_fine, r_s[2], r_iota, r_tmp, r_s[3], E)
            t1(r_tmp, r_oh1, 2 * NEG, None, ALU.mult)
            t3(r_fine, r_fine, r_tmp, ALU.add)
            red(r_s[4], r_fine, ALU.max)
            one_hot(r_oh2, r_fine, r_s[4], r_iota, r_tmp, r_s[3], E)
            v.tensor_tensor(r_s[5], r_s[4], r_s[2], ALU.subtract).then_inc(s_rsub, 1)
            dve.wait_ge(s_rexp, 2)
            red(r_s[6], r_e4, ALU.add)
            t1(r_s[7], r_s[5], 1.0, None, ALU.add)
            t3(r_s[8], r_s[7], r_s[6], ALU.mult)
            s(v.reciprocal(r_s[9], r_s[8]))
            ch.settle()
            t3(r_s[10], r_s[9], r_s[5], ALU.mult)
            t3(r_oh1, r_oh1, r_s[9].broadcast_to([P, TT, E]), ALU.mult)
            t3(r_oh2, r_oh2, r_s[10].broadcast_to([P, TT, E]), ALU.mult)
            v.tensor_tensor(combine, r_oh1, r_oh2, ALU.add).then_inc(s_Yfree, 1)
            dve.wait_ge(s_Yfree, 1)
            with nc.Fori(0, E, 1, engines=[dve.engine]) as e:
                for a in range(TT):
                    dve.wait_ge(s_sil, e * TT + (a + 1))
                    v.tensor_tensor(e_act, e_sil, bank(1), ALU.mult).then_inc(s_act2, 1)
                    dve.wait_ge(s_Y_ps, e * TT + (a + 1))
                    v.scalar_tensor_tensor(out=xs[:, a, :], in0=bank(4, 2), scalar=combine[:, a, bass.ds(e, 1)],
                                           in1=xs[:, a, :], op0=ALU.mult, op1=ALU.add).then_inc(s_Yfree, 1)
                    dve.wait_ge(s_Yfree, e * TT + (a + 2))


        @block.tensor
        def _(pe):
            mm, tr = nc.tensor.matmul, nc.tensor.transpose
            pe.wait_ge(s_const, 1)
            pe.wait_ge(s_small, 16 * 13)
            tr(bank(0)[:, 0:NVEC], vec_rows[0:NVEC, :], ident[0:NVEC, 0:NVEC])
            n = TAPS * CB
            tr(bank(0)[:, P:P + n], tap_rows[0:n, :], ident[0:n, 0:n]).then_inc(s_vec_ps, 1)

            def turn(src, ready, done):
                pe.wait_ge(ready, TT)
                for k in range(KD):
                    for a in range(TT):
                        last = tr(bank(4 + k // 2)[:, (k % 2) * S2 + a * P:(k % 2) * S2 + (a + 1) * P],
                                  src[:, a, k * P:(k + 1) * P], ident[:])
                    if k % 2:
                        last.then_inc(done, 1)

            turn(h_tok, s_h, s_hT_ps)
            pe.wait_ge(s_hT_odd, KD // 2)
            pe.wait_ge(s_hT_even, KD // 2)

            def begin(u):
                if u == 0:
                    pe.wait_ge(s_vec, 1)
                if u >= 2:
                    pe.wait_ge(s_free[u % 2], u // 2)
                return bank(2 * (u % 2), 2)

            def cols_by_tokens(u, l, rhs=None):
                o = begin(u)
                wait_landed(pe, l)
                w = wcols(l)
                for c in range(CB):
                    for k in range(KD):
                        last = mm(o[:, c * S2:(c + 1) * S2], w[:, k, c * P:(c + 1) * P], hT[:, k, :],
                                  start=k == 0, stop=k == KD - 1)
                last.then_inc(s_full, 1)

            def tokens_by_cols(u, l):
                o = begin(u)
                wait_landed(pe, l)
                w = wcols(l)
                for a in range(TT):
                    for k in range(KD):
                        last = mm(o[:, a * W:(a + 1) * W], hT[:, k, a * P:(a + 1) * P], w[:, k, :],
                                  start=k == 0, stop=k == KD - 1)
                last.then_inc(s_full, 1)

            def branch(u0, l, oT):
                w = wrows(l)
                wait_landed(pe, l)
                for half in range(2):
                    o = begin(u0 + half)
                    for c in range(CB):
                        for k in range(CB):
                            last = mm(o[:, c * S2:(c + 1) * S2], w[:, k, half * W + c * P:half * W + (c + 1) * P],
                                      oT[:, k, :], start=k == 0, stop=k == CB - 1)
                    last.then_inc(s_full, 1)

            def level(i):
                if i < 8:
                    q, k = Qx[i % 2], Kx[i % 2]
                    pe.wait_ge(s_Q, i + 1)
                    pe.wait_ge(s_K, i + (2 if i == 0 else 3))
                else:
                    q, k = hq, hk
                if i >= 2:
                    pe.wait_ge(s_SCfree, i - 1)
                b = 4 + 2 * (i % 2)
                for h in range(HH):
                    if i == 0:
                        last = mm(bank(b)[:, h * P:(h + 1) * P], k[:, h, 0:P], q[:, h, P:2 * P], start=True, stop=True)
                    else:
                        for a in range(TT):
                            last = mm(bank(b + a)[:, h * P:(h + 1) * P], k[:, h, a * P:(a + 1) * P],
                                      q[:, h, a * P:(a + 1) * P], start=True, stop=True)
                last.then_inc(s_SC, 1)

            cols_by_tokens(0, 0)
            cols_by_tokens(1, 1)
            cols_by_tokens(2, 2)
            cols_by_tokens(3, 3)
            tokens_by_cols(4, 4)
            tokens_by_cols(5, 5)
            tokens_by_cols(6, 6)
            pe.wait_ge(s_taps, TAPS * CB)
            pe.wait_ge(s_hT_odd, KD // 2)
            pe.wait_ge(s_hT_even, KD // 2)
            for c in range(CB):
                last = mm(bank(4)[:, 0:S2], ones[:], c_acc[:, c, :], start=c == 0, stop=c == CB - 1)
            last.then_inc(s_mean_ps, 1)
            tokens_by_cols(7, 7)
            tokens_by_cols(8, 8)
            pe.wait_ge(s_cdev, 1)
            level(0)
            for i in range(1, 9):
                level(i)
            pe.wait_ge(s_csq, 1)
            pe.wait_ge(s_SCfree, 8)
            for c in range(CB):
                last = mm(bank(7)[:, 0:S2], ones[:], c_sig[:, c, :], start=c == 0, stop=c == CB - 1)
            last.then_inc(s_var_ps, 1)
            pe.wait_ge(s_SCfree, 9)
            for h in range(HH):
                w = slice(h * P, (h + 1) * P)
                mm(bank(4)[:, w], ST[:, 0, h, :], hv[:, 0, w], start=True, stop=True)
                mm(bank(5)[:, w], ST[:, 2, h, :], hv[:, 0, w], start=True, stop=False)
                last = mm(bank(5)[:, w], ST[:, 1, h, :], hv[:, 1, w], start=False, stop=True)
            last.then_inc(s_ho_ps, 1)
            cols_by_tokens(9, 9)

            def turn4(src, b, done):
                for c in range(CB):
                    for a in range(TT):
                        last = tr(bank(b, 2)[:, c * S2 + a * P:c * S2 + (a + 1) * P], src[:, a, c * P:(c + 1) * P], ident[:])
                last.then_inc(done, 1)

            pe.wait_ge(s_hon, 1)
            pe.wait_ge(s_cn, 1)
            turn4(h_o, 6, s_hoT_ps)
            cols_by_tokens(10, 10)
            pe.wait_ge(s_an, 2)
            turn4(aq, 4, s_qkT_ps)
            pe.wait_ge(s_hoT, 1)
            turn4(ak, 6, s_qkT_ps)
            pe.wait_ge(s_convT, CB)
            branch(11, 11, c_acc)
            pe.wait_ge(s_qkT, 2)

            def scores(g):
                if g:
                    pe.wait_ge(s_ao, TT)
                for j in range(4):
                    h = 4 * g + j
                    r = slice(HD * (h % 2), HD * (h % 2) + HD)
                    mm(bank(4 + j)[:, 0:P], qT[r, h // 2, 0:P], kT[r, h // 2, 0:P], start=True, stop=True)
                    last = mm(bank(4 + j)[:, P:3 * P], qT[r, h // 2, P:2 * P], kT[r, h // 2, :], start=True, stop=True)
                last.then_inc(s_asc_ps, 1)

            def turn_p(g):
                pe.wait_ge(s_aexp, 8 * (g + 1))
                for j in range(4):
                    for b in range(3):
                        last = tr(bank(4 + j)[:, b * P:(b + 1) * P], Pm[:, j, b * P:(b + 1) * P], ident[:])
                last.then_inc(s_PT_ps, 1)

            def values(g):
                pe.wait_ge(s_PT, g + 1)
                for j in range(4):
                    h = 4 * g + j
                    w, o = slice(h * HD, (h + 1) * HD), slice(j * HD, (j + 1) * HD)
                    mm(bank(4)[:, o], PT[:, j, 0:P], av[:, 0, w], start=True, stop=True)
                    mm(bank(5)[:, o], PT[:, j, P:2 * P], av[:, 0, w], start=True, stop=False)
                    last = mm(bank(5)[:, o], PT[:, j, 2 * P:3 * P], av[:, 1, w], start=False, stop=True)
                last.then_inc(s_ao_ps, 1)

            scores(0)
            cols_by_tokens_no7 = cols_by_tokens
            cols_by_tokens_no7(13, 12)
            turn_p(0)
            values(0)
            scores(1)
            cols_by_tokens(14, 13)
            turn_p(1)
            values(1)
            branch(15, 14, h_oT)
            pe.wait_ge(s_ao, 2 * TT)
            turn4(a_o, 6, s_aoT_ps)
            cols_by_tokens(17, 15)
            cols_by_tokens(18, 16)
            pe.wait_ge(s_aoT, 1)
            branch(19, 17, a_oT)
            pe.wait_ge(s_gate_used, 4)
            for a in range(TT):
                o = begin(21 + a)
                for half in range(2):
                    wait_landed(pe, L_OUT + half)
                    for k in range(KD):
                        last = mm(o[:, half * W:(half + 1) * W], merged[:, k, a * P:(a + 1) * P],
                                  wcols(L_OUT + half)[:, k, :], start=k == 0, stop=k == KD - 1)
                last.then_inc(s_full, 1)
            turn(h2, s_h2, s_h2T_ps)
            pe.wait_ge(s_h2T_odd, KD // 2)
            pe.wait_ge(s_h2T_even, KD // 2)
            pe.wait_ge(s_router_w, 64)
            pe.wait_ge(s_x2, 2)
            for a in range(TT):
                o = bank(0)[:, a * 64:a * 64 + NL]
                for k in range(KD):
                    mm(o, hT[:, k, a * P:(a + 1) * P], w_router[:, k, :], start=k == 0, stop=False)
                last = mm(o, ones[0:1, :], b_router[0:1, :], start=False, stop=True)
            last.then_inc(s_log_ps, 1)
            pe.wait_ge(s_Yfree, 1)
            with nc.Fori(0, E // 2, 1, engines=[pe.engine]) as q:
                e = q * 2
                for j in range(2):
                    l = NMIX + EXP * j
                    for part in range(EXP):
                        pe.wait_ge(landed[(l + part) % NSLOT], q * 16 + 16 * ((l + part) // NSLOT + 1))
                    for a in range(TT):
                        n = j * TT + a
                        for part in range(2):
                            for k in range(KD):
                                last = mm(bank(part), hT[:, k, a * P:(a + 1) * P], wcols(l + part)[:, k, :],
                                          start=k == 0, stop=k == KD - 1)
                        last.then_inc(s_H_ps, 1)
                        pe.wait_ge(s_act2, e * TT + (n + 1))
                        for f in range(FT):
                            last = tr(bank(2)[:, f * P:(f + 1) * P], e_act[:, f * P:(f + 1) * P], ident[:])
                        last.then_inc(s_T_ps, 1)
                        pe.wait_ge(s_T, e * TT + (n + 1))
                        pe.wait_ge(s_Yfree, e * TT + (n + 1))
                        for half in range(2):
                            for f in range(FT):
                                last = mm(bank(4 + half), e_actT[:, f, :], wrows(l + 2)[:, f, half * 512:(half + 1) * 512],
                                          start=f == 0, stop=f == FT - 1)
                        last.then_inc(s_Y_ps, 1)


_INS = ['x', 'mix_norm_g', 'w_in', 'b_gate', 'q_norm_g', 'k_norm_g', 'lb_logits', 'hgrn_norm_g', 'conv_w', 'conv_b',
        'conv_ln_g', 'conv_ln_b', 'w_att_o', 'w_hgrn_o', 'w_conv_o', 'w_out', 'ffn_norm_g', 'w_coarse', 'b_coarse',
        'w_fine', 'b_fine', 'w_exp_in', 'w_exp_out']


def kernel(**inputs):
    import numpy as _np
    import concourse.bacc as _bacc
    from concourse import mybir as _mybir
    from concourse.bass_utils import run_bass_kernel_spmd as _run

    nc = _bacc.Bacc("TRN2", target_bir_lowering=False, num_devices=1)
    arrays, args = {}, []
    for name in _INS:
        a = _np.ascontiguousarray(inputs[name])
        arrays[f"in_{name}_dram"] = a
        args.append(nc.dram_tensor(f"in_{name}_dram", a.shape, _mybir.dt.from_np(a.dtype), kind="ExternalInput").ap())
    x = inputs['x']
    args.append(nc.dram_tensor("out_0_dram", x.shape, _mybir.dt.float32, kind="ExternalOutput").ap())
    hybrid_decoder_layer(nc, *args)
    r = _run(nc, [arrays], core_ids=[0])
    return r.results[0]["out_0_dram"]
```

```python
from contextlib import ExitStack

import concourse.bass as bass
from concourse import mybir

ALU = mybir.AluOpType
ACT = mybir.ActivationFunctionType
F32 = mybir.dt.float32
I32 = mybir.dt.int32
AX_X = mybir.AxisListType.X

P = 128
NEG = -1e30
RMS_EPS = 1e-6
LN_EPS = 1e-5
LEAST_FORGET = 2.0 ** -63


class Chain:

    def __init__(self, eng, sem):
        self.eng, self.sem, self.n = eng, sem, 0

    def step(self, ins):
        ins.then_inc(self.sem, 1)
        self.n += 1
        return self.n

    def settle(self, upto=None):
        self.eng.wait_ge(self.sem, self.n if upto is None else upto)


def hybrid_decoder_layer(nc, x, mix_norm_g, w_in, b_gate, q_norm_g, k_norm_g, lb_logits, hgrn_norm_g,
                         conv_w, conv_b, conv_ln_g, conv_ln_b, w_att_o, w_hgrn_o, w_conv_o, w_out,
                         ffn_norm_g, w_coarse, b_coarse, w_fine, b_fine, w_exp_in, w_exp_out, out):
    _, SEQ, D = x.shape
    TT = SEQ // P
    KD = D // P
    HD = q_norm_g.shape[1]
    W = w_att_o.shape[1]
    CB = W // P
    AH = W // HD
    HH = W // hgrn_norm_g.shape[1]
    TAPS = conv_w.shape[1]
    G = w_coarse.shape[2]
    E = w_fine.shape[2]
    EG = E // G
    FF = w_exp_out.shape[2]
    FT = FF // P
    CHUNK = 64
    assert (SEQ, D, W, HD, HH, FF, EG) == (256, 1024, 512, 64, 4, 512, 8)
    SCALE = float(HD) ** -0.5
    S2 = TT * P
    CAP = 64
    EXP = 3

    with ExitStack() as ctx:
        def sb(name, shape, dt=F32):
            return ctx.enter_context(nc.sbuf_tensor(name, shape, dt))

        def sem(name):
            return ctx.enter_context(nc.semaphore(name))

        NSLOT = 6
        UNIT = 4096
        ring = sb("ring", [P, NSLOT, UNIT])
        xs = sb("xs", [P, TT, D])
        hT = sb("hT", [P, KD, S2])
        ident = sb("ident", [P, P])
        ones = sb("ones", [P, P])
        vecT = sb("vecT", [P, 64])
        tapT = sb("tapT", [P, TAPS * CB])
        causal = sb("causal", [P, 3, P])
        level_mask = sb("level_mask", [P, 8, P], I32)
        chunk_keep = sb("chunk_keep", [P, S2])
        w_router = sb("w_router", [P, KD, G + E])
        b_router = sb("b_router", [1, G + E])
        before = sb("before", [P, P])
        place_no = sb("place_no", [P, CAP])
        few = sb("few", [1, 1], I32)
        st = sb("st", [P, 256])
        K = 1024
        arena = sb("arena", [P, 21248])

        def at(k, n):
            o = int(k * K)
            return arena[:, o:o + n]

        def chan(k):
            return at(k, CB * S2).rearrange("p (c t) -> p c t", c=CB)

        def tok(k):
            return at(k, TT * W).rearrange("p (a w) -> p a w", a=TT)

        ps = ctx.enter_context(nc.psum_tensor("ps", [P, 8, 512], F32))

        def bank(b, n=1):
            return ps[:, b:b + n, :].rearrange("p b f -> p (b f)")

        h_tok = at(0, TT * D).rearrange("p (a d) -> p a d", a=TT)
        vec_rows = at(10.5, P)
        tap_rows = at(11, P)
        idx_s = at(2, P).bitcast(I32)
        idx_t = at(2.25, P).bitcast(I32)
        idx_x = at(2.5, P).bitcast(I32)
        hq, hk, hb = chan(0), chan(1), chan(2)
        hf = chan(3)
        Ex, Qx, Kx = [chan(3), chan(4)], [chan(5), chan(6)], [chan(7), chan(8)]
        ST = at(9, 3 * W).rearrange("p (a h t) -> p a h t", a=3, h=HH)
        hv, hg = tok(10.5), tok(11.5)
        h_sq, h_o = tok(5), tok(6)
        h_oT = chan(11.5)
        aq, ak, av = tok(12.5), tok(13.5), tok(14.5)
        a_sq = tok(4)
        qT, kT = chan(7), chan(8)
        Pm = at(0, 4 * 384).rearrange("p (h s) -> p h s", h=4)
        PT = at(2, 4 * 384).rearrange("p (h s) -> p h s", h=4)
        a_o = tok(13.5)
        a_oT = chan(12.5)
        PAD = TAPS - 1
        c_sig = chan(15.5)
        c_u = at(16.5, CB * (PAD + S2)).rearrange("p (c t) -> p c t", c=CB)
        c_acc = at(17.75, CB * S2).rearrange("p (c t) -> p c t", c=CB)
        gate = [chan(15.5), chan(16.5)]
        prod = c_acc
        merged = at(18.75, KD * S2).rearrange("p (k t) -> p k t", k=KD)

        MIXG, FFNG, BG, CVB, LNG, LNB, LB, HNG, QG, KG = 0, 8, 16, 40, 44, 48, 52, 56, 57, 58
        NVEC = 59

        s_x = sem("x_landed")
        s_small = sem("small_landed")
        s_router_w = sem("router_weights_landed")
        landed = [sem(f"slot{i}_landed") for i in range(NSLOT)]
        landed_top = [sem(f"arena_slot{i}_landed") for i in range(3)]
        s_const = sem("constants_ready")
        s_pool = sem("pool_chain")
        s_dve = sem("dve_chain")
        s_act = sem("act_chain")
        s_masks = sem("level_masks_ready")
        s_ssq = sem("square_sums_ready")
        s_root = sem("roots_ready")
        s_h = sem("h_ready")
        s_hT_ps = sem("hT_in_psum")
        s_hT_odd = sem("hT_odd_tiles_ready")
        s_hT_even = sem("hT_even_tiles_ready")
        s_vec_ps = sem("vectors_in_psum")
        s_vec = sem("vectors_ready")
        s_full = sem("unit_in_psum")
        s_free = [sem("pair0_free"), sem("pair1_free")]
        s_csig = sem("conv_sigmoid_ready")
        s_taps = sem("conv_tap_done")
        s_u = sem("conv_gated_ready")
        s_f = sem("forget_ready")
        s_hf = sem("forget_sigmoid_ready")
        s_lf = sem("log_forget_ready")
        s_hq = sem("hgrn_q_ready")
        s_hi = sem("hgrn_values_ready")
        s_hg = sem("hgrn_outgate_ready")
        s_D = sem("exponents_ready")
        s_E = sem("decays_ready")
        s_K = sem("level_keys_ready")
        s_Q = sem("level_queries_ready")
        s_SC = sem("level_scores_in_psum")
        s_SCfree = sem("level_scores_taken")
        s_lb0 = sem("lb_shifted")
        s_lb1 = sem("lb_exp_ready")
        s_aq = sem("attention_inputs_ready")
        s_asq = sem("attention_squares_ready")
        s_conv_done = sem("conv_taps_complete")
        s_mean_ps = sem("conv_mean_in_psum")
        s_cdev = sem("conv_deviation_ready")
        s_csq = sem("conv_squares_ready")
        s_var_ps = sem("conv_var_in_psum")
        s_cvar = sem("conv_var_ready")
        s_croot = sem("conv_root_ready")
        s_cn = sem("conv_normalised")
        s_convT = sem("conv_out_ready")
        s_ho_ps = sem("hgrn_o_in_psum")
        s_hosq = sem("hgrn_o_squares_ready")
        s_hms = sem("hgrn_ms_ready")
        s_hroot = sem("hgrn_root_ready")
        s_hon = sem("hgrn_o_normalised")
        s_hoT_ps = sem("hgrn_oT_in_psum")
        s_hoT = sem("hgrn_oT_ready")
        s_ams = sem("attention_ms_ready")
        s_aroot = sem("attention_roots_ready")
        s_an = sem("attention_qk_normalised")
        s_qkT_ps = sem("qkT_in_psum")
        s_qkT = sem("qkT_ready")
        s_asc_ps = sem("attention_scores_in_psum")
        s_amax = sem("attention_max_ready")
        s_aexp = sem("attention_exp_ready")
        s_PT_ps = sem("PT_in_psum")
        s_PT = sem("PT_ready")
        s_ao_ps = sem("attention_o_in_psum")
        s_ao = sem("attention_o_ready")
        s_aoT_ps = sem("attention_oT_in_psum")
        s_aoT = sem("attention_oT_ready")
        s_gate = sem("gate_half_ready")
        s_gate_used = sem("gate_half_used")
        s_merged = sem("merged_ready")
        s_x2 = sem("x2_ready")
        s_ssq2 = sem("square_sums2_ready")
        s_ms2 = sem("mean_squares2_ready")
        s_root2 = sem("root2_ready")
        s_h2 = sem("h2_ready")
        s_h2T_ps = sem("h2T_in_psum")
        s_h2T_odd = sem("h2T_odd_tiles_ready")
        s_h2T_even = sem("h2T_even_tiles_ready")
        s_ms = sem("mean_squares_ready")
        s_log_ps = sem("router_logits_in_psum")
        s_rsub = sem("router_exponents_ready")
        s_rexp = sem("router_exp_ready")
        s_sel = sem("selection_ready")
        s_rank_ps = sem("ranks_in_psum")
        s_count_ps = sem("counts_in_psum")
        s_few = sem("most_tokens_ready")
        s_combine = sem("ranks_and_weights_ready")
        s_in_used = sem("expert_hidden_complete")
        s_out_used = sem("expert_out_complete")
        s_H0_ps = sem("first_tile_hidden_in_psum")
        s_Y0_ps = sem("first_tile_out_in_psum")
        s_Yfree = sem("expert_out_taken")
        s_sil = sem("expert_silu_ready")
        s_act2 = sem("expert_act_ready")
        s_T_ps = sem("expert_actT_in_psum")
        s_T = sem("expert_actT_ready")
        s_placed = sem("unweighted_places_ready")
        s_G = sem("places_ready")
        s_gather = sem("gathered_in_psum")
        s_xg = sem("gathered_ready")
        s_GwT_ps = sem("weighted_placesT_in_psum")
        s_GwT = sem("weighted_placesT_ready")
        s_Yv = sem("expert_out_left_taken")
        s_Ya = sem("expert_out_right_taken")
        s_scat = sem("experts_added")
        s_final = [sem(f"result_tile{a}_ready") for a in range(TT)]
        s_out = sem("out_stored")

        wi = w_in[0].rearrange("(k p) n -> p k n", p=P)
        IN = {n: i for i, n in enumerate(["aq", "ak", "av", "hq", "hf", "hi", "hg", "ca", "cb"])}

        def in_cols(c):
            return wi[:, :, c * W:(c + 1) * W]

        def o_rows(w):
            return w[0].rearrange("(k p) n -> p k n", p=P)

        wo = w_out[0].rearrange("(k p) n -> p k n", p=P)
        order = ["cb", "ca", "hf", "hq", "hi", "hg", "aq", "ak", "av"]
        sources = [in_cols(IN[n]) for n in order]
        for b, w in ((2, w_conv_o), (1, w_hgrn_o), (0, w_att_o)):
            sources += [in_cols(9 + 2 * b), in_cols(10 + 2 * b), o_rows(w)]
        sources += [wo[:, :, 0:W], wo[:, :, W:D]]
        NMIX = len(sources)
        L_OUT = 18
        LAST_UNIT = [*range(9), 9, 10, 12, 13, 14, 16, 17, 18, 20, 22, 22]

        def slot(l):
            return ring[:, l % NSLOT, :]

        def wcols(l):
            return slot(l).rearrange("p (k n) -> p k n", k=KD)

        def wrows(l):
            return slot(l).rearrange("p (k n) -> p k n", k=CB)

        def wait_landed(eng, l):
            eng.wait_ge(landed[l % NSLOT], 16 * (l // NSLOT + 1))

        GROUPS = 3

        def expert_rows(g, part):
            if g == 0:
                return at(4 * part, UNIT).rearrange("p (k n) -> p k n", k=CB)
            return wrows(NMIX + EXP * (g - 1) + part)

        def expert_sem(g, part):
            if g == 0:
                return landed_top[part], 0
            l = NMIX + EXP * (g - 1) + part
            return landed[l % NSLOT], 16 * (l // NSLOT)

        def expert_cols(g, k, f):
            return expert_rows(g, k // CB)[:, k % CB, :].rearrange("p (g f n) -> p g f n", g=2, f=2)[:, :, f, :]

        h2 = at(12.5, TT * D).rearrange("p (a d) -> p a d", a=TT)
        FH = FF // 2
        xg = at(14.5, KD * 2 * CAP).rearrange("p (k c) -> p k c", k=KD)
        place = at(15.5, TT * 2 * CAP).rearrange("p (a c) -> p a c", a=TT)
        wplace = at(15.75, TT * 2 * CAP).rearrange("p (a c) -> p a c", a=TT)
        wplaceT = at(16, S2)
        e_sil = at(16.25, FF).rearrange("p (h n) -> p h n", h=2)
        e_act = at(16.75, FF).rearrange("p (h n) -> p h n", h=2)
        e_actT = at(17.25, FF).rearrange("p (f t) -> p f t", f=FT)
        NP_ = E + 2
        rank = at(17.75, TT * NP_).rearrange("p (a e) -> p a e", a=TT)
        weight = at(17.85, TT * NP_).rearrange("p (a e) -> p a e", a=TT)
        rank_q = rank.rearrange("p a (q j) -> p a q j", j=2)
        weight_q = weight.rearrange("p a (q j) -> p a q j", j=2)
        sel = at(17.95, TT * E).rearrange("p (a e) -> p a e", a=TT)
        most = at(18.05, 1)
        y_sb = at(18.75, D)
        NL = G + E
        logits = at(18.1, TT * NL).rearrange("p (a e) -> p a e", a=TT)

        def rt(i):
            return at(18.2 + i / 16, TT * E).rearrange("p (a e) -> p a e", a=TT)
        r_fine, r_pen, r_oh1, r_oh2, r_tmp, r_iota = (rt(i) for i in range(6))
        r_s = [at(19.75 + i / 64, TT).rearrange("p (a e) -> p a e", a=TT) for i in range(12)]
        r_grp, r_e4, r_i4, r_t4 = (at(20 + i / 32, TT * G).rearrange("p (a e) -> p a e", a=TT) for i in range(4))

        block = ctx.enter_context(nc.Block())

        @block.sync
        def _(sp):
            for a in range(TT):
                sp.dma_start(xs[:, a, :], x[0, a * P:(a + 1) * P, :]).then_inc(s_x, 16)
            sp.wait_ge(s_x, 16 * TT)
            for l, src in enumerate(sources):
                if l >= NSLOT:
                    sp.wait_ge(s_full, LAST_UNIT[l - NSLOT] + 1)
                k = KD if src.shape[1] == KD else CB
                sp.dma_start(slot(l).rearrange("p (k n) -> p k n", k=k), src).then_inc(landed[l % NSLOT], 16)
            def load_part(e, g, part):
                if part < 2:
                    src = w_exp_in[0][bass.ds(e, 1), part * D // 2:(part + 1) * D // 2, :]
                else:
                    src = w_exp_out[0][bass.ds(e, 1), :, :]
                sp.dma_start(expert_rows(g, part), src.rearrange("a (k p) n -> p (a k) n", p=P))\
                    .then_inc(expert_sem(g, part)[0], 16)

            sp.wait_ge(s_full, 17)
            for part in range(EXP):
                load_part(0, 0, part)
            for g in (1, 2):
                for part in range(EXP):
                    sp.wait_ge(s_full, LAST_UNIT[NMIX - NSLOT + EXP * (g - 1) + part] + 1)
                    load_part(g, g, part)

            def reload(e, g):
                for part in range(EXP):
                    sp.wait_ge(s_in_used if part < 2 else s_out_used, e - 2)
                    load_part(e, g, part)

            with nc.Fori(1, E // GROUPS, 1, engines=[sp.engine]) as r:
                for g in range(GROUPS):
                    reload(r * GROUPS + g, g)
            for e in range(E - E % GROUPS, E):
                reload(e, e % GROUPS)
            for a in range(TT):
                sp.wait_ge(s_final[a], 1)
                sp.dma_start(out[0, a * P:(a + 1) * P, :], xs[:, a, :]).then_inc(s_out, 16)
            sp.wait_ge(s_out, 16 * TT)

        @block.gpsimd
        def _(pool):
            ch = Chain(pool, s_pool)
            ch.step(nc.gpsimd.memset(ident[:], 0.0))
            ch.step(nc.gpsimd.memset(causal[:], 0.0))
            ch.step(nc.gpsimd.iota(idx_s, [[0, P]], base=0, channel_multiplier=1))
            ch.step(nc.gpsimd.iota(idx_t, [[1, P]], base=0, channel_multiplier=0))
            ch.step(nc.gpsimd.memset(ones[:], 1.0))
            ch.step(nc.gpsimd.memset(before[:], 1.0))
            ch.step(nc.gpsimd.iota(place_no[:], [[1, CAP]], base=0, channel_multiplier=0,
                                   allow_small_or_imprecise_dtypes=True))
            ch.step(nc.gpsimd.memset(chunk_keep[:], 1.0))
            ch.step(nc.gpsimd.memset(c_u[:, :, 0:PAD], 0.0))
            ch.settle()
            nc.gpsimd.affine_select(out=ident[:], in_=ident[:], compare_op=ALU.not_equal, fill=1.0, base=0,
                                    pattern=[[-1, P]], channel_multiplier=1).then_inc(s_const, 1)
            for c in (0, 2):
                nc.gpsimd.affine_select(out=causal[:, c, :], in_=causal[:, c, :], compare_op=ALU.is_ge, fill=NEG,
                                        base=0, pattern=[[-1, P]], channel_multiplier=1).then_inc(s_const, 1)
            nc.gpsimd.memset(chunk_keep[:].rearrange("p (c i) -> p c i", i=CHUNK)[:, :, 0:1], 0.0)\
                .then_inc(s_const, 1)
            nc.gpsimd.affine_select(out=before[:], in_=before[:], compare_op=ALU.is_gt, fill=0.0, base=0,
                                    pattern=[[1, P]], channel_multiplier=-1).then_inc(s_const, 1)
            pool.wait_ge(s_masks, 1)
            nc.gpsimd.affine_select(out=idx_x, in_=idx_x, compare_op=ALU.is_ge, fill=4096.0, base=0,
                                    pattern=[[1, P]], channel_multiplier=-1).then_inc(s_const, 1)
            for i in range(8):
                m = 128 >> i
                pool.wait_ge(s_E, i + 1)
                if i >= 2:
                    pool.wait_ge(s_SC, i - 1)
                kv = hk.rearrange("p c t -> p (c t)").rearrange("p (b a m) -> p b a m", a=2, m=m)
                ev = Ex[i % 2].rearrange("p c t -> p (c t)").rearrange("p (b a m) -> p b a m", a=2, m=m)
                ov = Kx[i % 2].rearrange("p c t -> p (c t)").rearrange("p (b a m) -> p b a m", a=2, m=m)
                if i < 2:
                    nc.gpsimd.memset(ov[:, :, 1, :], 0.0).then_inc(s_K, 1)
                nc.gpsimd.tensor_tensor(ov[:, :, 0, :], kv[:, :, 0, :], ev[:, :, 0, :], ALU.mult).then_inc(s_K, 1)

        @block.scalar
        def _(act):
            ch = Chain(act, s_act)
            rows = [(MIXG, mix_norm_g, 8), (FFNG, ffn_norm_g, 8), (BG, b_gate, 24), (CVB, conv_b, 4),
                    (LNG, conv_ln_g, 4), (LNB, conv_ln_b, 4), (LB, lb_logits, 4), (HNG, hgrn_norm_g, 1)]
            for r, v, n in rows:
                act.dma_start(vec_rows[r:r + n, :], v[0].rearrange("(r p) -> r p", p=P)).then_inc(s_small, 16)
            for r, v in ((QG, q_norm_g), (KG, k_norm_g)):
                for i in range(P // HD):
                    act.dma_start(vec_rows[r:r + 1, i * HD:(i + 1) * HD], v[0:1, :]).then_inc(s_small, 16)
            act.dma_start(tap_rows[0:TAPS * CB, :], conv_w[0].rearrange("j (c p) -> (j c) p", p=P)).then_inc(s_small, 16)
            act.wait_ge(s_x, 16 * TT)
            for a in range(TT):
                nc.scalar.activation(at(4 + a, D), xs[:, a, :], ACT.Square, accum_out=st[:, a:a + 1]).then_inc(s_ssq, 1)
            act.wait_ge(s_ms, 1)
            nc.scalar.activation(st[:, 6:8], st[:, 4:6], ACT.Sqrt).then_inc(s_root, 1)
            act.wait_ge(s_vec, 1)
            for k in range(1, KD, 2):
                act.wait_ge(s_hT_ps, k // 2 + 1)
                nc.scalar.activation(hT[:, k, :], bank(4 + k // 2)[:, S2:2 * S2], ACT.Copy,
                                     scale=vecT[:, MIXG + k:MIXG + k + 1]).then_inc(s_hT_odd, 1)
            act.wait_ge(s_lb0, 1)
            nc.scalar.activation(st[:, 20:24], st[:, 16:20], ACT.Exp).then_inc(s_lb1, 1)

            def unit(u):
                return bank(2 * (u % 2), 2)

            act.wait_ge(s_full, 1)
            nc.scalar.activation(c_sig, unit(0).rearrange("p (c t) -> p c t", c=CB), ACT.Sigmoid).then_inc(s_free[0], 1)
            act.wait_ge(s_full, 3)
            nc.scalar.activation(hf, unit(2).rearrange("p (c t) -> p c t", c=CB), ACT.Sigmoid).then_inc(s_free[0], 1)
            act.wait_ge(s_full, 4)
            nc.scalar.activation(hq, unit(3).rearrange("p (c t) -> p c t", c=CB), ACT.Silu).then_inc(s_free[1], 1)
            act.wait_ge(s_full, 5)
            nc.scalar.activation(hv, unit(4).rearrange("p (a w) -> p a w", a=TT), ACT.Copy).then_inc(s_free[0], 1)
            act.wait_ge(s_full, 6)
            nc.scalar.activation(hg, unit(5).rearrange("p (a w) -> p a w", a=TT), ACT.Silu).then_inc(s_free[1], 1)
            for j, buf in enumerate((aq, ak, av)):
                act.wait_ge(s_full, 7 + j)
                nc.scalar.activation(buf, unit(6 + j).rearrange("p (a w) -> p a w", a=TT), ACT.Copy)\
                    .then_inc(s_free[j % 2], 1)
            act.dma_start(b_router[0:1, 0:G], b_coarse[0:1, :]).then_inc(s_router_w, 16)
            act.dma_start(b_router[0:1, G:G + E], b_fine[0:1, :]).then_inc(s_router_w, 16)
            act.dma_start(w_router[:, :, 0:G], w_coarse[0].rearrange("(k p) n -> p k n", p=P)).then_inc(s_router_w, 16)
            act.dma_start(w_router[:, :, G:G + E], w_fine[0].rearrange("(k p) n -> p k n", p=P)).then_inc(s_router_w, 16)
            act.wait_ge(s_f, 1)
            nc.scalar.activation(hf, hf, ACT.Ln).then_inc(s_lf, 1)
            for i in range(8):
                act.wait_ge(s_D, i + 1)
                nc.scalar.activation(Ex[i % 2], Ex[i % 2], ACT.Exp).then_inc(s_E, 1)

            act.wait_ge(s_cdev, 1)
            nc.scalar.activation(c_sig, c_acc, ACT.Square).then_inc(s_csq, 1)
            act.wait_ge(s_cvar, 1)
            nc.scalar.activation(c_u[:, 0, 0:S2], c_u[:, 0, 0:S2], ACT.Sqrt).then_inc(s_croot, 1)
            act.wait_ge(s_ho_ps, 1)
            nc.scalar.activation(h_sq, bank(4, 2).rearrange("p (a w) -> p a w", a=TT), ACT.Square).then_inc(s_hosq, 1)
            act.wait_ge(s_hms, 1)
            nc.scalar.activation(st[:, 48:56], st[:, 40:48], ACT.Sqrt).then_inc(s_hroot, 1)
            for j, buf in enumerate((aq, ak)):
                if j == 0:
                    act.wait_ge(s_SC, 8)
                act.wait_ge(s_free[j % 2], 4 if j == 0 else 4)
                if j:
                    act.wait_ge(s_ams, 1)
                nc.scalar.activation(a_sq, buf, ACT.Square).then_inc(s_asq, 1)
            act.wait_ge(s_ams, 2)
            nc.scalar.activation(st[:, 96:128], st[:, 64:96], ACT.Sqrt).then_inc(s_aroot, 1)
            act.wait_ge(s_cn, 1)
            for c in range(CB):
                nc.scalar.activation(c_acc[:, c, :], c_acc[:, c, :], ACT.Silu, bias=vecT[:, LNB + c:LNB + c + 1],
                                     scale=vecT[:, LNG + c:LNG + c + 1]).then_inc(s_convT, 1)
            def gates(b, n):
                for half in range(2):
                    u = [9, 13, 17][n] + half
                    act.wait_ge(s_full, u + 1)
                    if n == 0:
                        act.wait_ge(s_convT, 4)
                    else:
                        act.wait_ge(s_free[(u - 2) % 2], (u - 2) // 2 + 1)
                    for c in range(CB):
                        last = nc.scalar.activation(gate[half][:, c, :], unit(u)[:, c * S2:(c + 1) * S2], ACT.Sigmoid,
                                                    bias=vecT[:, BG + 8 * b + 4 * half + c:BG + 8 * b + 4 * half + c + 1])
                        if c < CB - 1:
                            last.then_inc(s_act, 1)
                    last.then_inc(s_free[u % 2], 1)

            def hgrn_oT():
                act.wait_ge(s_hoT_ps, 1)
                nc.scalar.activation(h_oT, bank(6, 2).rearrange("p (c t) -> p c t", c=CB), ACT.Copy,
                                     scale=vecT[:, HNG:HNG + 1]).then_inc(s_hoT, 1)

            def softmax_half(g):
                act.wait_ge(s_amax, g + 1)
                for h in range(4):
                    for a in range(TT):
                        w = slice(0, P) if a == 0 else slice(P, 3 * P)
                        nc.scalar.activation(Pm[:, h, w], Pm[:, h, w], ACT.Exp, scale=SCALE,
                                             bias=st[:, 144 + 2 * h + a:145 + 2 * h + a],
                                             accum_out=st[:, 160 + 8 * g + 2 * h + a:161 + 8 * g + 2 * h + a])\
                            .then_inc(s_aexp, 1)
                act.wait_ge(s_PT_ps, g + 1)
                if g:
                    act.wait_ge(s_ao_ps, g)
                nc.scalar.activation(PT, ps[:, 4:8, 0:384], ACT.Copy).then_inc(s_PT, 1)

            hgrn_oT()
            gates(2, 0)
            softmax_half(0)
            softmax_half(1)
            gates(1, 1)
            act.wait_ge(s_aoT_ps, 1)
            nc.scalar.activation(a_oT, bank(6, 2).rearrange("p (c t) -> p c t", c=CB), ACT.Copy).then_inc(s_aoT, 1)
            gates(0, 2)

            act.wait_ge(s_x2, 2)
            for a in range(TT):
                nc.scalar.activation(at(14.5 + a, D), xs[:, a, :], ACT.Square, accum_out=st[:, 200 + a:201 + a]).then_inc(s_ssq2, 1)
            act.wait_ge(s_ms2, 1)
            nc.scalar.activation(st[:, 206:208], st[:, 204:206], ACT.Sqrt).then_inc(s_root2, 1)
            for k in range(1, KD, 2):
                act.wait_ge(s_h2T_ps, k // 2 + 1)
                nc.scalar.activation(hT[:, k, :], bank(4 + k // 2)[:, S2:2 * S2], ACT.Copy,
                                     scale=vecT[:, FFNG + k:FFNG + k + 1]).then_inc(s_h2T_odd, 1)
            act.wait_ge(s_rsub, 1)
            nc.scalar.activation(r_e4, r_e4, ACT.Exp).then_inc(s_rexp, 1)
            act.wait_ge(s_rsub, 2)
            nc.scalar.activation(r_s[5], r_s[5], ACT.Exp).then_inc(s_rexp, 1)
            act.wait_ge(s_few, 1)
            n_most = act.value_load(few[0:1, 0:1], min_val=0, max_val=SEQ)
            with act.If(n_most <= CAP):
                with nc.Fori(0, E // 2, 1, engines=[act.engine]) as q:
                    for j in range(2):
                        act.wait_ge(s_in_used, q * 2 + (j + 1))
                        nc.scalar.activation(e_sil[:, j, :], bank(6 + j)[:, 0:FH], ACT.Silu).then_inc(s_sil, 1)
                        if j == 0:
                            act.wait_ge(s_GwT_ps, q + 1)
                            nc.scalar.activation(wplaceT, bank(4)[:, 0:S2], ACT.Copy).then_inc(s_GwT, 1)
                        act.wait_ge(s_T_ps, q * 2 + (j + 1))
                        nc.scalar.activation(e_actT[:, 2 * j:2 * j + 2, :],
                                             bank(6 + j)[:, 0:FH].rearrange("p (f t) -> p f t", f=2), ACT.Copy)\
                            .then_inc(s_T, 1)
                        act.wait_ge(s_out_used, q * 2 + (j + 1))
                        nc.scalar.activation(y_sb[j * CAP:(j + 1) * CAP, 512:1024], bank(6 + j)[CAP:2 * CAP, :], ACT.Copy)\
                            .then_inc(s_Ya, 1)
                act.wait_ge(s_scat, E // 2 + 1)
                nc.scalar.activation(xs[:, 1, :], bank(2, 2), ACT.Copy).then_inc(s_final[1], 1)
            with act.Else():
                with nc.Fori(0, E, 1, engines=[act.engine]) as e:
                    for a in range(TT):
                        if a == 0:
                            act.wait_ge(s_H0_ps, e + 1)
                        else:
                            act.wait_ge(s_in_used, e + 1)
                        nc.scalar.activation(e_sil, ps[:, 0:2, 0:FH], ACT.Silu).then_inc(s_sil, 1)
                        act.wait_ge(s_T_ps, e * TT + (a + 1))
                        nc.scalar.activation(e_actT.rearrange("p f t -> p (f t)"), bank(2), ACT.Copy).then_inc(s_T, 1)

        @block.vector
        def _(dve):
            v = nc.vector
            ch = Chain(dve, s_dve)
            s = ch.step

            def unit(u):
                return bank(2 * (u % 2), 2)

            dve.wait_ge(s_pool, 4)
            v.tensor_tensor(idx_x, idx_s, idx_t, ALU.bitwise_xor).then_inc(s_masks, 1)
            dve.wait_ge(s_ssq, 2)
            v.tensor_scalar(st[:, 4:6], st[:, 0:2], 1.0 / D, RMS_EPS, ALU.mult, ALU.add).then_inc(s_ms, 1)
            dve.wait_ge(s_root, 1)
            s(v.reciprocal(st[:, 8:10], st[:, 6:8]))
            ch.settle()
            for a in range(TT):
                v.tensor_scalar(h_tok[:, a, :], xs[:, a, :], st[:, 8 + a:9 + a], None, ALU.mult).then_inc(s_h, 1)
            dve.wait_ge(s_vec_ps, 1)
            v.tensor_copy(vecT[:, 0:NVEC], bank(0)[:, 0:NVEC])
            v.tensor_copy(tapT[:], bank(0)[:, P:P + TAPS * CB]).then_inc(s_vec, 1)
            for k in range(0, KD, 2):
                dve.wait_ge(s_hT_ps, k // 2 + 1)
                if k == 0:
                    dve.wait_ge(s_vec, 1)
                dve.wait_ge(s_hT_odd, k // 2 + 1)
                v.tensor_scalar(hT[:, k, :], bank(4 + k // 2)[:, 0:S2], vecT[:, MIXG + k:MIXG + k + 1], None,
                                ALU.mult).then_inc(s_hT_even, 1)
            dve.wait_ge(s_const, 6)
            for i in range(8):
                s(v.tensor_scalar(level_mask[:, i, :], idx_x, float(P >> i), None, ALU.is_lt))
            lbt = vecT[:, LB:LB + HH]
            v.tensor_tensor(st[:, 16:20], lbt, lbt, ALU.subtract).then_inc(s_lb0, 1)
            dve.wait_ge(s_lb1, 1)
            s(v.reciprocal(st[:, 24:28], st[:, 20:24]))
            ch.settle()
            s(v.tensor_tensor(st[:, 28:32], st[:, 20:24], st[:, 24:28], ALU.mult))
            ch.settle()
            s(v.tensor_tensor(st[:, 28:32], st[:, 28:32], st[:, 28:32], ALU.subtract))
            ch.settle()
            s(v.tensor_scalar(st[:, 28:32], st[:, 28:32], 0.0, None, ALU.max))
            ch.settle()
            s(v.tensor_scalar(st[:, 32:36], st[:, 28:32], -1.0, 1.0, ALU.mult, ALU.add))
            s(v.tensor_scalar(st[:, 36:40], st[:, 28:32], 1.0, -1.0, ALU.mult, ALU.add))
            ch.settle()
            lb, one_lb, lb_one = 28, 32, 36
            dve.wait_ge(s_free[0], 1)
            dve.wait_ge(s_full, 2)
            v.tensor_tensor(c_u[:, :, PAD:PAD + S2], unit(1).rearrange("p (c t) -> p c t", c=CB), c_sig, ALU.mult)\
                .then_inc(s_free[1], 1)
            dve.wait_ge(s_free[1], 1)
            for c in range(CB):
                v.tensor_scalar(c_acc[:, c, :], c_u[:, c, 0:S2], tapT[:, c:c + 1], vecT[:, CVB + c:CVB + c + 1],
                                ALU.mult, ALU.add).then_inc(s_taps, 1)
            with nc.Fori(1, TAPS, 1, engines=[dve.engine]) as j:
                for c in range(CB):
                    dve.wait_ge(s_taps, j * CB + (c + 1 - CB))
                    v.scalar_tensor_tensor(out=c_acc[:, c, :], in0=c_u[:, c, bass.ds(j, S2)],
                                           scalar=tapT[:, bass.ds(j * CB + c, 1)], in1=c_acc[:, c, :],
                                           op0=ALU.mult, op1=ALU.add).then_inc(s_taps, 1)
            dve.wait_ge(s_free[0], 2)
            for h in range(HH):
                s(v.tensor_scalar(hk[:, h, :], hf[:, h, :], st[:, lb_one + h:lb_one + h + 1],
                                  st[:, one_lb + h:one_lb + h + 1], ALU.mult, ALU.add))
            ch.settle()
            for h in range(HH):
                s(v.tensor_scalar(hf[:, h, :], hf[:, h, :], st[:, one_lb + h:one_lb + h + 1],
                                  st[:, lb + h:lb + h + 1], ALU.mult, ALU.add))
            ch.settle()
            v.tensor_scalar(hf, hf, LEAST_FORGET, None, ALU.max).then_inc(s_f, 1)
            dve.wait_ge(s_mean_ps, 1)
            mean = bank(4)[:, 0:S2]
            v.scalar_tensor_tensor(out=c_acc, in0=mean.unsqueeze(1).broadcast_to([P, CB, S2]), scalar=-1.0 / W,
                                   in1=c_acc, op0=ALU.mult, op1=ALU.add).then_inc(s_cdev, 1)
            dve.wait_ge(s_lf, 1)
            for h in range(HH):
                s(v.tensor_tensor_scan(hb[:, h, :], chunk_keep[:], hf[:, h, :], 0.0, ALU.mult, ALU.add))
            ch.settle()

            def halves(t, m):
                return t.rearrange("p c t -> p (c t)").rearrange("p (b a m) -> p b a m", a=2, m=m)

            def exponents(i):
                m = P >> i
                if i >= 2:
                    dve.wait_ge(s_K, 2 if i == 2 else i + 1)
                    dve.wait_ge(s_Q, i - 1)
                D = Ex[i % 2]
                dv, bv = halves(D, m), halves(hb, m)
                if m <= CHUNK:
                    nb = HH * S2 // (2 * m)
                    ref = bv[:, :, 0, m - 1:m].broadcast_to([P, nb, m])
                    if m < CHUNK:
                        v.tensor_tensor(dv[:, :, 1, :], bv[:, :, 1, :], ref, ALU.subtract)
                    else:
                        v.tensor_copy(dv[:, :, 1, :], bv[:, :, 1, :])
                    v.tensor_tensor(dv[:, :, 0, :], ref, bv[:, :, 0, :], ALU.subtract).then_inc(s_D, 1)
                else:
                    dc = D.rearrange("p h (c t) -> p h c t", t=CHUNK)
                    bc = hb.rearrange("p h (c t) -> p h c t", t=CHUNK)

                    def end(c):
                        return bc[:, :, c, CHUNK - 1:CHUNK].broadcast_to([P, HH, CHUNK])
                    s(v.tensor_tensor(dc[:, :, 0, :], end(0), bc[:, :, 0, :], ALU.subtract))
                    v.tensor_tensor(dc[:, :, 1, :], end(1), bc[:, :, 1, :], ALU.subtract)
                    v.tensor_copy(dc[:, :, 2, :], bc[:, :, 2, :])
                    v.tensor_tensor(dc[:, :, 3, :], bc[:, :, 3, :], end(2), ALU.add)
                    ch.settle()
                    v.tensor_tensor(dc[:, :, 0, :], dc[:, :, 0, :], end(1), ALU.add).then_inc(s_D, 1)

            def queries(i):
                m = P >> i
                dve.wait_ge(s_E, i + 1)
                if i == 0:
                    dve.wait_ge(s_free[1], 2)
                if i >= 2:
                    dve.wait_ge(s_SC, i - 1)
                ov, qv, ev = halves(Qx[i % 2], m), halves(hq, m), halves(Ex[i % 2], m)
                if i < 2:
                    s(v.memset(ov[:, :, 0, :], 0.0))
                    ch.settle()
                v.tensor_tensor(ov[:, :, 1, :], qv[:, :, 1, :], ev[:, :, 1, :], ALU.mult).then_inc(s_Q, 1)

            def take(i):
                b = 4 + 2 * (i % 2)
                dve.wait_ge(s_SC, i + 1)
                if i == 0:
                    v.tensor_copy(ST[:, 2, :, :], bank(b).rearrange("p (h t) -> p h t", h=HH)).then_inc(s_SCfree, 1)
                else:
                    if i == 1:
                        s(v.memset(ST[:, 0:2, :, :], 0.0))
                        ch.settle()
                    else:
                        dve.wait_ge(s_SCfree, i)
                    mask = level_mask[:, i - 1, :].unsqueeze(1).broadcast_to([P, 2 * HH, P])
                    v.copy_predicated(ST[:, 0:2, :, :].rearrange("p a h t -> p (a h) t"), mask,
                                      bank(b, 2).rearrange("p (g t) -> p g t", t=P)).then_inc(s_SCfree, 1)

            exponents(0)
            for i in range(8):
                if i + 1 < 8:
                    exponents(i + 1)
                queries(i)
                if i:
                    take(i - 1)
            take(7)
            take(8)
            dve.wait_ge(s_var_ps, 1)
            root = c_u[:, 0, 0:S2]
            v.tensor_scalar(root, bank(7)[:, 0:S2], 1.0 / W, LN_EPS, ALU.mult, ALU.add).then_inc(s_cvar, 1)
            dve.wait_ge(s_croot, 1)
            s(v.reciprocal(c_u[:, 1, 0:S2], root))
            ch.settle()
            v.tensor_tensor(c_acc, c_acc, c_u[:, 1:2, 0:S2].broadcast_to([P, CB, S2]), ALU.mult).then_inc(s_cn, 1)
            dve.wait_ge(s_hosq, 1)
            s(v.tensor_reduce(st[:, 40:48], h_sq.rearrange("p a (h w) -> p (a h) w", w=P), AX_X, ALU.add))
            ch.settle()
            v.tensor_scalar(st[:, 40:48], st[:, 40:48], 1.0 / P, RMS_EPS, ALU.mult, ALU.add).then_inc(s_hms, 1)
            dve.wait_ge(s_hroot, 1)
            s(v.reciprocal(st[:, 56:64], st[:, 48:56]))
            ch.settle()
            s(v.tensor_tensor(h_o.rearrange("p a (h w) -> p (a h) w", w=P),
                              bank(4, 2).rearrange("p (g w) -> p g w", w=P),
                              st[:, 56:64].unsqueeze(2).broadcast_to([P, TT * HH, P]), ALU.mult))
            ch.settle()
            dve.wait_ge(s_free[1], 3)
            v.tensor_tensor(h_o, h_o, hg, ALU.mult).then_inc(s_hon, 1)
            for j in range(2):
                dve.wait_ge(s_asq, j + 1)
                s(v.tensor_reduce(st[:, 64 + 16 * j:80 + 16 * j], a_sq.rearrange("p a (h w) -> p (a h) w", w=HD),
                                  AX_X, ALU.add))
                ch.settle()
                v.tensor_scalar(st[:, 64 + 16 * j:80 + 16 * j], st[:, 64 + 16 * j:80 + 16 * j], 1.0 / HD, RMS_EPS,
                                ALU.mult, ALU.add).then_inc(s_ams, 1)
            dve.wait_ge(s_aroot, 1)
            s(v.reciprocal(st[:, 96:128], st[:, 96:128]))
            ch.settle()
            for j, buf in enumerate((aq, ak)):
                b = buf.rearrange("p a (h w) -> p (a h) w", w=HD)
                v.tensor_tensor(b, b, st[:, 96 + 16 * j:112 + 16 * j].unsqueeze(2).broadcast_to([P, TT * AH, HD]),
                                ALU.mult).then_inc(s_an, 1)
            for j, (buf, g) in enumerate(((qT, QG), (kT, KG))):
                dve.wait_ge(s_qkT_ps, j + 1)
                v.tensor_scalar(buf, bank(4 + 2 * j, 2)
                                .rearrange("p (c t) -> p c t", c=CB), vecT[:, g:g + 1], None, ALU.mult)\
                    .then_inc(s_qkT, 1)
            def merge(n):
                for half in range(2):
                    u = [11, 15, 19][n] + half
                    dve.wait_ge(s_full, u + 1)
                    dve.wait_ge(s_free[(u - 2) % 2], (u - 2) // 2 + 1)
                    y = unit(u).rearrange("p (c t) -> p c t", c=CB)
                    m = merged[:, 4 * half:4 * half + 4, :]
                    to = m if n == 0 else prod
                    if n:
                        dve.wait_ge(s_gate_used, 2 * (n - 1) + half)
                    v.tensor_tensor(to, gate[half], y, ALU.mult).then_inc(s_free[u % 2], 1)
                    dve.wait_ge(s_free[u % 2], u // 2 + 1)
                    if n:
                        v.tensor_tensor(m, m, prod, ALU.add).then_inc(s_gate_used, 1)

            merge(0)
            for g in range(2):
                dve.wait_ge(s_asc_ps, g + 1)
                if g:
                    dve.wait_ge(s_PT_ps, 1)
                s(v.tensor_tensor(Pm, ps[:, 4:8, 0:384],
                                  causal[:].rearrange("p a s -> p (a s)").unsqueeze(1).broadcast_to([P, 4, 384]), ALU.add))
                ch.settle()
                mx = st[:, 128:136].rearrange("p (h a) -> p h a", a=TT)
                s(v.tensor_reduce(mx[:, :, 0], Pm[:, :, 0:P], AX_X, ALU.max))
                s(v.tensor_reduce(mx[:, :, 1], Pm[:, :, P:3 * P], AX_X, ALU.max))
                ch.settle()
                v.tensor_scalar(st[:, 144:152], st[:, 128:136], -SCALE, None, ALU.mult).then_inc(s_amax, 1)
                dve.wait_ge(s_aexp, 8 * (g + 1))
                s(v.reciprocal(st[:, 176 + 8 * g:184 + 8 * g], st[:, 160 + 8 * g:168 + 8 * g]))
                ch.settle()
                dve.wait_ge(s_ao_ps, g + 1)
                r = st[:, 176 + 8 * g:184 + 8 * g].rearrange("p (h a) -> p h a", a=TT)
                for a in range(TT):
                    v.tensor_tensor(a_o[:, a, 256 * g:256 * g + 256].rearrange("p (h w) -> p h w", w=HD),
                                    bank(4 + a)[:, 0:256].rearrange("p (h w) -> p h w", w=HD),
                                    r[:, :, a:a + 1].broadcast_to([P, 4, HD]), ALU.mult).then_inc(s_ao, 1)
            merge(1)
            merge(2)
            for a in range(TT):
                u = 21 + a
                dve.wait_ge(s_full, u + 1)
                v.tensor_tensor(xs[:, a, :], xs[:, a, :], unit(u), ALU.add).then_inc(s_x2, 1)
            dve.wait_ge(s_ssq2, 2)
            v.tensor_scalar(st[:, 204:206], st[:, 200:202], 1.0 / D, RMS_EPS, ALU.mult, ALU.add).then_inc(s_ms2, 1)
            dve.wait_ge(s_root2, 1)
            s(v.reciprocal(st[:, 208:210], st[:, 206:208]))
            ch.settle()
            for a in range(TT):
                v.tensor_scalar(h2[:, a, :], xs[:, a, :], st[:, 208 + a:209 + a], None, ALU.mult).then_inc(s_h2, 1)
            for k in range(0, KD, 2):
                dve.wait_ge(s_h2T_ps, k // 2 + 1)
                dve.wait_ge(s_h2T_odd, k // 2 + 1)
                v.tensor_scalar(hT[:, k, :], bank(4 + k // 2)[:, 0:S2], vecT[:, FFNG + k:FFNG + k + 1], None,
                                ALU.mult).then_inc(s_h2T_even, 1)

            def t3(o, a, b, op):
                s(v.tensor_tensor(o, a, b, op))
                ch.settle()

            def t1(o, a, s1, s2, op0, op1=None):
                s(v.tensor_scalar(o, a, s1, s2, op0, op1) if op1 is not None else v.tensor_scalar(o, a, s1, None, op0))
                ch.settle()

            def red(o, a, op):
                s(v.tensor_reduce(o, a, AX_X, op))
                ch.settle()

            def one_hot(o, vals, top, index, tmp, first, n):
                t3(tmp, vals, top.broadcast_to([P, TT, n]), ALU.is_equal)
                t1(tmp, tmp, -4096.0, 4096.0, ALU.mult, ALU.add)
                t3(tmp, tmp, index, ALU.add)
                red(first, tmp, ALU.min)
                t3(o, index, first.broadcast_to([P, TT, n]), ALU.is_equal)

            for j in range(E):
                last = v.memset(r_iota[:, :, j:j + 1], float(j))
                s(last)
            for j in range(G):
                s(v.memset(r_i4[:, :, j:j + 1], float(j)))
            dve.wait_ge(s_log_ps, 1)
            s(v.tensor_copy(logits, bank(0)[:, 0:TT * 64].rearrange("p (a e) -> p a e", a=TT)[:, :, 0:NL]))
            ch.settle()
            lc, lf = logits[:, :, 0:G], logits[:, :, G:NL]
            red(r_s[0], lc, ALU.max)
            one_hot(r_grp, lc, r_s[0], r_i4, r_t4, r_s[1], G)
            v.tensor_tensor(r_e4, lc, r_s[0].broadcast_to([P, TT, G]), ALU.subtract).then_inc(s_rsub, 1)
            grp_e = r_grp.unsqueeze(3).broadcast_to([P, TT, G, EG])

            def by_group(t):
                return t.rearrange("p a (g e) -> p a g e", g=G)
            for a in range(TT):
                s(v.tensor_copy(by_group(r_pen)[:, a], grp_e[:, a]))
            ch.settle()
            t3(r_fine, lf, r_pen, ALU.mult)
            t1(r_pen, r_pen, -NEG, NEG, ALU.mult, ALU.add)
            t3(r_fine, r_fine, r_pen, ALU.add)
            red(r_s[2], r_fine, ALU.max)
            one_hot(r_oh1, r_fine, r_s[2], r_iota, r_tmp, r_s[3], E)
            t1(r_tmp, r_oh1, 2 * NEG, None, ALU.mult)
            t3(r_fine, r_fine, r_tmp, ALU.add)
            red(r_s[4], r_fine, ALU.max)
            one_hot(r_oh2, r_fine, r_s[4], r_iota, r_tmp, r_s[3], E)
            v.tensor_tensor(r_s[5], r_s[4], r_s[2], ALU.subtract).then_inc(s_rsub, 1)
            v.tensor_tensor(sel, r_oh1, r_oh2, ALU.add).then_inc(s_sel, 1)
            s(v.memset(rank, 0.0))
            dve.wait_ge(s_count_ps, 1)
            s(v.tensor_reduce(most, bank(2)[:, 0:E], AX_X, ALU.max))
            ch.settle()
            v.tensor_copy(few[0:1, :], most[0:1, :]).then_inc(s_few, 1)
            dve.wait_ge(s_few, 1)
            dve.wait_ge(s_rexp, 2)
            red(r_s[6], r_e4, ALU.add)
            t1(r_s[7], r_s[5], 1.0, None, ALU.add)
            t3(r_s[8], r_s[7], r_s[6], ALU.mult)
            s(v.reciprocal(r_s[9], r_s[8]))
            ch.settle()
            t3(r_s[10], r_s[9], r_s[5], ALU.mult)
            t3(r_oh1, r_oh1, r_s[9].broadcast_to([P, TT, E]), ALU.mult)
            t3(r_oh2, r_oh2, r_s[10].broadcast_to([P, TT, E]), ALU.mult)
            s(v.tensor_tensor(weight[:, :, 0:E], r_oh1, r_oh2, ALU.add))
            dve.wait_ge(s_rank_ps, 1)
            t1(rank[:, :, 0:E], bank(0)[:, 0:TT * E].rearrange("p (a e) -> p a e", a=TT), 1.0, None, ALU.add)
            t3(rank[:, :, 0:E], rank[:, :, 0:E], sel, ALU.mult)
            v.tensor_scalar(rank, rank, -1.0, None, ALU.add).then_inc(s_combine, 1)
            dve.wait_ge(s_combine, 1)
            n_most = dve.value_load(few[0:1, 0:1], min_val=0, max_val=SEQ)
            with dve.If(n_most <= CAP):
                def places(q):
                    p4 = place.rearrange("p a (j c) -> p a j c", j=2)
                    w4 = wplace.rearrange("p a (j c) -> p a j c", j=2)
                    for a in range(TT):
                        s_pl = v.tensor_tensor(
                            p4[:, a], place_no[:].unsqueeze(1).broadcast_to([P, 2, CAP]),
                            rank_q[:, a, bass.ds(q, 1), :].rearrange("p q j -> p (q j)").unsqueeze(2)
                            .broadcast_to([P, 2, CAP]), ALU.is_equal)
                    s_pl.then_inc(s_placed, 1)
                    dve.wait_ge(s_placed, q + 1)
                    for a in range(TT):
                        s_pl = v.tensor_tensor(
                            w4[:, a], p4[:, a],
                            weight_q[:, a, bass.ds(q, 1), :].rearrange("p q j -> p (q j)").unsqueeze(2)
                            .broadcast_to([P, 2, CAP]), ALU.mult)
                    s_pl.then_inc(s_G, 1)

                def gathered(q):
                    dve.wait_ge(s_gather, q + 1)
                    gain = vecT[:, FFNG:FFNG + KD].unsqueeze(2).broadcast_to([P, KD, 2 * CAP])
                    v.tensor_tensor(xg, bank(4, 2).rearrange("p (k c) -> p k c", k=KD), gain, ALU.mult).then_inc(s_xg, 1)

                places(0)
                gathered(0)
                with nc.Fori(0, E // 2, 1, engines=[dve.engine]) as q:
                    for j in range(2):
                        dve.wait_ge(s_sil, q * 2 + (j + 1))
                        v.tensor_tensor(e_act[:, j, :], e_sil[:, j, :], bank(6 + j)[:, FH:2 * FH], ALU.mult)\
                            .then_inc(s_act2, 1)
                        if j == 0:
                            dve.wait_ge(s_GwT_ps, q + 1)
                            places(q + 1)
                        else:
                            gathered(q + 1)
                        dve.wait_ge(s_out_used, q * 2 + (j + 1))
                        v.tensor_copy(y_sb[j * CAP:(j + 1) * CAP, 0:512], bank(6 + j)[0:CAP, :]).then_inc(s_Yv, 1)
                dve.wait_ge(s_scat, E // 2 + 1)
                v.tensor_copy(xs[:, 0, :], bank(0, 2)).then_inc(s_final[0], 1)
            with dve.Else():
                with nc.Fori(0, E, 1, engines=[dve.engine]) as e:
                    for a in range(TT):
                        dve.wait_ge(s_sil, e * TT + (a + 1))
                        v.tensor_tensor(e_act, e_sil, ps[:, 0:2, FH:2 * FH], ALU.mult).then_inc(s_act2, 1)
                        if a == 0:
                            dve.wait_ge(s_Y0_ps, e + 1)
                        else:
                            dve.wait_ge(s_out_used, e + 1)
                        v.scalar_tensor_tensor(out=xs[:, a, :], in0=bank(4, 2), scalar=weight[:, a, bass.ds(e, 1)],
                                               in1=xs[:, a, :], op0=ALU.mult, op1=ALU.add).then_inc(s_Yfree, 1)
                        dve.wait_ge(s_Yfree, e * TT + (a + 1))
                for a in range(TT):
                    v.tensor_copy(e_sil[:, a, 0:1], xs[:, a, 0:1]).then_inc(s_final[a], 1)

        @block.tensor
        def _(pe):
            mm, tr = nc.tensor.matmul, nc.tensor.transpose
            pe.wait_ge(s_const, 1)
            pe.wait_ge(s_small, 16 * 13)
            tr(bank(0)[:, 0:NVEC], vec_rows[0:NVEC, :], ident[0:NVEC, 0:NVEC])
            n = TAPS * CB
            tr(bank(0)[:, P:P + n], tap_rows[0:n, :], ident[0:n, 0:n]).then_inc(s_vec_ps, 1)

            def turn(src, ready, done):
                pe.wait_ge(ready, TT)
                for k in range(KD):
                    for a in range(TT):
                        last = tr(bank(4 + k // 2)[:, (k % 2) * S2 + a * P:(k % 2) * S2 + (a + 1) * P],
                                  src[:, a, k * P:(k + 1) * P], ident[:])
                    if k % 2:
                        last.then_inc(done, 1)

            turn(h_tok, s_h, s_hT_ps)
            pe.wait_ge(s_hT_odd, KD // 2)
            pe.wait_ge(s_hT_even, KD // 2)

            def begin(u):
                if u == 0:
                    pe.wait_ge(s_vec, 1)
                if u >= 2:
                    pe.wait_ge(s_free[u % 2], u // 2)
                return bank(2 * (u % 2), 2)

            def cols_by_tokens(u, l, rhs=None):
                o = begin(u)
                wait_landed(pe, l)
                w = wcols(l)
                for c in range(CB):
                    for k in range(KD):
                        last = mm(o[:, c * S2:(c + 1) * S2], w[:, k, c * P:(c + 1) * P], hT[:, k, :],
                                  start=k == 0, stop=k == KD - 1)
                last.then_inc(s_full, 1)

            def tokens_by_cols(u, l):
                o = begin(u)
                wait_landed(pe, l)
                w = wcols(l)
                for a in range(TT):
                    for k in range(KD):
                        last = mm(o[:, a * W:(a + 1) * W], hT[:, k, a * P:(a + 1) * P], w[:, k, :],
                                  start=k == 0, stop=k == KD - 1)
                last.then_inc(s_full, 1)

            def branch(u0, l, oT):
                w = wrows(l)
                wait_landed(pe, l)
                for half in range(2):
                    o = begin(u0 + half)
                    for c in range(CB):
                        for k in range(CB):
                            last = mm(o[:, c * S2:(c + 1) * S2], w[:, k, half * W + c * P:half * W + (c + 1) * P],
                                      oT[:, k, :], start=k == 0, stop=k == CB - 1)
                    last.then_inc(s_full, 1)

            def level(i):
                if i < 8:
                    q, k = Qx[i % 2], Kx[i % 2]
                    pe.wait_ge(s_Q, i + 1)
                    pe.wait_ge(s_K, i + (2 if i == 0 else 3))
                else:
                    q, k = hq, hk
                if i >= 2:
                    pe.wait_ge(s_SCfree, i - 1)
                b = 4 + 2 * (i % 2)
                for h in range(HH):
                    if i == 0:
                        last = mm(bank(b)[:, h * P:(h + 1) * P], k[:, h, 0:P], q[:, h, P:2 * P], start=True, stop=True)
                    else:
                        for a in range(TT):
                            last = mm(bank(b + a)[:, h * P:(h + 1) * P], k[:, h, a * P:(a + 1) * P],
                                      q[:, h, a * P:(a + 1) * P], start=True, stop=True)
                last.then_inc(s_SC, 1)

            cols_by_tokens(0, 0)
            cols_by_tokens(1, 1)
            cols_by_tokens(2, 2)
            cols_by_tokens(3, 3)
            tokens_by_cols(4, 4)
            tokens_by_cols(5, 5)
            tokens_by_cols(6, 6)
            pe.wait_ge(s_taps, TAPS * CB)
            pe.wait_ge(s_hT_odd, KD // 2)
            pe.wait_ge(s_hT_even, KD // 2)
            for c in range(CB):
                last = mm(bank(4)[:, 0:S2], ones[:], c_acc[:, c, :], start=c == 0, stop=c == CB - 1)
            last.then_inc(s_mean_ps, 1)
            tokens_by_cols(7, 7)
            tokens_by_cols(8, 8)
            pe.wait_ge(s_cdev, 1)
            level(0)
            for i in range(1, 9):
                level(i)
            pe.wait_ge(s_csq, 1)
            pe.wait_ge(s_SCfree, 8)
            for c in range(CB):
                last = mm(bank(7)[:, 0:S2], ones[:], c_sig[:, c, :], start=c == 0, stop=c == CB - 1)
            last.then_inc(s_var_ps, 1)
            pe.wait_ge(s_SCfree, 9)
            for h in range(HH):
                w = slice(h * P, (h + 1) * P)
                mm(bank(4)[:, w], ST[:, 0, h, :], hv[:, 0, w], start=True, stop=True)
                mm(bank(5)[:, w], ST[:, 2, h, :], hv[:, 0, w], start=True, stop=False)
                last = mm(bank(5)[:, w], ST[:, 1, h, :], hv[:, 1, w], start=False, stop=True)
            last.then_inc(s_ho_ps, 1)
            cols_by_tokens(9, 9)

            def turn4(src, b, done):
                for c in range(CB):
                    for a in range(TT):
                        last = tr(bank(b, 2)[:, c * S2 + a * P:c * S2 + (a + 1) * P], src[:, a, c * P:(c + 1) * P], ident[:])
                last.then_inc(done, 1)

            pe.wait_ge(s_hon, 1)
            pe.wait_ge(s_cn, 1)
            turn4(h_o, 6, s_hoT_ps)
            cols_by_tokens(10, 10)
            pe.wait_ge(s_an, 2)
            turn4(aq, 4, s_qkT_ps)
            pe.wait_ge(s_hoT, 1)
            turn4(ak, 6, s_qkT_ps)
            pe.wait_ge(s_convT, CB)
            branch(11, 11, c_acc)
            pe.wait_ge(s_qkT, 2)

            def scores(g):
                if g:
                    pe.wait_ge(s_ao, TT)
                for j in range(4):
                    h = 4 * g + j
                    r = slice(HD * (h % 2), HD * (h % 2) + HD)
                    mm(bank(4 + j)[:, 0:P], qT[r, h // 2, 0:P], kT[r, h // 2, 0:P], start=True, stop=True)
                    last = mm(bank(4 + j)[:, P:3 * P], qT[r, h // 2, P:2 * P], kT[r, h // 2, :], start=True, stop=True)
                last.then_inc(s_asc_ps, 1)

            def turn_p(g):
                pe.wait_ge(s_aexp, 8 * (g + 1))
                for j in range(4):
                    for b in range(3):
                        last = tr(bank(4 + j)[:, b * P:(b + 1) * P], Pm[:, j, b * P:(b + 1) * P], ident[:])
                last.then_inc(s_PT_ps, 1)

            def values(g):
                pe.wait_ge(s_PT, g + 1)
                for j in range(4):
                    h = 4 * g + j
                    w, o = slice(h * HD, (h + 1) * HD), slice(j * HD, (j + 1) * HD)
                    mm(bank(4)[:, o], PT[:, j, 0:P], av[:, 0, w], start=True, stop=True)
                    mm(bank(5)[:, o], PT[:, j, P:2 * P], av[:, 0, w], start=True, stop=False)
                    last = mm(bank(5)[:, o], PT[:, j, 2 * P:3 * P], av[:, 1, w], start=False, stop=True)
                last.then_inc(s_ao_ps, 1)

            scores(0)
            cols_by_tokens_no7 = cols_by_tokens
            cols_by_tokens_no7(13, 12)
            turn_p(0)
            values(0)
            scores(1)
            cols_by_tokens(14, 13)
            turn_p(1)
            values(1)
            branch(15, 14, h_oT)
            pe.wait_ge(s_ao, 2 * TT)
            turn4(a_o, 6, s_aoT_ps)
            cols_by_tokens(17, 15)
            cols_by_tokens(18, 16)
            pe.wait_ge(s_aoT, 1)
            branch(19, 17, a_oT)
            pe.wait_ge(s_gate_used, 4)
            for a in range(TT):
                o = begin(21 + a)
                for half in range(2):
                    wait_landed(pe, L_OUT + half)
                    for k in range(KD):
                        last = mm(o[:, half * W:(half + 1) * W], merged[:, k, a * P:(a + 1) * P],
                                  wcols(L_OUT + half)[:, k, :], start=k == 0, stop=k == KD - 1)
                last.then_inc(s_full, 1)
            turn(h2, s_h2, s_h2T_ps)
            pe.wait_ge(s_h2T_odd, KD // 2)
            pe.wait_ge(s_h2T_even, KD // 2)
            pe.wait_ge(s_router_w, 64)
            pe.wait_ge(s_x2, 2)
            for a in range(TT):
                o = bank(0)[:, a * 64:a * 64 + NL]
                for k in range(KD):
                    mm(o, hT[:, k, a * P:(a + 1) * P], w_router[:, k, :], start=k == 0, stop=False)
                last = mm(o, ones[0:1, :], b_router[0:1, :], start=False, stop=True)
            last.then_inc(s_log_ps, 1)
            pe.wait_ge(s_sel, 1)
            mm(bank(0)[:, 0:E], before[:], sel[:, 0, :], start=True, stop=True)
            mm(bank(0)[:, E:2 * E], ones[:], sel[:, 0, :], start=True, stop=False)
            mm(bank(0)[:, E:2 * E], before[:], sel[:, 1, :], start=False, stop=True).then_inc(s_rank_ps, 1)
            for a in range(TT):
                last = mm(bank(2)[:, 0:E], ones[:], sel[:, a, :], start=a == 0, stop=a == TT - 1)
            last.then_inc(s_count_ps, 1)
            pe.wait_ge(s_combine, 1)
            n_most = pe.value_load(few[0:1, 0:1], min_val=0, max_val=SEQ)

            def expert_landed(r, g, parts):
                for part in parts:
                    landed_part, before_first = expert_sem(g, part)
                    pe.wait_ge(landed_part, r * 16 + (before_first + 16))

            with pe.If(n_most <= CAP):
                for a in range(TT):
                    for c in range(2):
                        last = mm(bank(2 * a + c), ident[:], xs[:, a, c * 512:(c + 1) * 512], start=True, stop=False,
                                  skip_group_check=True)
                last.then_inc(s_scat, 1)

                def gather(q):
                    pe.wait_ge(s_G, q + 1)
                    for k in range(KD):
                        o = bank(4, 2)[:, k * 2 * CAP:(k + 1) * 2 * CAP]
                        for a in range(TT):
                            last = mm(o, h2[:, a, k * P:(k + 1) * P], place[:, a, :], start=a == 0, stop=a == TT - 1)
                    last.then_inc(s_gather, 1)

                def expert_in(r, g, j):
                    expert_landed(r, g, (0, 1))
                    for k in range(KD):
                        for f in range(2):
                            last = mm(ps[f * CAP:(f + 1) * CAP, 6 + j, :].rearrange("p (g n) -> p g n", g=2),
                                      xg[:, k, j * CAP:(j + 1) * CAP], expert_cols(g, k, f), start=k == 0, stop=k == KD - 1)
                    last.then_inc(s_in_used, 1)

                def expert_out(q, r, g, j):
                    pe.wait_ge(s_act2, q * 2 + (j + 1))
                    for b in range(2):
                        last = tr(bank(6 + j)[:, b * P:(b + 1) * P], e_act[:, j, b * P:(b + 1) * P], ident[:])
                    last.then_inc(s_T_ps, 1)
                    expert_landed(r, g, (2,))
                    pe.wait_ge(s_T, q * 2 + (j + 1))
                    for f in range(FT):
                        for c in range(2):
                            last = mm(bank(6 + j)[c * CAP:(c + 1) * CAP, :],
                                      e_actT[:, 2 * j + f % 2, (f // 2) * CAP:(f // 2 + 1) * CAP],
                                      expert_rows(g, 2)[:, f, c * 512:(c + 1) * 512], start=f == 0, stop=f == FT - 1)
                    last.then_inc(s_out_used, 1)

                def scatter(n_taken):
                    pe.wait_ge(s_Yv, n_taken)
                    pe.wait_ge(s_Ya, n_taken)
                    for a in range(TT):
                        for c in range(2):
                            last = mm(bank(2 * a + c), wplaceT[:, a * P:(a + 1) * P], y_sb[:, c * 512:(c + 1) * 512],
                                      start=False, stop=False, skip_group_check=True)
                    last.then_inc(s_scat, 1)

                def pair(q, experts, first):
                    pe.wait_ge(s_xg, q + 1)
                    if not first:
                        pe.wait_ge(s_Yv, q * 2 - 1)
                        pe.wait_ge(s_Ya, q * 2 - 1)
                    expert_in(*experts[0], 0)
                    if not first:
                        scatter(q * 2)
                    for a in range(TT):
                        last = tr(bank(4)[:, a * P:(a + 1) * P], wplace[:, a, :], ident[:])
                    last.then_inc(s_GwT_ps, 1)
                    expert_out(q, *experts[0], 0)
                    expert_in(*experts[1], 1)
                    pe.wait_ge(s_GwT, q + 1)
                    gather(q + 1)
                    expert_out(q, *experts[1], 1)

                gather(0)
                pair(0, [(0, 0), (0, 1)], True)
                with nc.Fori(0, (E // 2 - 1) // 3, 1, engines=[pe.engine]) as t:
                    for i in range(3):
                        n = 2 * (i + 1)
                        pair(t * 3 + (i + 1), [(t * 2 + (n + j) // GROUPS, (n + j) % GROUPS) for j in range(2)], False)
                scatter(E)
            with pe.Else():
                def dense(e, r, g):
                    expert_landed(r, g, range(EXP))
                    for a in range(TT):
                        for f in range(2):
                            for k in range(KD):
                                last = mm(ps[:, f, :].rearrange("p (g n) -> p g n", g=2), hT[:, k, a * P:(a + 1) * P],
                                          expert_cols(g, k, f),
                                          start=k == 0, stop=k == KD - 1)
                        last.then_inc(s_H0_ps if a == 0 else s_in_used, 1)
                        pe.wait_ge(s_act2, e * TT + (a + 1))
                        for f in range(FT):
                            last = tr(bank(2)[:, f * P:(f + 1) * P], e_act[:, f // 2, (f % 2) * P:(f % 2 + 1) * P],
                                      ident[:])
                        last.then_inc(s_T_ps, 1)
                        pe.wait_ge(s_T, e * TT + (a + 1))
                        for c in range(2):
                            for f in range(FT):
                                last = mm(bank(4 + c), e_actT[:, f, :], expert_rows(g, 2)[:, f, c * 512:(c + 1) * 512],
                                          start=f == 0, stop=f == FT - 1)
                        last.then_inc(s_Y0_ps if a == 0 else s_out_used, 1)
                        pe.wait_ge(s_Yfree, e * TT + (a + 1))

                with nc.Fori(0, E // GROUPS, 1, engines=[pe.engine]) as r:
                    for g in range(GROUPS):
                        dense(r * GROUPS + g, r, g)
                for e in range(E - E % GROUPS, E):
                    dense(e, e // GROUPS, e % GROUPS)


_INS = ['x', 'mix_norm_g', 'w_in', 'b_gate', 'q_norm_g', 'k_norm_g', 'lb_logits', 'hgrn_norm_g', 'conv_w', 'conv_b',
        'conv_ln_g', 'conv_ln_b', 'w_att_o', 'w_hgrn_o', 'w_conv_o', 'w_out', 'ffn_norm_g', 'w_coarse', 'b_coarse',
        'w_fine', 'b_fine', 'w_exp_in', 'w_exp_out']


def kernel(**inputs):
    import numpy as _np
    import concourse.bacc as _bacc
    from concourse import mybir as _mybir
    from concourse.bass_utils import run_bass_kernel_spmd as _run

    nc = _bacc.Bacc("TRN2", target_bir_lowering=False, num_devices=1)
    arrays, args = {}, []
    for name in _INS:
        a = _np.ascontiguousarray(inputs[name])
        arrays[f"in_{name}_dram"] = a
        args.append(nc.dram_tensor(f"in_{name}_dram", a.shape, _mybir.dt.from_np(a.dtype), kind="ExternalInput").ap())
    x = inputs['x']
    args.append(nc.dram_tensor("out_0_dram", x.shape, _mybir.dt.float32, kind="ExternalOutput").ap())
    hybrid_decoder_layer(nc, *args)
    r = _run(nc, [arrays], core_ids=[0])
    return r.results[0]["out_0_dram"]
```

```python
from contextlib import ExitStack

import concourse.bass as bass
from concourse import mybir

ALU = mybir.AluOpType
ACT = mybir.ActivationFunctionType
F32 = mybir.dt.float32
I32 = mybir.dt.int32
AX_X = mybir.AxisListType.X

P = 128
NEG = -1e30
RMS_EPS = 1e-6
LN_EPS = 1e-5
LEAST_FORGET = 2.0 ** -63


class Chain:

    def __init__(self, eng, sem):
        self.eng, self.sem, self.n = eng, sem, 0

    def step(self, ins):
        ins.then_inc(self.sem, 1)
        self.n += 1
        return self.n

    def settle(self, upto=None):
        self.eng.wait_ge(self.sem, self.n if upto is None else upto)


def hybrid_decoder_layer(nc, x, mix_norm_g, w_in, b_gate, q_norm_g, k_norm_g, lb_logits, hgrn_norm_g,
                         conv_w, conv_b, conv_ln_g, conv_ln_b, w_att_o, w_hgrn_o, w_conv_o, w_out,
                         ffn_norm_g, w_coarse, b_coarse, w_fine, b_fine, w_exp_in, w_exp_out, out):
    _, SEQ, D = x.shape
    TT = SEQ // P
    KD = D // P
    HD = q_norm_g.shape[1]
    W = w_att_o.shape[1]
    CB = W // P
    AH = W // HD
    HH = W // hgrn_norm_g.shape[1]
    TAPS = conv_w.shape[1]
    G = w_coarse.shape[2]
    E = w_fine.shape[2]
    EG = E // G
    FF = w_exp_out.shape[2]
    FT = FF // P
    CHUNK = 64
    assert (SEQ, D, W, HD, HH, FF, EG) == (256, 1024, 512, 64, 4, 512, 8)
    SCALE = float(HD) ** -0.5
    S2 = TT * P
    CAP = 64
    EXP = 3

    with ExitStack() as ctx:
        def sb(name, shape, dt=F32):
            return ctx.enter_context(nc.sbuf_tensor(name, shape, dt))

        def sem(name):
            return ctx.enter_context(nc.semaphore(name))

        NSLOT = 6
        UNIT = 4096
        ring = sb("ring", [P, NSLOT, UNIT])
        xs = sb("xs", [P, TT, D])
        hT = sb("hT", [P, KD, S2])
        ident = sb("ident", [P, P])
        ones = sb("ones", [P, P])
        vecT = sb("vecT", [P, 64])
        tapT = sb("tapT", [P, TAPS * CB])
        causal = sb("causal", [P, 3, P])
        level_mask = sb("level_mask", [P, 8, P], I32)
        chunk_keep = sb("chunk_keep", [P, S2])
        w_router = sb("w_router", [P, KD, G + E])
        b_router = sb("b_router", [1, G + E])
        before = sb("before", [P, P])
        place_no = sb("place_no", [P, CAP])
        few = sb("few", [1, 1], I32)
        st = sb("st", [P, 256])
        K = 1024
        arena = sb("arena", [P, 21248])

        def at(k, n):
            o = int(k * K)
            return arena[:, o:o + n]

        def chan(k):
            return at(k, CB * S2).rearrange("p (c t) -> p c t", c=CB)

        def tok(k):
            return at(k, TT * W).rearrange("p (a w) -> p a w", a=TT)

        ps = ctx.enter_context(nc.psum_tensor("ps", [P, 8, 512], F32))

        def bank(b, n=1):
            return ps[:, b:b + n, :].rearrange("p b f -> p (b f)")

        h_tok = at(0, TT * D).rearrange("p (a d) -> p a d", a=TT)
        vec_rows = at(10.5, P)
        tap_rows = at(11, P)
        idx_s = at(2, P).bitcast(I32)
        idx_t = at(2.25, P).bitcast(I32)
        idx_x = at(2.5, P).bitcast(I32)
        hq, hk, hb = chan(0), chan(1), chan(2)
        hf = chan(3)
        Ex, Qx, Kx = [chan(3), chan(4)], [chan(5), chan(6)], [chan(7), chan(8)]
        ST = at(9, 3 * W).rearrange("p (a h t) -> p a h t", a=3, h=HH)
        hv, hg = tok(10.5), tok(11.5)
        h_sq, h_o = tok(5), tok(6)
        h_oT = chan(11.5)
        aq, ak, av = tok(12.5), tok(13.5), tok(14.5)
        q_sq, k_sq = tok(4), tok(15.5)
        qT, kT = chan(7), chan(8)
        Pm = at(0, 4 * 384).rearrange("p (h s) -> p h s", h=4)
        PT = at(2, 4 * 384).rearrange("p (h s) -> p h s", h=4)
        a_o = tok(13.5)
        a_oT = chan(12.5)
        PAD = TAPS - 1
        c_sig = chan(15.5)
        c_u = at(16.5, CB * (PAD + S2)).rearrange("p (c t) -> p c t", c=CB)
        c_acc = at(17.75, CB * S2).rearrange("p (c t) -> p c t", c=CB)
        gate = [chan(15.5), chan(16.5)]
        prod = c_acc
        merged = at(18.75, KD * S2).rearrange("p (k t) -> p k t", k=KD)

        X_SSQ, X_MS, X_ROOT, X_RSTD = 0, 4, 6, 8
        LB_SHIFT, LB_EXP, LB_INV, LBOUND, ONE_LB, LB_ONE = 16, 20, 24, 28, 32, 36
        HO_MS, HO_ROOT, HO_RSTD = 40, 48, 56
        QK_MS, QK_RSTD = 64, 96
        A_MAX, A_BIAS, A_SUM, A_INV = 128, 144, 160, 176
        X2_SSQ, X2_MS, X2_ROOT, X2_RSTD, X2_PART = 200, 204, 206, 208, 210
        WARM = 240

        def col(name, i, n=1):
            return st[:, name + i:name + i + n]

        MIXG, FFNG, BG, CVB, LNG, LNB, LB, HNG, QG, KG = 0, 8, 16, 40, 44, 48, 52, 56, 57, 58
        NVEC = 59
        N_SMALL = 12

        s_x = [sem(f"x_tile{a}_landed") for a in range(TT)]
        s_first = sem("first_half_load_landed")
        s_gain = sem("mixer_gain_landed")
        s_small = sem("small_landed")
        s_router_w = sem("router_weights_landed")
        landed = [sem(f"slot{i}_landed") for i in range(NSLOT)]
        landed_top = [sem(f"arena_slot{i}_landed") for i in range(3)]
        s_const = sem("constants_ready")
        s_pool = sem("pool_chain")
        s_dve = sem("dve_chain")
        s_masks = sem("level_masks_ready")
        s_ssq = sem("square_sums_ready")
        s_root = sem("roots_ready")
        s_h = sem("h_ready")
        s_hT_ps = sem("hT_in_psum")
        s_hT = sem("hT_ready")
        s_vec_ps = sem("vectors_in_psum")
        s_vec = sem("vectors_ready")
        s_full = sem("unit_in_psum")
        s_free = [sem("pair0_free"), sem("pair1_free")]
        s_taps = sem("conv_tap_done")
        s_f = sem("forget_ready")
        s_lf = sem("log_forget_ready")
        s_D = sem("exponents_ready")
        s_E = sem("decays_ready")
        s_K = sem("level_keys_ready")
        s_Q = sem("level_queries_ready")
        s_SC = sem("level_scores_in_psum")
        s_SCfree = sem("level_scores_taken")
        s_lb0 = sem("lb_shifted")
        s_lb1 = sem("lb_exp_ready")
        s_asq = sem("attention_squares_ready")
        s_mean_ps = sem("conv_mean_in_psum")
        s_cdev = sem("conv_deviation_ready")
        s_csq = sem("conv_squares_ready")
        s_var_ps = sem("conv_var_in_psum")
        s_cvar = sem("conv_var_ready")
        s_croot = sem("conv_root_ready")
        s_cn = sem("conv_normalised")
        s_convT = sem("conv_out_ready")
        s_ho_ps = sem("hgrn_o_in_psum")
        s_hosq = sem("hgrn_o_squares_ready")
        s_hms = sem("hgrn_ms_ready")
        s_hroot = sem("hgrn_root_ready")
        s_hon = sem("hgrn_o_normalised")
        s_hoT_ps = sem("hgrn_oT_in_psum")
        s_hoT = sem("hgrn_oT_ready")
        s_ams = sem("attention_ms_ready")
        s_aroot = sem("attention_roots_ready")
        s_an = sem("attention_qk_normalised")
        s_qkT_ps = sem("qkT_in_psum")
        s_qkT = sem("qkT_ready")
        s_asc_ps = sem("attention_scores_in_psum")
        s_amax = sem("attention_max_ready")
        s_aexp = sem("attention_exp_ready")
        s_PT_ps = sem("PT_in_psum")
        s_PT = sem("PT_ready")
        s_ao_ps = sem("attention_o_in_psum")
        s_ao = sem("attention_o_ready")
        s_aoT_ps = sem("attention_oT_in_psum")
        s_aoT = sem("attention_oT_ready")
        s_gate_used = sem("gate_half_used")
        s_x2 = sem("x2_ready")
        s_ssq2 = sem("square_sums2_ready")
        s_ms2 = sem("mean_squares2_ready")
        s_root2 = sem("root2_ready")
        s_h2 = sem("h2_ready")
        s_h2T_ps = sem("h2T_in_psum")
        s_h2T = sem("h2T_ready")
        s_ms = sem("mean_squares_ready")
        s_log_ps = sem("router_logits_in_psum")
        s_rneg = sem("router_maxima_ready")
        s_rexp = sem("router_exp_ready")
        s_sel = sem("selection_ready")
        s_rank_ps = sem("ranks_in_psum")
        s_count_ps = sem("counts_in_psum")
        s_few = sem("most_tokens_ready")
        s_in_used = [sem(f"expert_in_part{i}_used") for i in range(2)]
        s_out_used = sem("expert_out_complete")
        s_H0_ps = sem("first_tile_hidden_in_psum")
        s_Y0_ps = sem("first_tile_out_in_psum")
        s_Yfree = sem("expert_out_taken")
        s_sil = sem("expert_silu_ready")
        s_act2 = sem("expert_act_ready")
        s_T_ps = sem("expert_actT_in_psum")
        s_T = sem("expert_actT_ready")
        s_placed = sem("unweighted_places_ready")
        s_G = sem("places_ready")
        s_gather = sem("gathered_in_psum")
        s_xg = sem("gathered_ready")
        s_GwT_ps = sem("weighted_placesT_in_psum")
        s_GwT = sem("weighted_placesT_ready")
        s_Yv = sem("expert_out_left_taken")
        s_Ya = sem("expert_out_right_taken")
        s_scat = sem("experts_added")
        s_final = [[sem(f"result_tile{a}_half{c}_ready") for c in range(2)] for a in range(TT)]
        s_out = sem("out_stored")

        wi = w_in[0].rearrange("(k p) n -> p k n", p=P)
        IN = {n: i for i, n in enumerate(["aq", "ak", "av", "hq", "hf", "hi", "hg", "ca", "cb"])}

        def in_cols(c):
            return wi[:, :, c * W:(c + 1) * W]

        def o_rows(w):
            return w[0].rearrange("(k p) n -> p k n", p=P)

        wo = w_out[0].rearrange("(k p) n -> p k n", p=P)
        order = ["hf", "hq", "hi", "cb", "ca", "hg", "aq", "ak", "av"]
        sources = [in_cols(IN[n]) for n in order]
        for b, w in ((2, w_conv_o), (1, w_hgrn_o), (0, w_att_o)):
            sources += [in_cols(9 + 2 * b), in_cols(10 + 2 * b), o_rows(w)]
        sources += [wo[:, :, 0:W], wo[:, :, W:D]]
        NMIX = len(sources)
        L_OUT = 18
        LAST_UNIT = [*range(9), 9, 10, 12, 13, 14, 16, 17, 18, 20, 23, 24]

        def slot(l):
            return ring[:, l % NSLOT, :]

        def wcols(l):
            return slot(l).rearrange("p (k n) -> p k n", k=KD)

        def wrows(l):
            return slot(l).rearrange("p (k n) -> p k n", k=CB)

        def wait_landed(eng, l):
            eng.wait_ge(landed[l % NSLOT], 16 * (l // NSLOT + 1))

        GROUPS = 3

        def expert_rows(g, part):
            if g == 0:
                return at(4 * part, UNIT).rearrange("p (k n) -> p k n", k=CB)
            return wrows(NMIX + EXP * (g - 1) + part)

        def expert_sem(g, part):
            if g == 0:
                return landed_top[part], 0
            l = NMIX + EXP * (g - 1) + part
            return landed[l % NSLOT], 16 * (l // NSLOT)

        def expert_cols(g, k, f):
            return expert_rows(g, k // CB)[:, k % CB, :].rearrange("p (g f n) -> p g f n", g=2, f=2)[:, :, f, :]

        h2 = at(12.5, TT * D).rearrange("p (a d) -> p a d", a=TT)
        FH = FF // 2
        xg = at(14.5, KD * 2 * CAP).rearrange("p (k c) -> p k c", k=KD)
        place = at(15.5, TT * 2 * CAP).rearrange("p (a c) -> p a c", a=TT)
        wplace = at(15.75, TT * 2 * CAP).rearrange("p (a c) -> p a c", a=TT)
        wplaceT = at(16, S2)
        e_sil = at(16.25, FF).rearrange("p (h n) -> p h n", h=2)
        e_act = at(16.75, FF).rearrange("p (h n) -> p h n", h=2)
        e_actT = at(17.25, FF).rearrange("p (f t) -> p f t", f=FT)
        rank = at(17.75, TT * E).rearrange("p (a e) -> p a e", a=TT)
        weight = at(17.85, TT * E).rearrange("p (a e) -> p a e", a=TT)
        rank_q = rank.rearrange("p a (q j) -> p a q j", j=2)
        weight_q = weight.rearrange("p a (q j) -> p a q j", j=2)
        sel = at(17.95, TT * E).rearrange("p (a e) -> p a e", a=TT)
        most = at(18.05, 1)
        y_sb = at(18.75, D)
        SCATTERS = TT + E // 2 - 1
        NL = G + E

        def rt(i):
            return at(18.2 + i / 16, TT * E).rearrange("p (a e) -> p a e", a=TT)
        r_fine, r_fine2, r_tmp, r_oh1, r_oh2 = (rt(i) for i in range(5))
        r_iota = at(18.52, E)
        r_i4 = at(18.56, G)
        r_max, r_neg, r_first4, r_top1, r_neg1, r_first1, r_top2, r_first2, r_exp, r_sum, r_w1, r_w2, r_den = (
            at(19.75 + i / 64, TT) for i in range(13))
        r_e4, r_gm, r_t4 = (at(20 + i / 32, TT * G).rearrange("p (a e) -> p a e", a=TT) for i in range(3))
        BIG = 4096.0

        def router_ps(a):
            return bank(4 + 2 * a)[:, 0:NL]

        def rank_ps(a):
            return bank(5 + 2 * a)[:, 0:E]
        count_ps = bank(5)[:, 2 * E:3 * E]

        def result(a):
            return bank(2 * ((21 + a) % 2), 2)

        block = ctx.enter_context(nc.Block())

        @block.sync
        def _(sp):
            for a in range(TT):
                sp.dma_start(xs[:, a, :], x[0, a * P:(a + 1) * P, :]).then_inc(s_x[a], 16)
            sp.dma_start(vec_rows[MIXG:MIXG + 8, :], mix_norm_g[0].rearrange("(r p) -> r p", p=P)).then_inc(s_gain, 16)
            for l, src in enumerate(sources):
                if l >= NSLOT:
                    sp.wait_ge(s_full, LAST_UNIT[l - NSLOT] + 1)
                k = KD if src.shape[1] == KD else CB
                to = slot(l).rearrange("p (k n) -> p k n", k=k)
                if l == 0:
                    sp.dma_start(to[:, :, 0:W // 2], src[:, :, 0:W // 2]).then_inc(s_first, 16)
                    rows = [(FFNG, ffn_norm_g, 8), (BG, b_gate, 24), (CVB, conv_b, 4),
                            (LNG, conv_ln_g, 4), (LNB, conv_ln_b, 4), (LB, lb_logits, 4), (HNG, hgrn_norm_g, 1)]
                    for r, v, n in rows:
                        sp.dma_start(vec_rows[r:r + n, :], v[0].rearrange("(r p) -> r p", p=P)).then_inc(s_small, 16)
                    for r, v in ((QG, q_norm_g), (KG, k_norm_g)):
                        for i in range(P // HD):
                            sp.dma_start(vec_rows[r:r + 1, i * HD:(i + 1) * HD], v[0:1, :]).then_inc(s_small, 16)
                    sp.dma_start(tap_rows[0:TAPS * CB, :], conv_w[0].rearrange("j (c p) -> (j c) p", p=P)).then_inc(s_small, 16)
                    to, src = to[:, :, W // 2:W], src[:, :, W // 2:W]
                sp.dma_start(to, src).then_inc(landed[l % NSLOT], 16)

            def load_part(e, g, part):
                if part < 2:
                    src = w_exp_in[0][bass.ds(e, 1), part * D // 2:(part + 1) * D // 2, :]
                else:
                    src = w_exp_out[0][bass.ds(e, 1), :, :]
                sp.dma_start(expert_rows(g, part), src.rearrange("a (k p) n -> p (a k) n", p=P))\
                    .then_inc(expert_sem(g, part)[0], 16)

            sp.wait_ge(s_ao_ps, 2)
            for part in range(EXP):
                load_part(0, 0, part)
            for g in (1, 2):
                for part in range(EXP):
                    sp.wait_ge(s_full, LAST_UNIT[NMIX - NSLOT + EXP * (g - 1) + part] + 1)
                    load_part(g, g, part)

            def reload(e, g):
                for part in range(EXP):
                    sp.wait_ge(s_in_used[part] if part < 2 else s_out_used, e - 2)
                    load_part(e, g, part)

            with nc.Fori(1, E // GROUPS, 1, engines=[sp.engine]) as r:
                for g in range(GROUPS):
                    reload(r * GROUPS + g, g)
            for e in range(E - E % GROUPS, E):
                reload(e, e % GROUPS)
            for a in range(TT):
                for c in range(2):
                    sp.wait_ge(s_final[a][c], 1)
                    sp.dma_start(out[0, a * P:(a + 1) * P, c * 512:(c + 1) * 512], xs[:, a, c * 512:(c + 1) * 512])\
                        .then_inc(s_out, 16)
            sp.wait_ge(s_out, 16 * 2 * TT)

        @block.gpsimd
        def _(pool):
            ch = Chain(pool, s_pool)
            ch.step(nc.gpsimd.memset(ident[:], 0.0))
            ch.step(nc.gpsimd.memset(causal[:], 0.0))
            ch.step(nc.gpsimd.iota(idx_s, [[0, P]], base=0, channel_multiplier=1))
            ch.step(nc.gpsimd.iota(idx_t, [[1, P]], base=0, channel_multiplier=0))
            ch.step(nc.gpsimd.memset(ones[:], 1.0))
            ch.step(nc.gpsimd.memset(before[:], 1.0))
            ch.step(nc.gpsimd.iota(place_no[:], [[1, CAP]], base=1, channel_multiplier=0,
                                   allow_small_or_imprecise_dtypes=True))
            ch.step(nc.gpsimd.memset(chunk_keep[:], 1.0))
            ch.step(nc.gpsimd.memset(c_u[:, :, 0:PAD], 0.0))
            ch.settle()
            nc.gpsimd.affine_select(out=ident[:], in_=ident[:], compare_op=ALU.not_equal, fill=1.0, base=0,
                                    pattern=[[-1, P]], channel_multiplier=1).then_inc(s_const, 1)
            for c in (0, 2):
                nc.gpsimd.affine_select(out=causal[:, c, :], in_=causal[:, c, :], compare_op=ALU.is_ge, fill=NEG,
                                        base=0, pattern=[[-1, P]], channel_multiplier=1).then_inc(s_const, 1)
            nc.gpsimd.memset(chunk_keep[:].rearrange("p (c i) -> p c i", i=CHUNK)[:, :, 0:1], 0.0)\
                .then_inc(s_const, 1)
            nc.gpsimd.affine_select(out=before[:], in_=before[:], compare_op=ALU.is_gt, fill=0.0, base=0,
                                    pattern=[[1, P]], channel_multiplier=-1).then_inc(s_const, 1)
            pool.wait_ge(s_masks, 1)
            nc.gpsimd.affine_select(out=idx_x, in_=idx_x, compare_op=ALU.is_ge, fill=4096.0, base=0,
                                    pattern=[[1, P]], channel_multiplier=-1).then_inc(s_const, 1)
            for i in range(8):
                m = P >> i
                pool.wait_ge(s_E, i + 1)
                if i >= 2:
                    pool.wait_ge(s_SC, i - 1)
                kv = hk.rearrange("p c t -> p (c t)").rearrange("p (b a m) -> p b a m", a=2, m=m)
                ev = Ex[i % 2].rearrange("p c t -> p (c t)").rearrange("p (b a m) -> p b a m", a=2, m=m)
                ov = Kx[i % 2].rearrange("p c t -> p (c t)").rearrange("p (b a m) -> p b a m", a=2, m=m)
                if i < 2:
                    nc.gpsimd.memset(ov[:, :, 1, :], 0.0).then_inc(s_K, 1)
                nc.gpsimd.tensor_tensor(ov[:, :, 0, :], kv[:, :, 0, :], ev[:, :, 0, :], ALU.mult).then_inc(s_K, 1)

        @block.scalar
        def _(act):
            def warm(f, n):
                nc.scalar.activation(col(WARM, n), ones[:, 0:1], f)

            act.wait_ge(s_pool, 5)
            warm(ACT.Sqrt, 3)
            for a in range(TT):
                act.wait_ge(s_x[a], 16)
                nc.scalar.activation(at(4 + a, D), xs[:, a, :], ACT.Square, accum_out=col(X_SSQ, a)).then_inc(s_ssq, 1)
            for a in range(TT):
                act.wait_ge(s_ms, a + 1)
                nc.scalar.activation(col(X_ROOT, a), col(X_MS, a), ACT.Sqrt).then_inc(s_root, 1)
            act.wait_ge(s_lb0, 1)
            nc.scalar.activation(col(LB_EXP, 0, 4), col(LB_SHIFT, 0, 4), ACT.Exp).then_inc(s_lb1, 1)

            def unit(u):
                return bank(2 * (u % 2), 2)

            act.wait_ge(s_full, 1)
            nc.scalar.activation(hf, unit(0).rearrange("p (c t) -> p c t", c=CB), ACT.Sigmoid).then_inc(s_free[0], 1)
            act.wait_ge(s_f, 1)
            nc.scalar.activation(hf, hf, ACT.Ln).then_inc(s_lf, 1)
            for i in range(8):
                act.wait_ge(s_D, i + 1)
                nc.scalar.activation(Ex[i % 2], Ex[i % 2], ACT.Exp).then_inc(s_E, 1)
                if i == 1:
                    act.wait_ge(s_full, 2)
                    nc.scalar.activation(hq, unit(1).rearrange("p (c t) -> p c t", c=CB), ACT.Silu).then_inc(s_free[1], 1)
                if i == 3:
                    act.wait_ge(s_full, 3)
                    nc.scalar.activation(hv, unit(2).rearrange("p (a w) -> p a w", a=TT), ACT.Copy).then_inc(s_free[0], 1)
            act.wait_ge(s_full, 4)
            nc.scalar.activation(c_sig, unit(3).rearrange("p (c t) -> p c t", c=CB), ACT.Sigmoid).then_inc(s_free[1], 1)
            act.wait_ge(s_full, 6)
            nc.scalar.activation(hg, unit(5).rearrange("p (a w) -> p a w", a=TT), ACT.Silu).then_inc(s_free[1], 1)
            act.wait_ge(s_ho_ps, 1)
            nc.scalar.activation(h_sq, bank(4, 2).rearrange("p (a w) -> p a w", a=TT), ACT.Square).then_inc(s_hosq, 1)
            for j, (buf, sq) in enumerate(((aq, q_sq), (ak, k_sq))):
                act.wait_ge(s_full, 7 + j)
                nc.scalar.activation(buf, unit(6 + j).rearrange("p (a w) -> p a w", a=TT), ACT.Copy)\
                    .then_inc(s_free[j], 1)
                if j == 0:
                    act.wait_ge(s_SC, 8)
                else:
                    act.wait_ge(s_free[0], 3)
                act.wait_ge(s_free[j], 4)
                nc.scalar.activation(sq, buf, ACT.Square).then_inc(s_asq, 1)
            act.wait_ge(s_full, 9)
            nc.scalar.activation(av, unit(8).rearrange("p (a w) -> p a w", a=TT), ACT.Copy).then_inc(s_free[0], 1)
            act.dma_start(b_router[0:1, 0:G], b_coarse[0:1, :]).then_inc(s_router_w, 16)
            act.dma_start(b_router[0:1, G:G + E], b_fine[0:1, :]).then_inc(s_router_w, 16)
            act.dma_start(w_router[:, :, 0:G], w_coarse[0].rearrange("(k p) n -> p k n", p=P)).then_inc(s_router_w, 16)
            act.dma_start(w_router[:, :, G:G + E], w_fine[0].rearrange("(k p) n -> p k n", p=P)).then_inc(s_router_w, 16)
            act.wait_ge(s_hms, 1)
            nc.scalar.activation(col(HO_ROOT, 0, 8), col(HO_MS, 0, 8), ACT.Sqrt).then_inc(s_hroot, 1)
            act.wait_ge(s_ams, 2)
            nc.scalar.activation(col(QK_RSTD, 0, 32), col(QK_MS, 0, 32), ACT.Sqrt).then_inc(s_aroot, 1)
            act.wait_ge(s_cdev, 1)
            nc.scalar.activation(c_sig, c_acc, ACT.Square).then_inc(s_csq, 1)
            act.wait_ge(s_cvar, 1)
            nc.scalar.activation(c_u[:, 0, 0:S2], c_u[:, 0, 0:S2], ACT.Sqrt).then_inc(s_croot, 1)

            def conv_out():
                act.wait_ge(s_cn, 1)
                for c in range(CB):
                    nc.scalar.activation(c_acc[:, c, :], c_acc[:, c, :], ACT.Silu, bias=vecT[:, LNB + c:LNB + c + 1],
                                         scale=vecT[:, LNG + c:LNG + c + 1]).then_inc(s_convT, 1)

            def gates(b, n, half):
                u = [9, 13, 17][n] + half
                act.wait_ge(s_full, u + 1)
                if n == 0:
                    act.wait_ge([s_var_ps, s_cn][half], 1)
                else:
                    act.wait_ge(s_free[(u - 2) % 2], (u - 2) // 2 + 1)
                for c in range(CB):
                    last = nc.scalar.activation(gate[half][:, c, :], unit(u)[:, c * S2:(c + 1) * S2], ACT.Sigmoid,
                                                bias=vecT[:, BG + 8 * b + 4 * half + c:BG + 8 * b + 4 * half + c + 1])
                last.then_inc(s_free[u % 2], 1)

            def hgrn_oT():
                act.wait_ge(s_hoT_ps, 1)
                nc.scalar.activation(h_oT, bank(6, 2).rearrange("p (c t) -> p c t", c=CB), ACT.Copy,
                                     scale=vecT[:, HNG:HNG + 1]).then_inc(s_hoT, 1)

            def exponentials(g):
                act.wait_ge(s_amax, g + 1)
                for h in range(4):
                    for a in range(TT):
                        w = slice(0, P) if a == 0 else slice(P, 3 * P)
                        nc.scalar.activation(Pm[:, h, w], Pm[:, h, w], ACT.Exp, scale=SCALE,
                                             bias=col(A_BIAS, 2 * h + a),
                                             accum_out=col(A_SUM, 8 * g + 2 * h + a))\
                            .then_inc(s_aexp, 1)

            def probabilities_T(g):
                act.wait_ge(s_PT_ps, g + 1)
                if g:
                    act.wait_ge(s_ao_ps, g)
                nc.scalar.activation(PT, ps[:, 4:8, 0:384], ACT.Copy).then_inc(s_PT, 1)

            gates(2, 0, 0)
            conv_out()
            gates(2, 0, 1)
            hgrn_oT()
            exponentials(0)
            gates(1, 1, 0)
            probabilities_T(0)
            gates(1, 1, 1)
            exponentials(1)
            probabilities_T(1)
            gates(0, 2, 0)
            act.wait_ge(s_aoT_ps, 1)
            nc.scalar.activation(a_oT, bank(6, 2).rearrange("p (c t) -> p c t", c=CB), ACT.Copy).then_inc(s_aoT, 1)
            gates(0, 2, 1)

            warm(ACT.Sqrt, 0)
            for a in range(TT):
                for half in range(2):
                    act.wait_ge(s_x2, 2 * a + half + 1)
                    nc.scalar.activation(at(14.5 + a + half / 2, W), xs[:, a, half * W:(half + 1) * W], ACT.Square,
                                         accum_out=col(X2_SSQ, 2 * a + half)).then_inc(s_ssq2, 1)
                act.wait_ge(s_ms2, a + 1)
                nc.scalar.activation(col(X2_ROOT, a), col(X2_MS, a), ACT.Sqrt).then_inc(s_root2, 1)
            warm(ACT.Exp, 1)
            for a in range(TT):
                act.wait_ge(s_rneg, 2 * a + 1)
                nc.scalar.activation(r_e4[:, a, :], r_e4[:, a, :], ACT.Exp, bias=r_neg[:, a:a + 1],
                                     accum_out=r_sum[:, a:a + 1]).then_inc(s_rexp, 1)
                act.wait_ge(s_rneg, 2 * a + 2)
                nc.scalar.activation(r_exp[:, a:a + 1], r_top2[:, a:a + 1], ACT.Exp, bias=r_neg1[:, a:a + 1])\
                    .then_inc(s_rexp, 1)
            warm(ACT.Silu, 2)
            act.wait_ge(s_few, 1)
            n_most = act.value_load(few[0:1, 0:1], min_val=0, max_val=SEQ)
            with act.If(n_most <= CAP):
                with nc.Fori(0, E // 2, 1, engines=[act.engine]) as q:
                    for j in range(2):
                        act.wait_ge(s_in_used[1], q * 2 + (j + 1))
                        nc.scalar.activation(e_sil[:, j, :], bank(6 + j)[:, 0:FH], ACT.Silu).then_inc(s_sil, 1)
                        if j == 0:
                            act.wait_ge(s_GwT_ps, q + 1)
                            nc.scalar.activation(wplaceT, bank(4)[:, 0:S2], ACT.Copy).then_inc(s_GwT, 1)
                        act.wait_ge(s_T_ps, q * 2 + (j + 1))
                        nc.scalar.activation(e_actT[:, 2 * j:2 * j + 2, :],
                                             bank(6 + j)[:, 0:FH].rearrange("p (f t) -> p f t", f=2), ACT.Copy)\
                            .then_inc(s_T, 1)
                        act.wait_ge(s_out_used, q * 2 + (j + 1))
                        nc.scalar.activation(y_sb[j * CAP:(j + 1) * CAP, 512:1024], bank(6 + j)[CAP:2 * CAP, :], ACT.Copy)\
                            .then_inc(s_Ya, 1)
                for a in range(TT):
                    act.wait_ge(s_scat, SCATTERS + 2 * a + 2)
                    nc.scalar.activation(xs[:, a, 512:1024], result(a)[:, 512:1024], ACT.Copy).then_inc(s_final[a][1], 1)
            with act.Else():
                with nc.Fori(0, E, 1, engines=[act.engine]) as e:
                    for a in range(TT):
                        if a == 0:
                            act.wait_ge(s_H0_ps, e + 1)
                        else:
                            act.wait_ge(s_in_used[1], e + 1)
                        nc.scalar.activation(e_sil, ps[:, 0:2, 0:FH], ACT.Silu).then_inc(s_sil, 1)
                        act.wait_ge(s_T_ps, e * TT + (a + 1))
                        nc.scalar.activation(e_actT.rearrange("p f t -> p (f t)"), bank(2), ACT.Copy).then_inc(s_T, 1)

        @block.vector
        def _(dve):
            v = nc.vector
            ch = Chain(dve, s_dve)
            s = ch.step

            def unit(u):
                return bank(2 * (u % 2), 2)

            dve.wait_ge(s_pool, 4)
            v.tensor_tensor(idx_x, idx_s, idx_t, ALU.bitwise_xor).then_inc(s_masks, 1)
            def scale_rows(to, a, rstd, done):
                for half in range(2):
                    c = slice(half * D // 2, (half + 1) * D // 2)
                    v.tensor_scalar(to[:, a, c], xs[:, a, c], rstd, None, ALU.mult).then_inc(done, 1)

            for a in range(TT):
                dve.wait_ge(s_ssq, a + 1)
                v.tensor_scalar(col(X_MS, a), col(X_SSQ, a), 1.0 / D, RMS_EPS, ALU.mult, ALU.add).then_inc(s_ms, 1)
            for a in range(TT):
                dve.wait_ge(s_root, a + 1)
                s(v.reciprocal(col(X_RSTD, a), col(X_ROOT, a)))
                ch.settle()
                scale_rows(h_tok, a, col(X_RSTD, a), s_h)
            dve.wait_ge(s_vec_ps, 1)
            v.tensor_copy(vecT[:, MIXG:MIXG + 8], bank(0)[:, 0:8]).then_inc(s_vec, 1)
            dve.wait_ge(s_vec, 1)

            def take_turned(a, gain, turned, done):
                for half in range(2):
                    k = slice(4 * half, 4 * half + 4)
                    dve.wait_ge(turned, 2 * a + half + 1)
                    v.tensor_tensor(hT[:, k, a * P:(a + 1) * P], bank(4 + 2 * a + half).rearrange("p (k t) -> p k t", t=P),
                                    vecT[:, gain + 4 * half:gain + 4 * half + 4].unsqueeze(2).broadcast_to([P, 4, P]),
                                    ALU.mult).then_inc(done, 1)

            for a in range(TT):
                take_turned(a, MIXG, s_hT_ps, s_hT)
            dve.wait_ge(s_const, 6)
            for i in range(8):
                s(v.tensor_scalar(level_mask[:, i, :], idx_x, float(P >> i), None, ALU.is_lt))
            dve.wait_ge(s_vec_ps, 2)
            v.tensor_copy(vecT[:, 8:NVEC], bank(7)[:, 8:NVEC]).then_inc(s_vec, 1)
            v.tensor_copy(tapT[:], bank(7)[:, P:P + TAPS * CB]).then_inc(s_vec, 1)
            dve.wait_ge(s_vec, 3)
            lbt = vecT[:, LB:LB + HH]
            v.tensor_tensor(col(LB_SHIFT, 0, 4), lbt, lbt, ALU.subtract).then_inc(s_lb0, 1)
            dve.wait_ge(s_lb1, 1)
            s(v.reciprocal(col(LB_INV, 0, 4), col(LB_EXP, 0, 4)))
            ch.settle()
            s(v.tensor_tensor(col(LBOUND, 0, 4), col(LB_EXP, 0, 4), col(LB_INV, 0, 4), ALU.mult))
            ch.settle()
            s(v.tensor_tensor(col(LBOUND, 0, 4), col(LBOUND, 0, 4), col(LBOUND, 0, 4), ALU.subtract))
            ch.settle()
            s(v.tensor_scalar(col(LBOUND, 0, 4), col(LBOUND, 0, 4), 0.0, None, ALU.max))
            ch.settle()
            s(v.tensor_scalar(col(ONE_LB, 0, 4), col(LBOUND, 0, 4), -1.0, 1.0, ALU.mult, ALU.add))
            s(v.tensor_scalar(col(LB_ONE, 0, 4), col(LBOUND, 0, 4), 1.0, -1.0, ALU.mult, ALU.add))
            ch.settle()
            dve.wait_ge(s_free[0], 1)
            for h in range(HH):
                s(v.tensor_scalar(hk[:, h, :], hf[:, h, :], col(LB_ONE, h),
                                  col(ONE_LB, h), ALU.mult, ALU.add))
            ch.settle()
            for h in range(HH):
                s(v.tensor_scalar(hf[:, h, :], hf[:, h, :], col(ONE_LB, h),
                                  col(LBOUND, h), ALU.mult, ALU.add))
            ch.settle()
            v.tensor_scalar(hf, hf, LEAST_FORGET, None, ALU.max).then_inc(s_f, 1)
            dve.wait_ge(s_lf, 1)
            for h in range(HH):
                s(v.tensor_tensor_scan(hb[:, h, :], chunk_keep[:], hf[:, h, :], 0.0, ALU.mult, ALU.add))
            ch.settle()

            def halves(t, m):
                return t.rearrange("p c t -> p (c t)").rearrange("p (b a m) -> p b a m", a=2, m=m)

            def exponents(i):
                m = P >> i
                if i >= 2:
                    dve.wait_ge(s_K, 2 if i == 2 else i + 1)
                    dve.wait_ge(s_Q, i - 1)
                D = Ex[i % 2]
                dv, bv = halves(D, m), halves(hb, m)
                if m <= CHUNK:
                    nb = HH * S2 // (2 * m)
                    ref = bv[:, :, 0, m - 1:m].broadcast_to([P, nb, m])
                    if m < CHUNK:
                        v.tensor_tensor(dv[:, :, 1, :], bv[:, :, 1, :], ref, ALU.subtract)
                    else:
                        v.tensor_copy(dv[:, :, 1, :], bv[:, :, 1, :])
                    v.tensor_tensor(dv[:, :, 0, :], ref, bv[:, :, 0, :], ALU.subtract).then_inc(s_D, 1)
                else:
                    dc = D.rearrange("p h (c t) -> p h c t", t=CHUNK)
                    bc = hb.rearrange("p h (c t) -> p h c t", t=CHUNK)

                    def end(c):
                        return bc[:, :, c, CHUNK - 1:CHUNK].broadcast_to([P, HH, CHUNK])
                    s(v.tensor_tensor(dc[:, :, 0, :], end(0), bc[:, :, 0, :], ALU.subtract))
                    v.tensor_tensor(dc[:, :, 1, :], end(1), bc[:, :, 1, :], ALU.subtract)
                    v.tensor_copy(dc[:, :, 2, :], bc[:, :, 2, :])
                    v.tensor_tensor(dc[:, :, 3, :], bc[:, :, 3, :], end(2), ALU.add)
                    ch.settle()
                    v.tensor_tensor(dc[:, :, 0, :], dc[:, :, 0, :], end(1), ALU.add).then_inc(s_D, 1)

            def queries(i):
                m = P >> i
                dve.wait_ge(s_E, i + 1)
                if i == 0:
                    dve.wait_ge(s_free[1], 1)
                if i >= 2:
                    dve.wait_ge(s_SC, i - 1)
                ov, qv, ev = halves(Qx[i % 2], m), halves(hq, m), halves(Ex[i % 2], m)
                if i < 2:
                    s(v.memset(ov[:, :, 0, :], 0.0))
                    ch.settle()
                v.tensor_tensor(ov[:, :, 1, :], qv[:, :, 1, :], ev[:, :, 1, :], ALU.mult).then_inc(s_Q, 1)

            def take(i):
                b = 4 + 2 * (i % 2)
                dve.wait_ge(s_SC, i + 1)
                if i == 0:
                    v.tensor_copy(ST[:, 2, :, :], bank(b).rearrange("p (h t) -> p h t", h=HH)).then_inc(s_SCfree, 1)
                else:
                    if i == 1:
                        s(v.memset(ST[:, 0:2, :, :], 0.0))
                        ch.settle()
                    else:
                        dve.wait_ge(s_SCfree, i)
                    mask = level_mask[:, i - 1, :].unsqueeze(1).broadcast_to([P, 2 * HH, P])
                    v.copy_predicated(ST[:, 0:2, :, :].rearrange("p a h t -> p (a h) t"), mask,
                                      bank(b, 2).rearrange("p (g t) -> p g t", t=P)).then_inc(s_SCfree, 1)

            exponents(0)
            for i in range(8):
                if i + 1 < 8:
                    exponents(i + 1)
                queries(i)
                if i:
                    take(i - 1)
            take(7)
            take(8)
            dve.wait_ge(s_free[1], 2)
            dve.wait_ge(s_full, 5)
            v.tensor_tensor(c_u[:, :, PAD:PAD + S2], unit(4).rearrange("p (c t) -> p c t", c=CB), c_sig, ALU.mult)\
                .then_inc(s_free[0], 1)
            dve.wait_ge(s_free[0], 3)
            for c in range(CB):
                v.tensor_scalar(c_acc[:, c, :], c_u[:, c, 0:S2], tapT[:, c:c + 1], vecT[:, CVB + c:CVB + c + 1],
                                ALU.mult, ALU.add).then_inc(s_taps, 1)
            with nc.Fori(1, TAPS, 1, engines=[dve.engine]) as j:
                for c in range(CB):
                    dve.wait_ge(s_taps, j * CB + (c + 1 - CB))
                    v.scalar_tensor_tensor(out=c_acc[:, c, :], in0=c_u[:, c, bass.ds(j, S2)],
                                           scalar=tapT[:, bass.ds(j * CB + c, 1)], in1=c_acc[:, c, :],
                                           op0=ALU.mult, op1=ALU.add).then_inc(s_taps, 1)
            dve.wait_ge(s_hosq, 1)
            s(v.tensor_reduce(col(HO_MS, 0, 8), h_sq.rearrange("p a (h w) -> p (a h) w", w=P), AX_X, ALU.add))
            ch.settle()
            v.tensor_scalar(col(HO_MS, 0, 8), col(HO_MS, 0, 8), 1.0 / P, RMS_EPS, ALU.mult, ALU.add).then_inc(s_hms, 1)
            dve.wait_ge(s_mean_ps, 1)
            mean = bank(6)[:, 0:S2]
            v.scalar_tensor_tensor(out=c_acc, in0=mean.unsqueeze(1).broadcast_to([P, CB, S2]), scalar=-1.0 / W,
                                   in1=c_acc, op0=ALU.mult, op1=ALU.add).then_inc(s_cdev, 1)
            for j in range(2):
                dve.wait_ge(s_asq, j + 1)
                s(v.tensor_reduce(col(QK_MS, 16 * j, 16), (q_sq, k_sq)[j].rearrange("p a (h w) -> p (a h) w", w=HD),
                                  AX_X, ALU.add))
                ch.settle()
                v.tensor_scalar(col(QK_MS, 16 * j, 16), col(QK_MS, 16 * j, 16), 1.0 / HD, RMS_EPS,
                                ALU.mult, ALU.add).then_inc(s_ams, 1)
            dve.wait_ge(s_hroot, 1)
            s(v.reciprocal(col(HO_RSTD, 0, 8), col(HO_ROOT, 0, 8)))
            ch.settle()
            s(v.tensor_tensor(h_o.rearrange("p a (h w) -> p (a h) w", w=P),
                              bank(4, 2).rearrange("p (g w) -> p g w", w=P),
                              col(HO_RSTD, 0, 8).unsqueeze(2).broadcast_to([P, TT * HH, P]), ALU.mult))
            ch.settle()
            dve.wait_ge(s_free[1], 3)
            v.tensor_tensor(h_o, h_o, hg, ALU.mult).then_inc(s_hon, 1)
            dve.wait_ge(s_aroot, 1)
            s(v.reciprocal(col(QK_RSTD, 0, 32), col(QK_RSTD, 0, 32)))
            ch.settle()
            for j, buf in enumerate((aq, ak)):
                b = buf.rearrange("p a (h w) -> p (a h) w", w=HD)
                v.tensor_tensor(b, b, col(QK_RSTD, 16 * j, 16).unsqueeze(2).broadcast_to([P, TT * AH, HD]),
                                ALU.mult).then_inc(s_an, 1)
            dve.wait_ge(s_var_ps, 1)
            root = c_u[:, 0, 0:S2]
            v.tensor_scalar(root, bank(6)[:, 0:S2], 1.0 / W, LN_EPS, ALU.mult, ALU.add).then_inc(s_cvar, 1)
            dve.wait_ge(s_croot, 1)
            s(v.reciprocal(c_u[:, 1, 0:S2], root))
            ch.settle()
            v.tensor_tensor(c_acc, c_acc, c_u[:, 1:2, 0:S2].broadcast_to([P, CB, S2]), ALU.mult).then_inc(s_cn, 1)

            def take_qk(j, buf, g):
                dve.wait_ge(s_qkT_ps, j + 1)
                v.tensor_scalar(buf, bank(4 + 2 * j, 2).rearrange("p (c t) -> p c t", c=CB), vecT[:, g:g + 1], None,
                                ALU.mult).then_inc(s_qkT, 1)

            def merge(n, half):
                u = [11, 15, 19][n] + half
                dve.wait_ge(s_full, u + 1)
                dve.wait_ge(s_free[(u - 2) % 2], (u - 2) // 2 + 1)
                y = unit(u).rearrange("p (c t) -> p c t", c=CB)
                m = merged[:, 4 * half:4 * half + 4, :]
                if n:
                    dve.wait_ge(s_gate_used, 2 * (n - 1) + half)
                v.tensor_tensor(prod if n else m, gate[half], y, ALU.mult).then_inc(s_free[u % 2], 1)
                dve.wait_ge(s_free[u % 2], u // 2 + 1)
                if n:
                    v.tensor_tensor(m, m, prod, ALU.add).then_inc(s_gate_used, 1)

            take_qk(0, qT, QG)
            merge(0, 0)
            take_qk(1, kT, KG)
            merge(0, 1)
            def masked_max(g):
                dve.wait_ge(s_asc_ps, g + 1)
                if g:
                    dve.wait_ge(s_PT_ps, 1)
                s(v.tensor_tensor(Pm, ps[:, 4:8, 0:384],
                                  causal[:].rearrange("p a s -> p (a s)").unsqueeze(1).broadcast_to([P, 4, 384]), ALU.add))
                ch.settle()
                mx = col(A_MAX, 0, 8).rearrange("p (h a) -> p h a", a=TT)
                s(v.tensor_reduce(mx[:, :, 0], Pm[:, :, 0:P], AX_X, ALU.max))
                s(v.tensor_reduce(mx[:, :, 1], Pm[:, :, P:3 * P], AX_X, ALU.max))
                ch.settle()
                v.tensor_scalar(col(A_BIAS, 0, 8), col(A_MAX, 0, 8), -SCALE, None, ALU.mult).then_inc(s_amax, 1)

            def attended(g):
                dve.wait_ge(s_aexp, 8 * (g + 1))
                s(v.reciprocal(col(A_INV, 8 * g, 8), col(A_SUM, 8 * g, 8)))
                ch.settle()
                dve.wait_ge(s_ao_ps, g + 1)
                r = col(A_INV, 8 * g, 8).rearrange("p (h a) -> p h a", a=TT)
                for a in range(TT):
                    v.tensor_tensor(a_o[:, a, 256 * g:256 * g + 256].rearrange("p (h w) -> p h w", w=HD),
                                    bank(4 + a)[:, 0:256].rearrange("p (h w) -> p h w", w=HD),
                                    r[:, :, a:a + 1].broadcast_to([P, 4, HD]), ALU.mult).then_inc(s_ao, 1)

            masked_max(0)
            attended(0)
            masked_max(1)
            merge(1, 0)
            merge(1, 1)
            attended(1)
            merge(2, 0)
            merge(2, 1)

            def residual(a, half):
                c = slice(half * W, (half + 1) * W)
                dve.wait_ge(s_full, 22 + 2 * a + half)
                v.tensor_tensor(xs[:, a, c], xs[:, a, c], result(a)[:, c], ALU.add).then_inc(s_x2, 1)

            def norm2(a):
                dve.wait_ge(s_ssq2, 2 * a + 1)
                s(v.tensor_scalar(col(X2_PART, a), col(X2_SSQ, 2 * a), 1.0 / D, RMS_EPS, ALU.mult, ALU.add))
                ch.settle()
                dve.wait_ge(s_ssq2, 2 * a + 2)
                v.scalar_tensor_tensor(out=col(X2_MS, a), in0=col(X2_SSQ, 2 * a + 1), scalar=1.0 / D,
                                       in1=col(X2_PART, a), op0=ALU.mult, op1=ALU.add).then_inc(s_ms2, 1)
                dve.wait_ge(s_root2, a + 1)
                s(v.reciprocal(col(X2_RSTD, a), col(X2_ROOT, a)))
                ch.settle()
                scale_rows(h2, a, col(X2_RSTD, a), s_h2)

            def t2(o, a, s1, s2, op0, op1=None):
                s(v.tensor_scalar(o, a, s1, s2, op0, op1) if op1 is not None else v.tensor_scalar(o, a, s1, None, op0))
                ch.settle()

            def t3(o, a, scalar, b, op0, op1):
                s(v.scalar_tensor_tensor(out=o, in0=a, scalar=scalar, in1=b, op0=op0, op1=op1))
                ch.settle()

            def red(o, a, op):
                s(v.tensor_reduce(o, a, AX_X, op))
                ch.settle()

            def choose(a):
                def of(t):
                    return t[:, a, :] if len(t.shape) == 3 else t[:, a:a + 1]
                lc, lf = router_ps(a)[:, 0:G], router_ps(a)[:, G:NL]
                dve.wait_ge(s_log_ps, a + 1)
                red(of(r_max), lc, ALU.max)
                v.tensor_copy(of(r_e4), lc)
                v.tensor_scalar(of(r_neg), of(r_max), -1.0, None, ALU.mult).then_inc(s_rneg, 1)
                t3(of(r_t4), lc, of(r_max), r_i4, ALU.is_equal, ALU.mult)
                red(of(r_first4), of(r_t4), ALU.min)
                t2(of(r_gm), r_i4, of(r_first4), -1.0, ALU.is_equal, ALU.add)
                t3(of(r_fine).rearrange("p (g e) -> p g e", g=G), of(r_gm).unsqueeze(2).broadcast_to([P, G, EG]), -NEG,
                   lf.rearrange("p (g e) -> p g e", g=G), ALU.mult, ALU.add)
                red(of(r_top1), of(r_fine), ALU.max)
                s(v.tensor_scalar(of(r_neg1), of(r_top1), -1.0, None, ALU.mult))
                t3(of(r_tmp), of(r_fine), of(r_top1), r_iota, ALU.is_equal, ALU.mult)
                red(of(r_first1), of(r_tmp), ALU.min)
                t2(of(r_oh1), r_iota, of(r_first1), None, ALU.is_equal)
                t3(of(r_fine2), of(r_oh1), 2 * NEG, of(r_fine), ALU.mult, ALU.add)
                s(v.tensor_reduce(of(r_top2), of(r_fine2), AX_X, ALU.max))
                ch.settle()
                t3(of(r_tmp), of(r_fine2), of(r_top2), r_iota, ALU.is_equal, ALU.mult)
                red(of(r_first2), of(r_tmp), ALU.min)
                v.scalar_tensor_tensor(out=of(sel), in0=r_iota, scalar=of(r_first2), in1=of(r_oh1), op0=ALU.is_equal,
                                       op1=ALU.add).then_inc(s_sel, 1)
                v.tensor_scalar(of(r_oh2), r_iota, of(r_first2), None, ALU.is_equal).then_inc(s_rneg, 1)

            def place_pair(q):
                p4 = place.rearrange("p a (j c) -> p a j c", j=2)
                for a in range(TT):
                    last = v.tensor_tensor(
                        p4[:, a], place_no[:].unsqueeze(1).broadcast_to([P, 2, CAP]),
                        rank_q[:, a, bass.ds(q, 1), :].rearrange("p q j -> p (q j)").unsqueeze(2)
                        .broadcast_to([P, 2, CAP]), ALU.is_equal)
                last.then_inc(s_placed, 1)

            def weigh_pair(q):
                p4 = place.rearrange("p a (j c) -> p a j c", j=2)
                w4 = wplace.rearrange("p a (j c) -> p a j c", j=2)
                dve.wait_ge(s_placed, q + 1)
                for a in range(TT):
                    last = v.tensor_tensor(
                        w4[:, a], p4[:, a],
                        weight_q[:, a, bass.ds(q, 1), :].rearrange("p q j -> p (q j)").unsqueeze(2)
                        .broadcast_to([P, 2, CAP]), ALU.mult)
                last.then_inc(s_G, 1)

            residual(0, 0)
            residual(0, 1)
            norm2(0)
            for j in range(E):
                s(v.memset(r_iota[:, j:j + 1], j - BIG))
            for j in range(G):
                s(v.memset(r_i4[:, j:j + 1], j - BIG))
            residual(1, 0)
            take_turned(0, FFNG, s_h2T_ps, s_h2T)
            choose(0)
            residual(1, 1)
            norm2(1)
            take_turned(1, FFNG, s_h2T_ps, s_h2T)
            choose(1)
            dve.wait_ge(s_count_ps, 1)
            red(most, count_ps, ALU.max)
            v.tensor_copy(few[0:1, :], most[0:1, :]).then_inc(s_few, 1)
            dve.wait_ge(s_rank_ps, 1)
            for a in range(TT):
                s(v.scalar_tensor_tensor(out=rank[:, a, :], in0=rank_ps(a), scalar=1.0, in1=sel[:, a, :], op0=ALU.add,
                                         op1=ALU.mult))
            ch.settle()
            place_pair(0)
            dve.wait_ge(s_rexp, 2 * TT)
            t2(r_w1, r_exp, 1.0, None, ALU.add)
            s(v.tensor_tensor(r_den, r_w1, r_sum, ALU.mult))
            ch.settle()
            s(v.reciprocal(r_w1, r_den))
            ch.settle()
            s(v.tensor_tensor(r_w2, r_w1, r_exp, ALU.mult))
            ch.settle()
            for a in range(TT):
                s(v.tensor_scalar(r_oh1[:, a, :], r_oh1[:, a, :], r_w1[:, a:a + 1], None, ALU.mult))
            ch.settle()
            for a in range(TT):
                last = v.scalar_tensor_tensor(out=weight[:, a, :], in0=r_oh2[:, a, :], scalar=r_w2[:, a:a + 1],
                                              in1=r_oh1[:, a, :], op0=ALU.mult, op1=ALU.add)
                s(last)
            ch.settle()
            weigh_pair(0)
            n_most = dve.value_load(few[0:1, 0:1], min_val=0, max_val=SEQ)
            with dve.If(n_most <= CAP):
                def gathered(q):
                    for half in range(2):
                        k = slice(4 * half, 4 * half + 4)
                        dve.wait_ge(s_gather, q * 2 + (half + 1))
                        gain = vecT[:, FFNG + 4 * half:FFNG + 4 * half + 4].unsqueeze(2).broadcast_to([P, 4, 2 * CAP])
                        v.tensor_tensor(xg[:, k, :], bank(4 + half).rearrange("p (k c) -> p k c", c=2 * CAP), gain,
                                        ALU.mult).then_inc(s_xg, 1)

                gathered(0)
                def pair(q, last=False):
                    for j in range(2):
                        dve.wait_ge(s_sil, q * 2 + (j + 1))
                        v.tensor_tensor(e_act[:, j, :], e_sil[:, j, :], bank(6 + j)[:, FH:2 * FH], ALU.mult)\
                            .then_inc(s_act2, 1)
                        if j == 0 and not last:
                            dve.wait_ge(s_GwT_ps, q + 1)
                            place_pair(q + 1)
                            weigh_pair(q + 1)
                        elif not last:
                            gathered(q + 1)
                        dve.wait_ge(s_out_used, q * 2 + (j + 1))
                        v.tensor_copy(y_sb[j * CAP:(j + 1) * CAP, 0:512], bank(6 + j)[0:CAP, :]).then_inc(s_Yv, 1)

                with nc.Fori(0, E // 2 - 1, 1, engines=[dve.engine]) as q:
                    pair(q)
                pair(E // 2 - 1, last=True)
                for a in range(TT):
                    dve.wait_ge(s_scat, SCATTERS + 2 * a + 1)
                    v.tensor_copy(xs[:, a, 0:512], result(a)[:, 0:512]).then_inc(s_final[a][0], 1)
            with dve.Else():
                with nc.Fori(0, E, 1, engines=[dve.engine]) as e:
                    for a in range(TT):
                        dve.wait_ge(s_sil, e * TT + (a + 1))
                        v.tensor_tensor(e_act, e_sil, ps[:, 0:2, FH:2 * FH], ALU.mult).then_inc(s_act2, 1)
                        if a == 0:
                            dve.wait_ge(s_Y0_ps, e + 1)
                        else:
                            dve.wait_ge(s_out_used, e + 1)
                        v.scalar_tensor_tensor(out=xs[:, a, :], in0=bank(4, 2), scalar=weight[:, a, bass.ds(e, 1)],
                                               in1=xs[:, a, :], op0=ALU.mult, op1=ALU.add).then_inc(s_Yfree, 1)
                        dve.wait_ge(s_Yfree, e * TT + (a + 1))
                for a in range(TT):
                    for c in range(2):
                        v.tensor_copy(e_sil[:, a, c:c + 1], xs[:, a, 512 * c:512 * c + 1]).then_inc(s_final[a][c], 1)

        @block.tensor
        def _(pe):
            mm, tr = nc.tensor.matmul, nc.tensor.transpose
            pe.wait_ge(s_const, 1)

            def keep_busy(n, b):
                for _ in range(n):
                    mm(bank(b)[:, 3 * P:4 * P], ones[:], ones[:], start=True, stop=True)

            keep_busy(8, 3)
            pe.wait_ge(s_gain, 16)
            tr(bank(0)[:, 0:8], vec_rows[MIXG:MIXG + 8, :], ident[0:8, 0:8]).then_inc(s_vec_ps, 1)

            def turn(a, src, ready, done):
                for k in range(KD):
                    if k % 4 == 0:
                        pe.wait_ge(ready, 2 * a + k // 4 + 1)
                    last = tr(bank(4 + 2 * a + k // 4)[:, (k % 4) * P:(k % 4 + 1) * P], src[:, a, k * P:(k + 1) * P],
                              ident[:])
                    if k % 4 == 3:
                        last.then_inc(done, 1)

            keep_busy(5, 3)
            for a in range(TT):
                turn(a, h_tok, s_h, s_hT_ps)
            pe.wait_ge(s_hT, 2 * TT)

            def begin(u):
                if u == 0:
                    pe.wait_ge(s_vec, 1)
                if u >= 2:
                    pe.wait_ge(s_free[u % 2], u // 2)
                return bank(2 * (u % 2), 2)

            def cols_by_tokens(u, l, halves=(0, 1)):
                if 0 in halves:
                    begin(u)
                o, w = bank(2 * (u % 2), 2), wcols(l)
                for half in halves:
                    if l == 0 and half == 0:
                        pe.wait_ge(s_first, 16)
                    else:
                        wait_landed(pe, l)
                    for c in (2 * half, 2 * half + 1):
                        for k in range(KD):
                            last = mm(o[:, c * S2:(c + 1) * S2], w[:, k, c * P:(c + 1) * P], hT[:, k, :],
                                      start=k == 0, stop=k == KD - 1)
                if 1 in halves:
                    last.then_inc(s_full, 1)

            def tokens_by_cols(u, l, halves=(0, 1)):
                if 0 in halves:
                    begin(u)
                o, w = bank(2 * (u % 2), 2), wcols(l)
                wait_landed(pe, l)
                for a in halves:
                    for k in range(KD):
                        last = mm(o[:, a * W:(a + 1) * W], hT[:, k, a * P:(a + 1) * P], w[:, k, :],
                                  start=k == 0, stop=k == KD - 1)
                if 1 in halves:
                    last.then_inc(s_full, 1)

            def branch(u, half, l, oT):
                w = wrows(l)
                wait_landed(pe, l)
                o = begin(u)
                for c in range(CB):
                    for k in range(CB):
                        last = mm(o[:, c * S2:(c + 1) * S2], w[:, k, half * W + c * P:half * W + (c + 1) * P],
                                  oT[:, k, :], start=k == 0, stop=k == CB - 1)
                last.then_inc(s_full, 1)

            def level(i):
                if i < 8:
                    q, k = Qx[i % 2], Kx[i % 2]
                    pe.wait_ge(s_Q, i + 1)
                    pe.wait_ge(s_K, i + (2 if i == 0 else 3))
                else:
                    q, k = hq, hk
                if i >= 2:
                    pe.wait_ge(s_SCfree, i - 1)
                b = 4 + 2 * (i % 2)
                for h in range(HH):
                    if i == 0:
                        last = mm(bank(b)[:, h * P:(h + 1) * P], k[:, h, 0:P], q[:, h, P:2 * P], start=True, stop=True)
                    else:
                        for a in range(TT):
                            last = mm(bank(b + a)[:, h * P:(h + 1) * P], k[:, h, a * P:(a + 1) * P],
                                      q[:, h, a * P:(a + 1) * P], start=True, stop=True)
                last.then_inc(s_SC, 1)

            cols_by_tokens(0, 0, (0,))
            pe.wait_ge(s_small, 16 * N_SMALL)
            tr(bank(7)[:, 0:NVEC], vec_rows[0:NVEC, :], ident[0:NVEC, 0:NVEC])
            n = TAPS * CB
            tr(bank(7)[:, P:P + n], tap_rows[0:n, :], ident[0:n, 0:n]).then_inc(s_vec_ps, 1)
            cols_by_tokens(0, 0, (1,))
            cols_by_tokens(1, 1)
            tokens_by_cols(2, 2, (0,))
            level(0)
            tokens_by_cols(2, 2, (1,))
            level(1)
            level(2)
            cols_by_tokens(3, 3, (0,))
            level(3)
            level(4)
            cols_by_tokens(3, 3, (1,))
            level(5)
            level(6)
            cols_by_tokens(4, 4, (0,))
            level(7)
            level(8)
            cols_by_tokens(4, 4, (1,))
            pe.wait_ge(s_SCfree, 9)
            for h in range(HH):
                w = slice(h * P, (h + 1) * P)
                mm(bank(4)[:, w], ST[:, 0, h, :], hv[:, 0, w], start=True, stop=True)
                mm(bank(5)[:, w], ST[:, 2, h, :], hv[:, 0, w], start=True, stop=False)
                last = mm(bank(5)[:, w], ST[:, 1, h, :], hv[:, 1, w], start=False, stop=True)
            last.then_inc(s_ho_ps, 1)
            for u in (5, 6, 7, 8):
                tokens_by_cols(u, u)

            def over_channels(x, done):
                for c in range(CB):
                    last = mm(bank(6)[:, 0:S2], ones[:], x[:, c, :], start=c == 0, stop=c == CB - 1)
                last.then_inc(done, 1)

            cols_by_tokens(9, 9, (0,))
            pe.wait_ge(s_taps, TAPS * CB)
            over_channels(c_acc, s_mean_ps)
            cols_by_tokens(9, 9, (1,))
            pe.wait_ge(s_csq, 1)
            over_channels(c_sig, s_var_ps)

            def turn4(src, b, done):
                for c in range(CB):
                    for a in range(TT):
                        last = tr(bank(b, 2)[:, c * S2 + a * P:c * S2 + (a + 1) * P], src[:, a, c * P:(c + 1) * P], ident[:])
                last.then_inc(done, 1)

            cols_by_tokens(10, 10)
            pe.wait_ge(s_hon, 1)
            pe.wait_ge(s_cvar, 1)
            turn4(h_o, 6, s_hoT_ps)
            pe.wait_ge(s_an, 1)
            turn4(aq, 4, s_qkT_ps)
            pe.wait_ge(s_convT, CB)
            branch(11, 0, 11, c_acc)
            pe.wait_ge(s_an, 2)
            pe.wait_ge(s_hoT, 1)
            turn4(ak, 6, s_qkT_ps)
            branch(12, 1, 11, c_acc)
            pe.wait_ge(s_qkT, 2)

            def scores(g):
                if g:
                    pe.wait_ge(s_ao, TT)
                for j in range(4):
                    h = 4 * g + j
                    r = slice(HD * (h % 2), HD * (h % 2) + HD)
                    mm(bank(4 + j)[:, 0:P], qT[r, h // 2, 0:P], kT[r, h // 2, 0:P], start=True, stop=True)
                    last = mm(bank(4 + j)[:, P:3 * P], qT[r, h // 2, P:2 * P], kT[r, h // 2, :], start=True, stop=True)
                last.then_inc(s_asc_ps, 1)

            def turn_p(g):
                pe.wait_ge(s_aexp, 8 * (g + 1))
                for j in range(4):
                    for b in range(3):
                        last = tr(bank(4 + j)[:, b * P:(b + 1) * P], Pm[:, j, b * P:(b + 1) * P], ident[:])
                last.then_inc(s_PT_ps, 1)

            def values(g):
                pe.wait_ge(s_PT, g + 1)
                for j in range(4):
                    h = 4 * g + j
                    w, o = slice(h * HD, (h + 1) * HD), slice(j * HD, (j + 1) * HD)
                    mm(bank(4)[:, o], PT[:, j, 0:P], av[:, 0, w], start=True, stop=True)
                    mm(bank(5)[:, o], PT[:, j, P:2 * P], av[:, 0, w], start=True, stop=False)
                    last = mm(bank(5)[:, o], PT[:, j, 2 * P:3 * P], av[:, 1, w], start=False, stop=True)
                last.then_inc(s_ao_ps, 1)

            scores(0)
            cols_by_tokens(13, 12)
            turn_p(0)
            cols_by_tokens(14, 13, (0,))
            values(0)
            cols_by_tokens(14, 13, (1,))
            scores(1)
            for half in range(2):
                branch(15 + half, half, 14, h_oT)
            turn_p(1)
            cols_by_tokens(17, 15, (0,))
            values(1)
            cols_by_tokens(17, 15, (1,))
            pe.wait_ge(s_ao, 2 * TT)
            turn4(a_o, 6, s_aoT_ps)
            cols_by_tokens(18, 16)
            pe.wait_ge(s_aoT, 1)
            for half in range(2):
                branch(19 + half, half, 17, a_oT)
            def w_out_part(a, half, ks):
                if ks[0] == 0 and half == 0:
                    begin(21 + a)
                wait_landed(pe, L_OUT + half)
                for k in ks:
                    if a == 0 and half == 0 and k % CB == 0:
                        pe.wait_ge(s_gate_used, 3 + k // CB)
                    last = mm(result(a)[:, half * W:(half + 1) * W], merged[:, k, a * P:(a + 1) * P],
                              wcols(L_OUT + half)[:, k, :], start=k == 0, stop=k == KD - 1)
                if ks[-1] == KD - 1:
                    last.then_inc(s_full, 1)

            def router_logits(a):
                pe.wait_ge(s_h2T, 2 * a + 2)
                for k in range(KD):
                    mm(router_ps(a), hT[:, k, a * P:(a + 1) * P], w_router[:, k, :], start=k == 0, stop=False)
                mm(router_ps(a), ones[0:1, :], b_router[0:1, :], start=False, stop=True).then_inc(s_log_ps, 1)

            def open_result(a):
                pe.wait_ge(s_x2, 2 * a + 2)
                for c in range(2):
                    last = mm(result(a)[:, c * 512:(c + 1) * 512], ident[:], xs[:, a, c * 512:(c + 1) * 512], start=True,
                              stop=False, skip_group_check=True)
                last.then_inc(s_scat, 1)

            w_out_part(0, 0, range(KD))
            w_out_part(0, 1, range(KD))
            w_out_part(1, 0, range(KD))
            turn(0, h2, s_h2, s_h2T_ps)
            w_out_part(1, 1, range(KD // 2))
            pe.wait_ge(s_router_w, 64)
            router_logits(0)
            w_out_part(1, 1, range(KD // 2, KD))
            pe.wait_ge(s_sel, 1)
            mm(rank_ps(0), before[:], sel[:, 0, :], start=True, stop=True)
            open_result(0)
            turn(1, h2, s_h2, s_h2T_ps)
            router_logits(1)
            open_result(1)
            mm(count_ps, ones[:], sel[:, 0, :], start=True, stop=False)
            pe.wait_ge(s_sel, 2)
            mm(count_ps, ones[:], sel[:, 1, :], start=False, stop=True).then_inc(s_count_ps, 1)
            mm(rank_ps(1), ones[:], sel[:, 0, :], start=True, stop=False)
            mm(rank_ps(1), before[:], sel[:, 1, :], start=False, stop=True).then_inc(s_rank_ps, 1)

            keep_busy(5, 6)

            def gather(q):
                pe.wait_ge(s_placed, q + 1)
                for k in range(KD):
                    o = bank(4, 2)[:, k * 2 * CAP:(k + 1) * 2 * CAP]
                    for a in range(TT):
                        last = mm(o, h2[:, a, k * P:(k + 1) * P], place[:, a, :], start=a == 0, stop=a == TT - 1)
                    if k % 4 == 3:
                        last.then_inc(s_gather, 1)

            gather(0)
            pe.wait_ge(s_few, 1)
            n_most = pe.value_load(few[0:1, 0:1], min_val=0, max_val=SEQ)

            def expert_landed(r, g, parts):
                for part in parts:
                    landed_part, before_first = expert_sem(g, part)
                    pe.wait_ge(landed_part, r * 16 + (before_first + 16))

            with pe.If(n_most <= CAP):
                def expert_in(q, r, g, j):
                    for k in range(KD):
                        if k % CB == 0:
                            expert_landed(r, g, (k // CB,))
                            if j == 0:
                                pe.wait_ge(s_xg, q * 2 + (k // CB + 1))
                        for f in range(2):
                            last = mm(ps[f * CAP:(f + 1) * CAP, 6 + j, :].rearrange("p (g n) -> p g n", g=2),
                                      xg[:, k, j * CAP:(j + 1) * CAP], expert_cols(g, k, f), start=k == 0, stop=k == KD - 1)
                        if k % CB == CB - 1:
                            last.then_inc(s_in_used[k // CB], 1)

                def expert_out(q, r, g, j):
                    pe.wait_ge(s_act2, q * 2 + (j + 1))
                    for b in range(2):
                        last = tr(bank(6 + j)[:, b * P:(b + 1) * P], e_act[:, j, b * P:(b + 1) * P], ident[:])
                    last.then_inc(s_T_ps, 1)
                    expert_landed(r, g, (2,))
                    pe.wait_ge(s_T, q * 2 + (j + 1))
                    for f in range(FT):
                        for c in range(2):
                            last = mm(bank(6 + j)[c * CAP:(c + 1) * CAP, :],
                                      e_actT[:, 2 * j + f % 2, (f // 2) * CAP:(f // 2 + 1) * CAP],
                                      expert_rows(g, 2)[:, f, c * 512:(c + 1) * 512], start=f == 0, stop=f == FT - 1)
                    last.then_inc(s_out_used, 1)

                def scatter(n_taken, final=False):
                    pe.wait_ge(s_Yv, n_taken)
                    pe.wait_ge(s_Ya, n_taken)
                    for a in range(TT):
                        for c in range(2):
                            last = mm(result(a)[:, c * 512:(c + 1) * 512], wplaceT[:, a * P:(a + 1) * P], y_sb[:, c * 512:(c + 1) * 512],
                                      start=False, stop=False, skip_group_check=True)
                            if final:
                                last.then_inc(s_scat, 1)
                    if not final:
                        last.then_inc(s_scat, 1)

                def pair(q, t, n, first=False, last=False):
                    experts = [(t * 2 + (n + j) // GROUPS, (n + j) % GROUPS) for j in range(2)]
                    if not first:
                        pe.wait_ge(s_Yv, q * 2 - 1)
                        pe.wait_ge(s_Ya, q * 2 - 1)
                    expert_in(q, *experts[0], 0)
                    if not first:
                        scatter(q * 2)
                    pe.wait_ge(s_G, q + 1)
                    for a in range(TT):
                        turned = tr(bank(4)[:, a * P:(a + 1) * P], wplace[:, a, :], ident[:])
                    turned.then_inc(s_GwT_ps, 1)
                    expert_out(q, *experts[0], 0)
                    expert_in(q, *experts[1], 1)
                    if not last:
                        pe.wait_ge(s_GwT, q + 1)
                        gather(q + 1)
                    expert_out(q, *experts[1], 1)

                pair(0, 0, 0, first=True)
                steps = (E // 2 - 2) // 3
                with nc.Fori(0, steps, 1, engines=[pe.engine]) as t:
                    for i in range(3):
                        pair(t * 3 + (i + 1), t, 2 * (i + 1))
                for q in range(3 * steps + 1, E // 2):
                    pair(q, 0, 2 * q, last=q == E // 2 - 1)
                scatter(E, final=True)
            with pe.Else():
                def dense(e, r, g):
                    expert_landed(r, g, range(EXP))
                    for a in range(TT):
                        for f in range(2):
                            for k in range(KD):
                                last = mm(ps[:, f, :].rearrange("p (g n) -> p g n", g=2), hT[:, k, a * P:(a + 1) * P],
                                          expert_cols(g, k, f),
                                          start=k == 0, stop=k == KD - 1)
                                if a == TT - 1 and f == 1 and k == CB - 1:
                                    last.then_inc(s_in_used[0], 1)
                        last.then_inc(s_H0_ps if a == 0 else s_in_used[1], 1)
                        pe.wait_ge(s_act2, e * TT + (a + 1))
                        for f in range(FT):
                            last = tr(bank(2)[:, f * P:(f + 1) * P], e_act[:, f // 2, (f % 2) * P:(f % 2 + 1) * P],
                                      ident[:])
                        last.then_inc(s_T_ps, 1)
                        pe.wait_ge(s_T, e * TT + (a + 1))
                        for c in range(2):
                            for f in range(FT):
                                last = mm(bank(4 + c), e_actT[:, f, :], expert_rows(g, 2)[:, f, c * 512:(c + 1) * 512],
                                          start=f == 0, stop=f == FT - 1)
                        last.then_inc(s_Y0_ps if a == 0 else s_out_used, 1)
                        pe.wait_ge(s_Yfree, e * TT + (a + 1))

                with nc.Fori(0, E // GROUPS, 1, engines=[pe.engine]) as r:
                    for g in range(GROUPS):
                        dense(r * GROUPS + g, r, g)
                for e in range(E - E % GROUPS, E):
                    dense(e, e // GROUPS, e % GROUPS)


_INS = ['x', 'mix_norm_g', 'w_in', 'b_gate', 'q_norm_g', 'k_norm_g', 'lb_logits', 'hgrn_norm_g', 'conv_w', 'conv_b',
        'conv_ln_g', 'conv_ln_b', 'w_att_o', 'w_hgrn_o', 'w_conv_o', 'w_out', 'ffn_norm_g', 'w_coarse', 'b_coarse',
        'w_fine', 'b_fine', 'w_exp_in', 'w_exp_out']


def kernel(**inputs):
    import numpy as _np
    import concourse.bacc as _bacc
    from concourse import mybir as _mybir
    from concourse.bass_utils import run_bass_kernel_spmd as _run

    nc = _bacc.Bacc("TRN2", target_bir_lowering=False, num_devices=1)
    arrays, args = {}, []
    for name in _INS:
        a = _np.ascontiguousarray(inputs[name])
        arrays[f"in_{name}_dram"] = a
        args.append(nc.dram_tensor(f"in_{name}_dram", a.shape, _mybir.dt.from_np(a.dtype), kind="ExternalInput").ap())
    x = inputs['x']
    args.append(nc.dram_tensor("out_0_dram", x.shape, _mybir.dt.float32, kind="ExternalOutput").ap())
    hybrid_decoder_layer(nc, *args)
    r = _run(nc, [arrays], core_ids=[0])
    return r.results[0]["out_0_dram"]
```
